# Optimizing a Trainium2 kernel written in Bass

```python
import jax, jax.numpy as jnp
from jax import lax
import numpy as np

D_MODEL = 1024
BATCH = 1
SEQ = 512
DEPTH = 2
DEC_BATCH = 8
DEC_SEQ = 4
PAST_LEN = 2048
PAGE_SIZE = 128

N_MIXERS = 2
N_LRU_LAYERS = (DEPTH + 1) // 2
N_SWA_LAYERS = DEPTH // 2
D_RNN = D_MODEL
LRU_BLOCKS = 8
LRU_BLOCK = D_RNN // LRU_BLOCKS
CONV_W = 4
LRU_C = 8.0
N_HEADS = 16
HEAD_DIM = 64
N_KV_HEADS = 2
GROUP = N_HEADS // N_KV_HEADS
WINDOW = 128
BLK = WINDOW
QKV_DIM = (N_HEADS + 2 * N_KV_HEADS) * HEAD_DIM
D_FF = 4 * D_MODEL
ALPHA = (2.0 * DEPTH) ** 0.25
BETA = (8.0 * DEPTH) ** -0.25
LN_EPS = 1e-5

kernel_name = 'hybrid_rglru_swa_sink_decoder_step'

def layer_norm(x, g, b):
    xf = x.astype(jnp.float32)
    mu = jnp.mean(xf, axis=-1, keepdims=True)
    var = jnp.mean(jnp.square(xf - mu), axis=-1, keepdims=True)
    return ((xf - mu) * lax.rsqrt(var + LN_EPS) * g.astype(jnp.float32) + b.astype(jnp.float32)).astype(x.dtype)

def squared_relu_mlp(x, w_up, w_down):
    return jnp.square(jax.nn.relu(x @ w_up)) @ w_down

def recurrent_mixer(x, h0, conv_buf, w_x, b_x, w_y, b_y, conv_w, conv_b,
                    w_ga, b_ga, w_gi, b_gi, lam, w_out, b_out):
    B, T, _ = x.shape
    y = jax.nn.gelu(x @ w_y + b_y, approximate=True)
    u = x @ w_x + b_x
    upad = jnp.concatenate([conv_buf.astype(u.dtype), u], axis=1)
    xc = conv_b + sum(conv_w[k] * upad[:, k:k + T] for k in range(CONV_W))
    new_buf = upad[:, T:]
    xb = xc.reshape(B, T, LRU_BLOCKS, LRU_BLOCK)
    r = jax.nn.sigmoid(jnp.einsum('btni,nij->btnj', xb, w_ga) + b_ga).reshape(B, T, D_RNN)
    gi = jax.nn.sigmoid(jnp.einsum('btni,nij->btnj', xb, w_gi) + b_gi).reshape(B, T, D_RNN)
    log_a = -LRU_C * r.astype(jnp.float32) * jax.nn.softplus(-lam.astype(jnp.float32))
    a = jnp.exp(log_a)
    mult = jnp.sqrt(-jnp.expm1(2.0 * log_a))
    bterm = mult * (gi * xc).astype(jnp.float32)
    bterm = bterm.at[:, 0].add(a[:, 0] * h0.astype(jnp.float32))

    def combine(left, right):
        a1, b1 = left
        a2, b2 = right
        return a1 * a2, a2 * b1 + b2

    _, h = lax.associative_scan(combine, (a, bterm), axis=1)
    out = (h.astype(x.dtype) * y) @ w_out + b_out
    return out, h[:, -1].astype(x.dtype), new_buf

def split_qkv(x, w_qkv, b_qkv):
    B, T, _ = x.shape
    qkv = x @ w_qkv + b_qkv
    nq = N_HEADS * HEAD_DIM
    nk = N_KV_HEADS * HEAD_DIM
    q = qkv[..., :nq].reshape(B, T, N_KV_HEADS, GROUP, HEAD_DIM) * (HEAD_DIM ** -0.5)
    k = qkv[..., nq:nq + nk].reshape(B, T, N_KV_HEADS, HEAD_DIM)
    v = qkv[..., nq + nk:].reshape(B, T, N_KV_HEADS, HEAD_DIM)
    return q, k, v

def softmax_with_sink(scores, mask, sink):
    s = jnp.where(mask, scores, -jnp.inf)
    m = jnp.maximum(jnp.max(s, axis=-1, keepdims=True), sink)
    p = jnp.exp(s - m)
    return p / (jnp.sum(p, axis=-1, keepdims=True) + jnp.exp(sink - m))

def swa_prompt(x, w_qkv, b_qkv, sinks, w_o, b_o):
    B, S, _ = x.shape
    NB = S // BLK
    q, k, v = split_qkv(x, w_qkv, b_qkv)
    qb = q.reshape(B, NB, BLK, N_KV_HEADS, GROUP, HEAD_DIM)
    kb = k.reshape(B, NB, BLK, N_KV_HEADS, HEAD_DIM)
    vb = v.reshape(B, NB, BLK, N_KV_HEADS, HEAD_DIM)

    def band(t):
        prev = jnp.concatenate([jnp.zeros_like(t[:, :1]), t[:, :-1]], axis=1)
        return jnp.concatenate([prev, t], axis=2)

    kband, vband = band(kb), band(vb)
    scores = jnp.einsum('bnqkgd,bnskd->bnkgqs', qb, kband).astype(jnp.float32)
    blk0 = jnp.arange(NB)[:, None] * BLK
    qpos = blk0 + jnp.arange(BLK)[None, :]
    kpos = blk0 - BLK + jnp.arange(2 * BLK)[None, :]
    diff = qpos[:, :, None] - kpos[:, None, :]
    mask = (diff >= 0) & (diff < WINDOW) & (kpos[:, None, :] >= 0)
    sink = sinks.astype(jnp.float32).reshape(N_KV_HEADS, GROUP)[None, None, :, :, None, None]
    probs = softmax_with_sink(scores, mask[None, :, None, None], sink)
    o = jnp.einsum('bnkgqs,bnskd->bnqkgd', probs.astype(v.dtype), vband)
    out = o.reshape(B, S, N_HEADS * HEAD_DIM) @ w_o + b_o
    keep = min(WINDOW, S)
    return out, k[:, S - keep:], v[:, S - keep:]

def swa_sample(x, cache_k, cache_v, w_qkv, b_qkv, sinks, w_o, b_o):
    B, T, _ = x.shape
    w_buf = cache_k.shape[1]
    q, k, v = split_qkv(x, w_qkv, b_qkv)
    k_all = jnp.concatenate([cache_k.astype(k.dtype), k], axis=1)
    v_all = jnp.concatenate([cache_v.astype(v.dtype), v], axis=1)
    scores = jnp.einsum('bqkgd,bskd->bkgqs', q, k_all).astype(jnp.float32)
    qpos = PAST_LEN + jnp.arange(T)
    kpos = jnp.concatenate([PAST_LEN - w_buf + jnp.arange(w_buf), PAST_LEN + jnp.arange(T)])
    diff = qpos[:, None] - kpos[None, :]
    mask = (diff >= 0) & (diff < WINDOW)
    sink = sinks.astype(jnp.float32).reshape(N_KV_HEADS, GROUP)[None, :, :, None, None]
    probs = softmax_with_sink(scores, mask, sink)
    o = jnp.einsum('bkgqs,bskd->bqkgd', probs.astype(v.dtype), v_all)
    out = o.reshape(B, T, N_HEADS * HEAD_DIM) @ w_o + b_o
    return out, k_all[:, T:], v_all[:, T:]

def setup_inputs(seed: int = 0) -> dict:
    key = jax.random.key(seed)
    ks = iter(jax.random.split(key, 40))
    nrm = lambda shape, scale: jax.random.normal(next(ks), shape, jnp.float32) * scale
    w_buf = min(WINDOW, PAST_LEN)
    a0 = jax.random.uniform(next(ks), (N_LRU_LAYERS, D_RNN), jnp.float32, minval=0.9, maxval=0.999)
    return {
        'x_prompt': nrm((BATCH, SEQ, D_MODEL), 1.0),
        'x_sample': nrm((DEC_BATCH, DEC_SEQ, D_MODEL), 1.0),
        'state_lru_h': nrm((N_LRU_LAYERS, DEC_BATCH, D_RNN), 0.5),
        'state_lru_conv': nrm((N_LRU_LAYERS, DEC_BATCH, CONV_W - 1, D_RNN), 1.0),
        'cache_swa_k': nrm((N_SWA_LAYERS, DEC_BATCH, w_buf, N_KV_HEADS, HEAD_DIM), 1.0),
        'cache_swa_v': nrm((N_SWA_LAYERS, DEC_BATCH, w_buf, N_KV_HEADS, HEAD_DIM), 1.0),
        'lru_w_x': nrm((N_LRU_LAYERS, D_MODEL, D_RNN), D_MODEL ** -0.5),
        'lru_b_x': nrm((N_LRU_LAYERS, D_RNN), 0.01),
        'lru_w_y': nrm((N_LRU_LAYERS, D_MODEL, D_RNN), D_MODEL ** -0.5),
        'lru_b_y': nrm((N_LRU_LAYERS, D_RNN), 0.01),
        'lru_conv_w': nrm((N_LRU_LAYERS, CONV_W, D_RNN), CONV_W ** -0.5),
        'lru_conv_b': nrm((N_LRU_LAYERS, D_RNN), 0.01),
        'lru_w_ga': nrm((N_LRU_LAYERS, LRU_BLOCKS, LRU_BLOCK, LRU_BLOCK), LRU_BLOCK ** -0.5),
        'lru_b_ga': nrm((N_LRU_LAYERS, LRU_BLOCKS, LRU_BLOCK), 0.01),
        'lru_w_gi': nrm((N_LRU_LAYERS, LRU_BLOCKS, LRU_BLOCK, LRU_BLOCK), LRU_BLOCK ** -0.5),
        'lru_b_gi': nrm((N_LRU_LAYERS, LRU_BLOCKS, LRU_BLOCK), 0.01),
        'lru_lam': jnp.log(a0) - jnp.log1p(-a0),
        'lru_w_out': nrm((N_LRU_LAYERS, D_RNN, D_MODEL), BETA * D_RNN ** -0.5),
        'lru_b_out': nrm((N_LRU_LAYERS, D_MODEL), 0.01),
        'swa_w_qkv': nrm((N_SWA_LAYERS, D_MODEL, QKV_DIM), D_MODEL ** -0.5),
        'swa_b_qkv': nrm((N_SWA_LAYERS, QKV_DIM), 0.02),
        'swa_sinks': nrm((N_SWA_LAYERS, N_HEADS), 1.0),
        'swa_w_o': nrm((N_SWA_LAYERS, N_HEADS * HEAD_DIM, D_MODEL), BETA * (N_HEADS * HEAD_DIM) ** -0.5),
        'swa_b_o': nrm((N_SWA_LAYERS, D_MODEL), 0.01),
        'mlp_w_up': nrm((DEPTH, D_MODEL, D_FF), D_MODEL ** -0.5),
        'mlp_w_down': nrm((DEPTH, D_FF, D_MODEL), BETA * D_FF ** -0.5),
        'ln1_g': 1.0 + nrm((DEPTH, D_MODEL), 0.01),
        'ln1_b': nrm((DEPTH, D_MODEL), 0.01),
        'ln2_g': 1.0 + nrm((DEPTH, D_MODEL), 0.01),
        'ln2_b': nrm((DEPTH, D_MODEL), 0.01),
    }

def reference(x_prompt, x_sample, state_lru_h, state_lru_conv, cache_swa_k, cache_swa_v,
              lru_w_x, lru_b_x, lru_w_y, lru_b_y, lru_conv_w, lru_conv_b,
              lru_w_ga, lru_b_ga, lru_w_gi, lru_b_gi, lru_lam, lru_w_out, lru_b_out,
              swa_w_qkv, swa_b_qkv, swa_sinks, swa_w_o, swa_b_o,
              mlp_w_up, mlp_w_down, ln1_g, ln1_b, ln2_g, ln2_b):
    xp, xs = x_prompt, x_sample
    h_p, conv_p, k_p, v_p = [], [], [], []
    h_s, conv_s, k_s, v_s = [], [], [], []
    for i in range(DEPTH):
        j = i // N_MIXERS
        if i % N_MIXERS == 0:
            params = (lru_w_x[j], lru_b_x[j], lru_w_y[j], lru_b_y[j], lru_conv_w[j], lru_conv_b[j],
                      lru_w_ga[j], lru_b_ga[j], lru_w_gi[j], lru_b_gi[j], lru_lam[j],
                      lru_w_out[j], lru_b_out[j])
            h0 = jnp.zeros((xp.shape[0], D_RNN), xp.dtype)
            buf0 = jnp.zeros((xp.shape[0], CONV_W - 1, D_RNN), xp.dtype)
            mp, hp, cp = recurrent_mixer(xp, h0, buf0, *params)
            ms, hs, cs = recurrent_mixer(xs, state_lru_h[j], state_lru_conv[j], *params)
            h_p.append(hp); conv_p.append(cp); h_s.append(hs); conv_s.append(cs)
        else:
            params = (swa_w_qkv[j], swa_b_qkv[j], swa_sinks[j], swa_w_o[j], swa_b_o[j])
            mp, kp, vp = swa_prompt(xp, *params)
            ms, ks_, vs_ = swa_sample(xs, cache_swa_k[j], cache_swa_v[j], *params)
            k_p.append(kp); v_p.append(vp); k_s.append(ks_); v_s.append(vs_)
        xp = layer_norm(ALPHA * xp + mp, ln1_g[i], ln1_b[i])
        xs = layer_norm(ALPHA * xs + ms, ln1_g[i], ln1_b[i])
        xp = layer_norm(ALPHA * xp + squared_relu_mlp(xp, mlp_w_up[i], mlp_w_down[i]), ln2_g[i], ln2_b[i])
        xs = layer_norm(ALPHA * xs + squared_relu_mlp(xs, mlp_w_up[i], mlp_w_down[i]), ln2_g[i], ln2_b[i])
    return (xp, xs,
            jnp.stack(h_p), jnp.stack(conv_p), jnp.stack(k_p), jnp.stack(v_p),
            jnp.stack(h_s), jnp.stack(conv_s), jnp.stack(k_s), jnp.stack(v_s))


_drawn_inputs = setup_inputs


def setup_inputs(seed=0):
    import zlib

    import numpy as np

    out = dict(_drawn_inputs(seed))
    spreads = {}
    factors = {'lru_b_y': 21.574,
     'lru_b_ga': 24.629,
     'lru_b_gi': 8.0,
     'lru_b_out': 7.281,
     'swa_sinks': 47.957,
     'swa_b_o': 29.162,
     'ln1_g': 3.982,
     'ln1_b': 10.005,
     'ln2_g': 3.832,
     'ln2_b': 11.801,
     'swa_b_qkv': 8.0}
    for name, (base, spread) in spreads.items():
        noise = np.random.default_rng([zlib.crc32(name.encode()), seed]).standard_normal(out[name].shape)
        drawn = base * np.exp(spread * noise) if base else spread * noise
        out[name] = __import__('jax').numpy.asarray(drawn.astype(out[name].dtype))
    for name, factor in factors.items():
        out[name] = (out[name] * factor).astype(out[name].dtype)
    return out
```

```python
import numpy as np
import concourse.bass as bass
from concourse import mybir
from contextlib import ExitStack

F32 = mybir.dt.float32
F32R = mybir.dt.float32r
ALU = mybir.AluOpType
ACT = mybir.ActivationFunctionType
AX = mybir.AxisListType

D = 1024
SEQ, DEC_B, DEC_T = 512, 8, 4
NS = DEC_B * DEC_T
TOK = SEQ + NS
KT = D // 128
DFF = 4 * D
CHUNKS = DFF // 512
WIN = 128
NB = SEQ // WIN
NKV, GRP, HD = 2, 8, 64
CONV = 4
ALPHA = float(4.0 ** 0.25)
EPS = 1e-5
GELU_IN = 1.0 / 0.044715
GELU_OUT = 0.044715 * float(np.sqrt(2.0 / np.pi))
NEG = -1.0e30

HALF = [(0, 256), (256, TOK - 256)]
HW = TOK - 256

VEC = {}
_at = 0
for _name, _cols in [("b_y", KT), ("b_x", KT), ("conv_w", CONV * KT), ("conv_b", KT), ("b_ga", KT), ("b_gi", KT),
                     ("lam", KT), ("b_out", KT), ("b_o", KT), ("ln_g", 4 * KT), ("ln_b", 4 * KT), ("b_qkv", KT + 2),
                     ("h0", KT * DEC_B), ("conv_state", KT * DEC_B * (CONV - 1)), ("sinks", 16), ("sink_rows", 4),
                     ("mask", 2 * WIN), ("mask_rows", 2 * (WIN + NS)), ("ident", 128)]:
    VEC[_name] = (_at, _cols)
    _at += _cols
NVEC = _at



def step_width(T):
    return WIN + NS if T == 16 else (WIN if T % 4 == 0 else 2 * WIN)


def wide_steps(T):
    return sum(step_width(t) > WIN for t in range(T))


def tile_pos(L, h, m):
    if L % 2:
        return 16 * L + 8 * h + m
    return 16 * L + 8 * (m // 4) + 4 * h + m % 4


STAGES = 4
SLOTS = 8
BANKS = 8


def build(nc, xp_t, xs_t, vec, w_y, w_x, w_ga, w_gi, w_out, w_qkv, w_o, w_up, w_down,
          ck_t, cache_k, cache_v, y_t, small, k_p, v_p, k_s, v_s):
    ctx = ExitStack()
    with ctx:
        top = [nc.sbuf_base]

        def place(name, shape, dt, at=None):
            size = int(np.prod(shape[1:])) * 4
            if at is None:
                at = (top[0] + 31) // 32 * 32
                top[0] = at + size
            t = nc.alloc_sbuf_tensor_at(name, shape, dt, offset=at)
            t_at[name] = at
            return t

        t_at = {}
        w_hi = place("w_hi", [128, SLOTS, 1024], F32R)
        w_lo = place("w_lo", [128, SLOTS, 1024], F32R)
        stage = place("stage", [128, STAGES, 1024], F32)
        x_hi = place("x_hi", [128, KT, TOK], F32R)
        x_lo = place("x_lo", [128, KT, TOK], F32R)
        m_hi = place("m_hi", [128, KT, TOK], F32R)
        m_lo = place("m_lo", [128, KT, TOK], F32R)
        acc = place("acc", [128, KT, TOK], F32)
        vecs = place("vecs", [128, NVEC], F32)
        gate_hi = place("gate_hi", [128, 2, 512], F32R)
        gate_lo = place("gate_lo", [128, 2, 512], F32R)
        xc_hi = place("xc_hi", [128, 2, HW], F32R)
        xc_lo = place("xc_lo", [128, 2, HW], F32R)
        ones = place("ones", [128, 128], F32)
        zeros = place("zeros", [128, HW], F32)
        dv = place("dv", [128, 12, KT], F32)
        tiny = place("tiny", [128, 8, KT], F32)
        out_small = place("out_small", [128, KT, 9 * 4], F32)
        scratch = (top[0] + 31) // 32 * 32
        z = place("z", [128, 2, 2, HW], F32)
        sq = place("sq", [128, 2, HW], F32)
        xc = place("xc", [128, 2, HW], F32)
        th_r = place("th_r", [128, 2, HW], F32)
        th_g = place("th_g", [128, 2, HW], F32)
        decay = place("decay", [128, 2, HW], F32)
        u = place("u", [128, 2, 3 + 256], F32)
        us = place("us", [128, 2, DEC_B, 3 + DEC_T], F32)
        sums = [[place("sum_a", [128, HW], F32, t_at["z"]), place("sumsq_a", [128, HW], F32, t_at["z"] + 4 * HW)],
                [place("sum_b", [128, HW], F32), place("sumsq_b", [128, HW], F32)]]
        sqt = place("sqt", [128, 2, HW], F32, t_at["sq"])
        mean = place("mean", [128, HW], F32, t_at["th_r"])
        rstd = place("rstd", [128, HW], F32, t_at["th_r"] + 4 * HW)
        msq = place("msq", [128, HW], F32, t_at["decay"])
        y_tmp = place("y_tmp", [128, 2, HW], F32, t_at["th_g"])
        relu = place("relu", [128, 2, HW], F32, t_at["xc"])
        h_sq = place("h_sq", [128, 2, HW], F32, t_at["z"] + 8 * HW)
        assert top[0] <= nc.sbuf_usable_end, (top[0], nc.sbuf_usable_end)
        m_half = 4 * TOK * 4
        kc_t = place("kc_t", [128, DEC_B, WIN], F32, t_at["m_hi"] + m_half)
        vc = place("vc", [128, DEC_B, WIN], F32, t_at["m_hi"] + m_half + 4096)
        v_t = place("v_t", [128, TOK], F32, t_at["m_lo"] + m_half)
        k_t = place("k_t", [128, TOK], F32, t_at["m_lo"] + m_half + 4 * TOK)
        v_tok = place("v_tok", [128, NB, 128], F32, t_at["m_lo"] + m_half + 8 * TOK)
        k_tok = place("k_tok", [128, 128], F32, t_at["m_lo"] + m_half + 8 * TOK + 2048)
        kv_new = place("kv_new", [NS, 2, 128], F32, t_at["m_lo"] + m_half + 8 * TOK + 2560)
        q_a = place("q_a", [128, 4, SEQ], F32, t_at["m_hi"])
        q_b = place("q_b", [128, 4, SEQ], F32, t_at["m_lo"])
        q_s = place("q_s", [128, DEC_B, KT, DEC_T], F32, t_at["u"])
        probs = place("probs", [128, 2, 4, 256], F32, scratch)
        probs_t = place("probs_t", [128, 2, 512], F32, scratch + 8192)
        stat = place("stat", [128, 2, 8, 4], F32, scratch + 12288)
        assert scratch + 12288 + 256 <= top[0]

        def q_tile(i):
            return (q_a if i < 4 else q_b)[:, i % 4, :]

        bank = ctx.enter_context(nc.psum_tensor("bank", [128, BANKS, 512], F32))

        def sem(name):
            return ctx.enter_context(nc.semaphore(name))

        s_vec = sem("vec_loaded")
        s_x = [sem(f"x_loaded_{h}") for h in "ab"]
        s_arrived = [sem(f"slab_arrived_{i}") for i in range(STAGES)]
        s_whi, s_wlo = sem("slab_hi_done"), sem("slab_lo_done")
        s_unit = sem("unit_done")
        s_evA, s_evV = sem("read_by_scalar"), sem("read_by_vector")
        s_xhi, s_xlo, s_res0 = sem("x_hi_done"), sem("x_lo_done"), sem("residual_ready")
        s_const = sem("constants_ready")
        s_sp, s_spe = sem("softplus_in"), sem("softplus_exp")
        s_dv = sem("derived_ready")
        s_gsq, s_gin, s_gth, s_gy = sem("gelu_sq"), sem("gelu_in"), sem("gelu_tanh"), sem("gelu_y")
        s_halo, s_conv0, s_conv = sem("halo_ready"), sem("conv_first"), sem("conv_done")
        s_xchi, s_xclo = sem("xc_hi_done"), sem("xc_lo_done")
        s_dec, s_root, s_gated = sem("decay_ready"), sem("root_ready"), sem("gated_ready")
        s_drive, s_scan, s_p = sem("drive_ready"), sem("scan_done"), sem("product_ready")
        s_phi, s_plo = sem("product_hi_done"), sem("product_lo_done")
        s_sqt, s_s1, s_s2 = sem("square_ready"), sem("sum_added"), sem("square_added")
        s_var, s_std = sem("variance_ready"), sem("deviation_ready")
        s_xhat, s_yhi, s_y, s_ylo, s_res = (sem("normed"), sem("y_hi_done"), sem("y_ready"), sem("y_lo_done"),
                                            sem("residual_done"))
        s_yout = [sem("y_out_even"), sem("y_out_odd")]
        s_hhi, s_hsq, s_hlo = sem("hidden_hi"), sem("hidden_sq"), sem("hidden_lo")
        s_cache = sem("cache_loaded")
        s_tok = sem("token_major_transposed")
        s_tokc = sem("token_major_copied")
        s_sc, s_sm, s_max = sem("scores_done"), sem("scores_masked"), sem("max_ready")
        s_exp, s_nrm = sem("exp_done"), sem("probs_normed")
        s_pt, s_ptA, s_ptV = sem("probs_transposed"), sem("probs_t_by_scalar"), sem("probs_t_by_vector")
        s_pv, s_ohi, s_olo = sem("values_done"), sem("mixed_hi"), sem("mixed_lo")
        s_out, s_kept = sem("trunk_written"), sem("states_written")
        s_seqA, s_seqV, s_seqP = sem("scalar_order"), sem("vector_order"), sem("pool_order")

        block = ctx.enter_context(nc.Block())

        def V(name, a=0, n=1):
            at = VEC[name][0]
            return vecs[:, at + a:at + a + n]

        reader = []
        mark = {}

        def plan(name, who):
            mark[name] = len(reader)
            reader.extend(who)

        for s in range(8):
            plan(("y", s), "AA")
            if s:
                plan(("gate", s - 1), "AAAA")
            plan(("x", s), "AA")

        def plan_project(l):
            plan(("o", l, 0, 0, 0), "VV")
            if l == 0:
                plan(("gate", 7), "AAAA")
            plan(("o", l, 0, 0, 2), "VV")
            plan(("o", l, 0, 1, 0), "VVVV")
            plan(("o", l, 1, 0, 0), "VVVV")
            plan(("o", l, 1, 1, 0), "VV")
            plan(("ln", 2 * l, 0), "AV")
            plan(("o", l, 1, 1, 2), "VV")
            plan(("ln", 2 * l, 1), "AV")

        def plan_mlp(l):
            plan(("mlp", l), ("A" * 8 + "V" * 16) * (CHUNKS - 1))
            plan(("up", l, 0), "AAAA")
            plan(("up", l, 1), "AAAA")
            plan(("down", l, 0), "V" * 8)
            plan(("down", l, 1, 0), "V" * 2)
            plan(("ln", 2 * l + 1, 0), "AV")
            plan(("down", l, 1, 2), "V" * 6)

        plan_project(0)
        plan_mlp(0)
        plan(("qkv", 0, 0, 0), "AA")
        plan(("ln", 1, 1), "AV")
        plan(("qkv", 0, 0, 2), "AA")
        plan(("qkv", 0, 1, 0), "AAAA")
        for g in (1, 2):
            for h in (0, 1):
                plan(("qkv", g, h, 0), "AAAA" if g == 1 else "AA")
        mark["attention"] = len(reader)
        plan_project(1)
        plan_mlp(1)
        plan(("ln", 3, 1), "AV")

        def read_by(n, who):
            return sum(1 for r in reader[:n] if r == who)

        yv, xv, ov, qv, pv = (w.rearrange("(k p) c -> p k c", p=128) for w in (w_y, w_x, w_out, w_qkv, w_o))
        uv = [w_up[l].rearrange("(k p) c -> p k c", p=128) for l in range(2)]
        dwv = [w_down[l].rearrange("(k p) c -> p k c", p=128) for l in range(2)]

        def quad(view, g, j):
            return view[:, 2 * j:2 * j + 2, 512 * g:512 * g + 512]

        job_at = {}
        jobs = []
        ring = [0]

        def plan_jobs(name, kinds):
            job_at[name] = (len(jobs), ring[0])
            for k in kinds:
                jobs.append((k, ring[0]))
                ring[0] += k == "w"

        for p in range(4):
            plan_jobs(("pair", p), "wwww")
            plan_jobs(("gates", p), "g")
        for g in range(2):
            plan_jobs(("o", 0, g), "wwww")
        plan_jobs(("mlp", 0), "w" * 8 * CHUNKS)
        for g, k in enumerate(["wwww", "wwww", "ww"]):
            plan_jobs(("qkv", g), k)
        for g in range(2):
            plan_jobs(("o", 1, g), "wwww")
        plan_jobs(("mlp", 1), "w" * 8 * CHUNKS)

        free_at = {}

        def frees(name, end, n=4):
            w = job_at[name][1]
            for k in range(n):
                free_at[w + k] = end

        for p in range(4):
            frees(("pair", p), mark[("x", 2 * p + 1)] + 2)
        for l in range(2):
            frees(("o", l, 0), mark[("o", l, 0, 1, 0)] + 4)
            frees(("o", l, 1), mark[("o", l, 1, 1, 2)] + 2)
            w0 = job_at[("mlp", l)][1]
            for c in range(CHUNKS):
                for k in range(4):
                    free_at[w0 + 8 * c + k] = mark[("mlp", l)] + 24 * c + 8
                    free_at[w0 + 8 * c + 4 + k] = mark[("mlp", l)] + 24 * c + 24 + (2 if c == CHUNKS - 1 else 0)
        frees(("qkv", 0), mark[("qkv", 0, 1, 0)] + 4)
        frees(("qkv", 1), mark[("qkv", 1, 1, 0)] + 4)
        frees(("qkv", 2), mark[("qkv", 2, 1, 0)] + 2, 2)

        def mixed(T, dst):
            src = bank[:, 6 + T % 2, 0:256]
            if T < 16:
                return (dst[:, 2 * (T // 4):2 * (T // 4) + 2, WIN * (T % 4):WIN * (T % 4) + WIN],
                        src.rearrange("p (i q) -> p i q", i=2))
            return (dst[:, :, SEQ:TOK].rearrange("p i (b t) -> p b i t", t=DEC_T),
                    src.rearrange("p (b i t) -> p b i t", b=DEC_B, i=KT))

        @block.sync
        def _(sp):
            def load(j, src, i=None, per=0):
                if i is None:
                    if j >= STAGES:
                        sp.wait_ge(s_wlo, j - STAGES + 1)
                else:
                    sp.wait_ge(s_wlo, i * per + (j - STAGES + 1))
                n = int(np.prod(src.shape[1:]))
                dst = stage[:, j % STAGES, 0:n]
                if len(src.shape) == 3:
                    dst = dst.rearrange("p (k c) -> p k c", k=src.shape[1])
                sp.dma_start(dst, src).then_inc(s_arrived[j % STAGES], 16)

            def load_pair(name, view, c, jj=0):
                for k in range(2):
                    load(job_at[name][0] + jj + k, view[:, 4 * k:4 * k + 4, c:c + 256])

            def load_quad(name, view, g):
                for k in range(4):
                    load(job_at[name][0] + k, quad(view, g, k))

            def load_mlp(l):
                j0 = job_at[("mlp", l)][0]
                for k in range(4):
                    load(j0 + k, quad(uv[l], 0, k))
                with sp.Fori(0, CHUNKS - 1) as i:
                    for k in range(4):
                        load(j0 + 4 + k, dwv[l][:, bass.ds(i * 4 + k, 1), :], i, 8)
                    for k in range(4):
                        load(j0 + 8 + k, uv[l][:, 2 * k:2 * k + 2, bass.ds(i * 512 + 512, 512)], i, 8)
                for k in range(4):
                    load(j0 + 8 * (CHUNKS - 1) + 4 + k, dwv[l][:, 4 * (CHUNKS - 1) + k, :])

            sp.dma_start(acc[:, :, 0:256], xp_t[:, 0:256].rearrange("(k p) t -> p k t", p=128)).then_inc(s_x[0], 16)
            for p in range(4):
                load_pair(("pair", p), yv, 256 * p)
                load_pair(("pair", p), xv, 256 * p, 2)
                if p == 0:
                    sp.dma_start(acc[:, :, 256:512],
                                 xp_t[:, 256:512].rearrange("(k p) t -> p k t", p=128)).then_inc(s_x[1], 16)
                    sp.dma_start(acc[:, :, 512:TOK], xs_t.rearrange("(k p) t -> p k t", p=128)).then_inc(s_x[1], 16)
                j = job_at[("gates", p)][0]
                sp.wait_ge(s_wlo, j - STAGES + 1)
                dst = stage[:, j % STAGES, 0:512].rearrange("p (b g c) -> p b g c", b=2, g=2)
                for n, w in enumerate((w_ga, w_gi)):
                    sp.dma_start(dst[:, :, n, :], w[2 * p:2 * p + 2].rearrange("b i j -> i b j"))\
                      .then_inc(s_arrived[j % STAGES], 16)
            for g in range(2):
                load_quad(("o", 0, g), ov, g)
            load_mlp(0)
            for g in range(2):
                load_quad(("qkv", g), qv, g)
            load_pair(("qkv", 2), qv, 1024)
            for g in range(2):
                load_quad(("o", 1, g), pv, g)
            load_mlp(1)
            for h, (c0, n) in enumerate(HALF):
                for k in range(KT):
                    sp.wait_ge(s_yout[k % 2], 4 * h + k // 2 + 1)
                    sp.dma_start(y_t[128 * k:128 * k + 128, c0:c0 + n], acc[:, k, c0:c0 + n]).then_inc(s_out, 16)
            sp.wait_ge(s_out, 16 * 2 * KT)
            sp.wait_ge(s_kept, 16 * (5 + 2 * DEC_B))

        arrivals = []
        count = [0] * STAGES
        for j, (kind, _) in enumerate(jobs):
            count[j % STAGES] += 32 if kind == "g" else 16
            arrivals.append(count[j % STAGES])

        def split_targets(j):
            kind, w = jobs[j]
            if kind == "g":
                p = (j - 4) // 5
                return gate_hi[:, p % 2, :], gate_lo[:, p % 2, :], stage[:, j % STAGES, 0:512]
            return w_hi[:, w % SLOTS, :], w_lo[:, w % SLOTS, :], stage[:, j % STAGES, :]

        @block.scalar
        def _(act):
            A = nc.scalar.activation
            seq = [0]

            def ordered(ins):
                seq[0] += 1
                ins.then_inc(s_seqA, 1)
                return seq[0]

            def split(js, i=None, per=0, per_units=0, freed=0):
                for j in js:
                    hi, _, raw = split_targets(j)
                    kind, w = jobs[j]
                    if i is None:
                        act.wait_ge(s_arrived[j % STAGES], arrivals[j])
                        if kind == "w" and w >= SLOTS:
                            act.wait_ge(s_unit, free_at[w - SLOTS])
                        if kind == "g" and j >= 14:
                            act.wait_ge(s_unit, mark[("gate", 2 * ((j - 4) // 5) - 3)] + 4)
                    else:
                        act.wait_ge(s_arrived[j % STAGES], i * (16 * per // STAGES) + arrivals[j])
                        act.wait_ge(s_unit, i * per_units + freed)
                    A(hi, raw, ACT.Copy).then_inc(s_whi, 1)

            def unit(n):
                act.wait_ge(s_unit, n + 1)
                return bank[:, n % BANKS, :]

            def x_split(h):
                c0, n = HALF[h]
                act.wait_ge(s_x[h], 16 * (1 + h))
                for k in (0, 4):
                    A(x_hi[:, k:k + 4, c0:c0 + n], acc[:, k:k + 4, c0:c0 + n], ACT.Copy).then_inc(s_xhi, 1)

            act.dma_start(vecs[:, :], vec).then_inc(s_vec, 16)
            x_split(0)
            split(range(0, 4))
            act.wait_ge(s_sp, 1)
            A(tiny[:, 2, :], tiny[:, 1, :], ACT.Exp, scale=-1.0).then_inc(s_spe, 1)
            x_split(1)
            split([4])
            act.wait_ge(s_dv, 1)

            def chain(s):
                p, (_, n) = s // 2, HALF[s % 2]
                m0 = mark[("gate", s)]
                if s >= 1:
                    act.wait_ge(s_p, s)
                for t in range(2):
                    m = 2 * p + t
                    A(th_r[:, t, :n], unit(m0 + 2 * t)[:, :n], ACT.Tanh, bias=dv[:, 0, m:m + 1], scale=0.5)\
                        .then_inc(s_evA, 1)
                    A(th_g[:, t, :n], unit(m0 + 2 * t + 1)[:, :n], ACT.Tanh, bias=dv[:, 1, m:m + 1], scale=0.5)\
                        .then_inc(s_evA, 1)
                act.wait_ge(s_evA, read_by(m0 + 4, "A"))
                for t in range(2):
                    m = 2 * p + t
                    last = ordered(A(decay[:, t, :n], th_r[:, t, :n], ACT.Exp, bias=dv[:, 2, m:m + 1],
                                     scale=dv[:, 2, m:m + 1]))
                act.wait_ge(s_seqA, last)
                for t in range(2):
                    m = 2 * p + t
                    last = ordered(A(th_r[:, t, :n], th_r[:, t, :n], ACT.Tanh, bias=dv[:, 3, m:m + 1],
                                     scale=dv[:, 3, m:m + 1]))
                return last

            def chain_root(s, last):
                _, n = HALF[s % 2]
                act.wait_ge(s_seqA, last)
                A(th_r[:, :, :n], th_r[:, :, :n], ACT.Sqrt).then_inc(s_root, 1)

            def chain_hi(s):
                p, (c0, n) = s // 2, HALF[s % 2]
                act.wait_ge(s_p, s + 1)
                A(m_hi[:, 2 * p:2 * p + 2, c0:c0 + n], z[:, s % 2, :, :n], ACT.Copy).then_inc(s_phi, 1)

            for s in range(8):
                p, h = s // 2, s % 2
                c0, n = HALF[h]
                if s >= 2:
                    act.wait_ge(s_plo, s - 1)
                for t in range(2):
                    A(z[:, s % 2, t, :n], unit(mark[("y", s)] + t)[:, :n], ACT.Identity,
                      bias=V("b_y", 2 * p + t)).then_inc(s_evA, 1)
                act.wait_ge(s_evA, read_by(mark[("y", s)] + 2, "A"))
                if s >= 1:
                    act.wait_ge(s_gy, s)
                A(sq[:, :, :n], z[:, s % 2, :, :n], ACT.Square).then_inc(s_gsq, 1)
                if h == 0:
                    nxt = list(range(*((job_at[("pair", p + 1)][0], job_at[("pair", p + 1)][0] + 5) if p < 3 else
                                       (job_at[("o", 0, 0)][0], job_at[("o", 0, 0)][0] + 4))))
                split(nxt[0:1] if h == 0 else nxt[2:3])
                if s:
                    last = chain(s - 1)
                act.wait_ge(s_gin, s + 1)
                A(sq[:, :, :n], sq[:, :, :n], ACT.Tanh, scale=GELU_OUT).then_inc(s_gth, 1)
                if s:
                    chain_root(s - 1, last)
                split(nxt[1:2] if h == 0 else nxt[3:5])
                if s:
                    chain_hi(s - 1)
                act.wait_ge(s_halo, s + 1)
                m0 = mark[("x", s)]
                for t in range(2):
                    src = unit(m0 + t)
                    if h == 1:
                        ordered(A(us[:, t, :, 3:], src[:, 256:n].rearrange("p (b t) -> p b t", t=DEC_T),
                                  ACT.Identity, bias=V("b_x", 2 * p + t)))
                    A(u[:, t, 3:3 + 256], src[:, 0:256], ACT.Identity, bias=V("b_x", 2 * p + t)).then_inc(s_evA, 1)
                act.wait_ge(s_conv, s + 1)
                if s >= 1:
                    act.wait_ge(s_unit, mark[("gate", s - 1)] + 4)
                A(xc_hi[:, :, :n], xc[:, :, :n], ACT.Copy).then_inc(s_xchi, 1)

            def square(L, h, m):
                c0, n = HALF[h]
                pos = tile_pos(L, h, m)
                act.wait_ge(s_s1, pos + 1)
                if pos >= 2:
                    act.wait_ge(s_s2, pos - 1)
                A(sqt[:, pos % 2, :n], acc[:, m, c0:c0 + n], ACT.Square).then_inc(s_sqt, 1)

            def norm_stats(L, h):
                _, n = HALF[h]
                m0 = mark[("ln", L, h)]
                idx = 2 * L + h
                if idx:
                    act.wait_ge(s_xhat, 4 * idx)
                A(mean[:, :n], unit(m0)[:, :n], ACT.Copy).then_inc(s_evA, 1)
                act.wait_ge(s_var, idx + 1)
                A(rstd[:, :n], msq[:, :n], ACT.Sqrt).then_inc(s_std, 1)

            def norm_apply(L, h):
                c0, n = HALF[h]
                idx = 2 * L + h
                for k in range(KT):
                    act.wait_ge(s_xhat, 4 * idx + k // 2 + 1)
                    g, b = V("ln_g", L * KT + k), V("ln_b", L * KT + k)
                    if L < 3:
                        A(x_hi[:, k, c0:c0 + n], acc[:, k, c0:c0 + n], ACT.Identity, bias=b, scale=g)\
                            .then_inc(s_yhi, 1)
                    elif k % 2 == 0:
                        A(acc[:, k, c0:c0 + n], acc[:, k, c0:c0 + n], ACT.Identity, bias=b, scale=g)\
                            .then_inc(s_yout[0], 1)

            def project(l):
                L = 2 * l
                for m in range(4):
                    if l == 0:
                        split([job_at[("o", 0, 1)][0] + m])
                    if l == 0 and m == 1:
                        last = chain(7)
                        chain_root(7, last)
                        chain_hi(7)
                    square(L, 0, m)
                for m in range(4):
                    square(L, 1, m)
                for m in range(4, 8):
                    square(L, 0, m)
                    if m in (5, 7):
                        split([job_at[("mlp", l)][0] + m // 2 - 2])
                for m in range(4, 8):
                    if m == 6:
                        split([job_at[("mlp", l)][0] + 2, job_at[("mlp", l)][0] + 3])
                        norm_stats(L, 0)
                        norm_apply(L, 0)
                    square(L, 1, m)
                norm_stats(L, 1)
                norm_apply(L, 1)

            def up(l, q, i=None):
                c = CHUNKS - 1 if i is None else 0
                it = 0 if i is None else i
                n = HALF[q // 4][1]
                c0 = HALF[q // 4][0]
                n0 = mark[("mlp", l)] + 24 * c + q
                t0 = (CHUNKS * l + c) * 8 + q
                act.wait_ge(s_unit, it * 24 + (n0 + 1))
                act.wait_ge(s_hsq, it * 8 + (t0 + 1))
                A(relu[:, q % 2, :n], bank[:, n0 % BANKS, :n], ACT.Relu).then_inc(s_evA, 1)
                act.wait_ge(s_evA, it * 8 + (read_by(n0 + 1, "A")))
                A(m_hi[:, q % 4, c0:c0 + n], relu[:, q % 2, :n], ACT.Square).then_inc(s_hhi, 1)

            def mlp(l):
                j0 = job_at[("mlp", l)][0]
                with act.Fori(0, CHUNKS - 1) as i:
                    for q in range(8):
                        if q % 2 == 0:
                            split([j0 + 4 + q // 2], i, 8, 24, mark[("mlp", l)])
                        up(l, q, i)
                    split(range(j0 + 8, j0 + 12), i, 8, 24, mark[("mlp", l)] + 8)
                last = j0 + 8 * (CHUNKS - 1)
                for q in range(8):
                    if q % 2 == 0:
                        split([last + 4 + q // 2])
                    up(l, q)
                L = 2 * l + 1
                for m in range(8):
                    square(L, 0, m)
                if l == 0:
                    split(range(job_at[("qkv", 0)][0], job_at[("qkv", 0)][0] + 4))
                for m in range(8):
                    if m == 2:
                        norm_stats(L, 0)
                        norm_apply(L, 0)
                    square(L, 1, m)

            project(0)
            mlp(0)
            def qkv(g, h, u0, nu):
                c0, n = HALF[h]
                for t in range(u0, u0 + nu):
                    i = 4 * g + t
                    src = unit(mark[("qkv", g, h, u0)] + t - u0)[:, :n]
                    if i < 2:
                        A((k_t if i == 0 else v_t)[:, c0:c0 + n], src, ACT.Identity, bias=V("b_qkv", i))\
                            .then_inc(s_evA, 1)
                    else:
                        bq = dv[:, 4, i - 2:i - 1]
                        if h == 1:
                            ordered(A(q_s[:, :, i - 2, :], src[:, 256:n].rearrange("p (b t) -> p b t", t=DEC_T),
                                      ACT.Identity, bias=bq, scale=HD ** -0.5))
                        A(q_tile(i - 2)[:, c0:c0 + 256], src[:, 0:256], ACT.Identity, bias=bq, scale=HD ** -0.5)\
                            .then_inc(s_evA, 1)
            qj = [job_at[("qkv", g)][0] for g in range(3)]
            qkv(0, 0, 0, 2)
            norm_stats(1, 1)
            norm_apply(1, 1)
            qkv(0, 0, 2, 2)
            split([qj[1], qj[1] + 1])
            qkv(0, 1, 0, 4)
            split([qj[1] + 2, qj[1] + 3])
            qkv(1, 0, 0, 4)
            split([qj[2], qj[2] + 1])
            qkv(1, 1, 0, 4)
            qkv(2, 0, 0, 2)
            qkv(2, 1, 0, 2)
            act.wait_ge(s_tok, 1)
            A(v_tok[:, :, :], bank[:, 4, :].rearrange("p (n d) -> p n d", n=NB), ACT.Copy).then_inc(s_tokc, 1)
            act.wait_ge(s_tok, 2)
            A(k_tok[:, :], bank[:, 5, 0:128], ACT.Copy).then_inc(s_tokc, 1)
            A(kv_new[:, :, :], bank[0:NS, 5, 128:384].rearrange("p (n d) -> p n d", n=2), ACT.Copy)\
                .then_inc(s_tokc, 1)
            oj = job_at[("o", 1, 0)][0]
            for T in range(17):
                w = step_width(T)
                act.wait_ge(s_max, T + 1)
                for e in range(4):
                    A(probs[:, T % 2, e, 0:w], probs[:, T % 2, e, 0:w], ACT.Exp, bias=stat[:, T % 2, 1, e:e + 1],
                      accum_out=stat[:, T % 2, 2, e:e + 1]).then_inc(s_seqA, 1)
                    seq[0] += 1
                A(stat[:, T % 2, 4, :], stat[:, T % 2, 3, :], ACT.Exp).then_inc(s_exp, 1)
                if T % 2 == 0 and T < 16:
                    split([oj + T // 2])
                act.wait_ge(s_pt, T + 1)
                if T:
                    act.wait_ge(s_pv, T)
                A(probs_t[:, 0, :], bank[:, 4, :], ACT.Copy).then_inc(s_ptA, 1)
                act.wait_ge(s_pv, T + 1)
                dst, src = mixed(T, x_hi)
                A(dst, src, ACT.Copy).then_inc(s_ohi, 1)
            project(1)
            mlp(1)
            norm_stats(3, 1)
            norm_apply(3, 1)

        @block.vector
        def _(dve):
            vt = nc.vector
            seq = [0]

            def ordered(ins):
                seq[0] += 1
                ins.then_inc(s_seqV, 1)
                dve.wait_ge(s_seqV, seq[0])

            def split(js, i=None, per=0):
                for j in js:
                    hi, lo, raw = split_targets(j)
                    dve.wait_ge(s_whi, j + 1 if i is None else i * per + (j + 1))
                    vt.tensor_tensor(lo, raw, hi.bitcast(F32), ALU.subtract).then_inc(s_wlo, 1)

            def unit(n):
                dve.wait_ge(s_unit, n + 1)
                return bank[:, n % BANKS, :]

            def x_split(h):
                c0, n = HALF[h]
                for k in (0, 4):
                    dve.wait_ge(s_xhi, 2 * h + k // 4 + 1)
                    vt.tensor_tensor(x_lo[:, k:k + 4, c0:c0 + n], acc[:, k:k + 4, c0:c0 + n],
                                     x_hi[:, k:k + 4, c0:c0 + n].bitcast(F32), ALU.subtract).then_inc(s_xlo, 1)

            vt.memset(ones[:, :], 1.0 / D).then_inc(s_const, 1)
            vt.memset(zeros[:, :], 0.0).then_inc(s_const, 1)
            vt.memset(tiny[:, 6, :], 0.0).then_inc(s_hsq, 2)
            vt.memset(tiny[:, 7, :], 0.0).then_inc(s_hlo, 2)
            dve.wait_ge(s_vec, 16)
            lam = V("lam", 0, KT)
            ordered(vt.tensor_scalar(tiny[:, 0, :], lam, -1.0, None, ALU.mult))
            vt.tensor_tensor(tiny[:, 1, :], tiny[:, 0, :], lam, ALU.max).then_inc(s_sp, 1)
            vt.tensor_scalar(dv[:, 0, :], V("b_ga", 0, KT), 0.5, None, ALU.mult)
            vt.tensor_scalar(dv[:, 1, :], V("b_gi", 0, KT), 0.5, None, ALU.mult)
            vt.tensor_scalar(dv[:, 4, :], V("b_qkv", 2, KT), HD ** -0.5, None, ALU.mult)
            for L in range(3):
                vt.tensor_scalar(dv[:, 5 + L, :], V("ln_g", L * KT, KT), ALPHA, None, ALU.mult)
                if L == 1:
                    vt.scalar_tensor_tensor(dv[:, 8 + L, :], V("ln_b", L * KT, KT), ALPHA, V("b_o", 0, KT),
                                            ALU.mult, ALU.add)
                else:
                    vt.tensor_scalar(dv[:, 8 + L, :], V("ln_b", L * KT, KT), ALPHA, None, ALU.mult)
            x_split(0)
            split(range(0, 4))
            dve.wait_ge(s_spe, 1)
            e, zz, z2, f = (tiny[:, k, :] for k in (2, 3, 4, 5))
            ordered(vt.tensor_scalar(zz, e, 2.0, None, ALU.add))
            ordered(vt.reciprocal(z2, zz))
            ordered(vt.tensor_tensor(zz, e, z2, ALU.mult))
            ordered(vt.tensor_tensor(z2, zz, zz, ALU.mult))
            ordered(vt.tensor_scalar(f, z2, 1.0 / 15.0, None, ALU.mult))
            for k in (13, 11, 9, 7, 5, 3):
                ordered(vt.scalar_tensor_tensor(f, f, 1.0 / k, z2, ALU.add, ALU.mult))
            ordered(vt.scalar_tensor_tensor(f, f, 1.0, zz, ALU.add, ALU.mult))
            ordered(vt.tensor_scalar(f, f, 2.0, None, ALU.mult))
            ordered(vt.tensor_scalar(tiny[:, 0, :], tiny[:, 0, :], 0.0, None, ALU.max))
            ordered(vt.tensor_tensor(f, f, tiny[:, 0, :], ALU.add))
            ordered(vt.tensor_scalar(dv[:, 3, :], f, 2.0, None, ALU.mult))
            vt.tensor_scalar(dv[:, 2, :], f, -4.0, None, ALU.mult).then_inc(s_dv, 1)
            x_split(1)
            split([4])

            def halo(s):
                p, h = s // 2, s % 2
                if s:
                    dve.wait_ge(s_conv, s)
                if h == 0:
                    vt.memset(u[:, :, 0:3], 0.0).then_inc(s_halo, 1)
                else:
                    at = VEC["conv_state"][0] + 2 * p * DEC_B * 3
                    state = vecs[:, at:at + 2 * DEC_B * 3].rearrange("p (t b k) -> p t b k", t=2, b=DEC_B)
                    for t in range(2):
                        seq[0] += 1
                        vt.tensor_copy(us[:, t, :, 0:3], state[:, t]).then_inc(s_seqV, 1)
                    vt.tensor_copy(u[:, :, 0:3], u[:, :, 256:259]).then_inc(s_halo, 1)

            def gated(s):
                _, n = HALF[s % 2]
                dve.wait_ge(s_evA, read_by(mark[("gate", s)] + 4, "A"))
                vt.scalar_tensor_tensor(th_g[:, :, :n], th_g[:, :, :n], 1.0, xc[:, :, :n], ALU.add, ALU.mult)\
                    .then_inc(s_gated, 1)

            def recur(s):
                p, h = s // 2, s % 2
                c0, n = HALF[h]
                dve.wait_ge(s_root, s + 1)
                dve.wait_ge(s_gated, s + 1)
                ordered(vt.scalar_tensor_tensor(th_r[:, :, :n], decay[:, :, :n], 1.0, th_r[:, :, :n],
                                                ALU.add, ALU.mult))
                ordered(vt.scalar_tensor_tensor(th_g[:, :, :n], th_r[:, :, :n], 0.5, th_g[:, :, :n],
                                                ALU.mult, ALU.mult))
                if h == 1:
                    first = slice(256, n, DEC_T)
                    h0 = V("h0", 2 * p * DEC_B, 2 * DEC_B).rearrange("p (t b) -> p t b", t=2)
                    t3 = tiny[:, 6:8, :]
                    ordered(vt.tensor_tensor(t3, decay[:, :, first], h0, ALU.mult))
                    ordered(vt.tensor_tensor(th_g[:, :, first], th_g[:, :, first], t3, ALU.add))
                    ordered(vt.memset(decay[:, :, first], 0.0))
                for t in range(2):
                    m = 2 * p + t
                    init = 0.0 if h == 0 else out_small[:, m, 0:1]
                    ins = vt.tensor_tensor_scan(th_r[:, t, :n], decay[:, t, :n], th_g[:, t, :n], init,
                                                ALU.mult, ALU.add)
                    ins.then_inc(s_scan, 1)
                dve.wait_ge(s_scan, 2 * s + 2)
                for t in range(2):
                    m = 2 * p + t
                    seq[0] += 1
                    vt.tensor_copy(out_small[:, m, 0:1], th_r[:, t, 255:256]).then_inc(s_seqV, 1)
                    if h == 1:
                        seq[0] += 1
                        vt.tensor_copy(out_small[:, m, 1:9], th_r[:, t, 256 + DEC_T - 1:n:DEC_T]).then_inc(s_seqV, 1)
                dve.wait_ge(s_gy, s + 1)
                vt.scalar_tensor_tensor(z[:, s % 2, :, :n], th_r[:, :, :n], 0.5, z[:, s % 2, :, :n],
                                        ALU.mult, ALU.mult).then_inc(s_p, 1)

            for s in range(8):
                p, h = s // 2, s % 2
                c0, n = HALF[h]
                halo(s)
                dve.wait_ge(s_gsq, s + 1)
                vt.scalar_tensor_tensor(sq[:, :, :n], sq[:, :, :n], GELU_IN, z[:, s % 2, :, :n], ALU.add, ALU.mult)\
                    .then_inc(s_gin, 1)
                if h == 0:
                    nxt = list(range(*((job_at[("pair", p + 1)][0], job_at[("pair", p + 1)][0] + 5) if p < 3 else
                                       (job_at[("o", 0, 0)][0], job_at[("o", 0, 0)][0] + 4))))
                split(nxt[0:1] if h == 0 else nxt[2:3])
                if s:
                    gated(s - 1)
                dve.wait_ge(s_gth, s + 1)
                vt.scalar_tensor_tensor(z[:, s % 2, :, :n], sq[:, :, :n], 1.0, z[:, s % 2, :, :n], ALU.add, ALU.mult)\
                    .then_inc(s_gy, 1)
                if s:
                    recur(s - 1)
                split(nxt[1:2] if h == 0 else nxt[3:5])
                dve.wait_ge(s_conv0, s + 1)
                for k in range(1, CONV):
                    for t in range(2):
                        m = 2 * p + t
                        wk = V("conv_w", k * KT + m)
                        ins = vt.scalar_tensor_tensor(xc[:, t, 0:256], u[:, t, k:k + 256], wk, xc[:, t, 0:256],
                                                      ALU.mult, ALU.add)
                        if h == 1:
                            seq[0] += 1
                            ins.then_inc(s_seqV, 1)
                            xs = xc[:, t, 256:n].rearrange("p (b t) -> p b t", t=DEC_T)
                            ins = vt.scalar_tensor_tensor(xs, us[:, t, :, k:k + DEC_T], wk, xs, ALU.mult, ALU.add)
                        if k == CONV - 1 and t == 1:
                            ins.then_inc(s_conv, 1)
                        else:
                            seq[0] += 1
                            ins.then_inc(s_seqV, 1)
                    if k < CONV - 1:
                        dve.wait_ge(s_seqV, seq[0])
                if h == 1:
                    for t in range(2):
                        m = 2 * p + t
                        rows = out_small[:, m, 9:36].rearrange("p (b k) -> p b k", k=3)
                        seq[0] += 2
                        vt.tensor_copy(rows[:, 0, :], u[:, t, 256:259]).then_inc(s_seqV, 1)
                        vt.tensor_copy(rows[:, 1:9, :], us[:, t, :, DEC_T:DEC_T + 3]).then_inc(s_seqV, 1)

            def tile_done(L, h, m, src, n_read):
                c0, n = HALF[h]
                if n_read > 8:
                    dve.wait_ge(s_evV, n_read - 8)
                vt.tensor_tensor(acc[:, m, c0:c0 + n], src[:, :n], acc[:, m, c0:c0 + n], ALU.add)\
                    .then_inc(s_evV, 1)
                pos = tile_pos(L, h, m)
                dve.wait_ge(s_evV, n_read)
                if pos:
                    dve.wait_ge(s_s1, pos)
                s1 = sums[h][0]
                vt.tensor_tensor(s1[:, :n], acc[:, m, c0:c0 + n], zeros[:, :n] if m == 0 else s1[:, :n], ALU.add)\
                    .then_inc(s_s1, 1)

            def norm_stats(L, h):
                _, n = HALF[h]
                m0 = mark[("ln", L, h)]
                idx = 2 * L + h
                dve.wait_ge(s_evA, read_by(m0 + 1, "A"))
                ordered(vt.tensor_tensor(msq[:, :n], mean[:, :n], mean[:, :n], ALU.mult))
                vt.tensor_tensor(msq[:, :n], unit(m0 + 1)[:, :n], msq[:, :n], ALU.subtract).then_inc(s_evV, 1)
                dve.wait_ge(s_evV, read_by(m0 + 2, "V"))
                vt.tensor_scalar(msq[:, :n], msq[:, :n], 0.0, EPS, ALU.max, ALU.add).then_inc(s_var, 1)

            def norm_apply(L, h):
                c0, n = HALF[h]
                idx = 2 * L + h

                def pair(a, t):
                    return a[:, 2 * t:2 * t + 2, c0:c0 + n]

                def wide(a):
                    return a[:, 0:n].rearrange("p (o n) -> p o n", o=1).broadcast_to([128, 2, n])

                def low(k):
                    if L == 3:
                        return
                    dve.wait_ge(s_y, 8 * idx + k + 1)
                    vt.tensor_tensor(x_lo[:, k, c0:c0 + n], y_tmp[:, k % 2, :n],
                                     x_hi[:, k, c0:c0 + n].bitcast(F32), ALU.subtract).then_inc(s_ylo, 1)

                for t in range(4):
                    seq[0] += 1
                    vt.tensor_tensor(pair(acc, t), pair(acc, t), wide(mean), ALU.subtract).then_inc(s_seqV, 1)
                centred = seq[0]
                dve.wait_ge(s_std, idx + 1)
                ordered(vt.reciprocal(rstd[:, :n], rstd[:, :n]))
                for t in range(4):
                    vt.tensor_tensor(pair(acc, t), pair(acc, t), wide(rstd), ALU.mult).then_inc(s_xhat, 1)
                    if t:
                        low(2 * t - 2)
                        low(2 * t - 1)
                low(6)
                low(7)

            def add_tiles(L, h, ms, name):
                for k, m in enumerate(ms):
                    n0 = mark[name] + k
                    tile_done(L, h, m, unit(n0), read_by(n0 + 1, "V"))

            def project(l):
                L = 2 * l
                if l == 0:
                    dve.wait_ge(s_res0, 2)
                else:
                    dve.wait_ge(s_res, 8 * 4)
                for m in range(4):
                    if l == 0:
                        split([job_at[("o", 0, 1)][0] + m])
                    if l == 0 and m == 1:
                        gated(7)
                        recur(7)
                    n0 = mark[("o", l, 0, 0, 0 if m < 2 else 2)] + m % 2
                    tile_done(L, 0, m, unit(n0), read_by(n0 + 1, "V"))
                add_tiles(L, 1, range(4), ("o", l, 0, 1, 0))
                for m in range(4, 8):
                    n0 = mark[("o", l, 1, 0, 0)] + m - 4
                    tile_done(L, 0, m, unit(n0), read_by(n0 + 1, "V"))
                    if m in (5, 7):
                        split([job_at[("mlp", l)][0] + m // 2 - 2])
                for m in range(4, 8):
                    if m == 6:
                        split([job_at[("mlp", l)][0] + 2, job_at[("mlp", l)][0] + 3])
                        norm_stats(L, 0)
                        norm_apply(L, 0)
                    n0 = mark[("o", l, 1, 1, 0 if m < 6 else 2)] + m - (4 if m < 6 else 6)
                    tile_done(L, 1, m, unit(n0), read_by(n0 + 1, "V"))
                norm_stats(L, 1)
                norm_apply(L, 1)

            def up(l, q, i=None):
                c = CHUNKS - 1 if i is None else 0
                it = 0 if i is None else i
                c0, n = HALF[q // 4]
                n0 = mark[("mlp", l)] + 24 * c + q
                t0 = (CHUNKS * l + c) * 8 + q
                dve.wait_ge(s_evA, it * 8 + read_by(n0 + 1, "A"))
                dve.wait_ge(s_hlo, it * 8 + (t0 + 1))
                vt.tensor_tensor(h_sq[:, q % 2, :n], relu[:, q % 2, :n], relu[:, q % 2, :n], ALU.mult)\
                    .then_inc(s_hsq, 1)
                dve.wait_ge(s_hhi, it * 8 + (t0 + 1))
                dve.wait_ge(s_hsq, it * 8 + (t0 + 3))
                vt.tensor_tensor(m_lo[:, q % 4, c0:c0 + n], h_sq[:, q % 2, :n],
                                 m_hi[:, q % 4, c0:c0 + n].bitcast(F32), ALU.subtract).then_inc(s_hlo, 1)

            def mlp(l):
                j0 = job_at[("mlp", l)][0]
                dve.wait_ge(s_res, 8 * (4 * l + 2))
                with dve.Fori(0, CHUNKS - 1) as i:
                    for q in range(8):
                        if q % 2 == 0:
                            split([j0 + 4 + q // 2], i, 8)
                        up(l, q, i)
                    for q in range(16):
                        c0, n = HALF[q // 8]
                        n0 = mark[("mlp", l)] + 8 + q
                        dve.wait_ge(s_unit, i * 24 + (n0 + 1))
                        dve.wait_ge(s_evV, i * 16 + (read_by(n0, "V") - 8))
                        vt.tensor_tensor(acc[:, q % 8, c0:c0 + n], bank[:, n0 % BANKS, :n],
                                         acc[:, q % 8, c0:c0 + n], ALU.add).then_inc(s_evV, 1)
                        if q % 4 == 1:
                            split([j0 + 8 + q // 4], i, 8)
                last = j0 + 8 * (CHUNKS - 1)
                for q in range(8):
                    if q % 2 == 0:
                        split([last + 4 + q // 2])
                    up(l, q)
                L = 2 * l + 1
                add_tiles(L, 0, range(8), ("down", l, 0))
                if l == 0:
                    split(range(job_at[("qkv", 0)][0], job_at[("qkv", 0)][0] + 4))
                add_tiles(L, 1, range(2), ("down", l, 1, 0))
                norm_stats(L, 0)
                norm_apply(L, 0)
                add_tiles(L, 1, range(2, 8), ("down", l, 1, 2))

            project(0)
            mlp(0)
            norm_stats(1, 1)
            norm_apply(1, 1)
            split(range(job_at[("qkv", 1)][0], job_at[("qkv", 1)][0] + 6))
            oj = job_at[("o", 1, 0)][0]

            def mask_max(T):
                w = step_width(T)
                st = stat[:, T % 2]
                dve.wait_ge(s_sc, T + 1)
                if T >= 2:
                    dve.wait_ge(s_pt, T - 1)
                pr = probs[:, T % 2, :, 0:w]
                src = bank[:, 2 * (T % 2):2 * (T % 2) + 2, :].rearrange("p v (i c) -> p (v i) c", i=2)[:, :, 0:w]
                if T < 16:
                    mk = V("mask", 2 * WIN - w, w).rearrange("p (o c) -> p o c", o=1).broadcast_to([128, 4, w])
                    vt.tensor_tensor(pr, src, mk, ALU.add).then_inc(s_sm, 1)
                else:
                    mk = V("mask_rows", 0, 2 * w).rearrange("p (b c) -> p b c", b=2)
                    for v in range(2):
                        ins = vt.tensor_tensor(pr[:, 2 * v:2 * v + 2, :], src[:, 2 * v:2 * v + 2, :], mk, ALU.add)
                        if v == 0:
                            seq[0] += 1
                            ins.then_inc(s_seqV, 1)
                    ins.then_inc(s_sm, 1)
                sink = V("sinks", 4 * (T // 4), 4) if T < 16 else V("sink_rows", 0, 4)
                dve.wait_ge(s_sm, T + 1)
                ordered(vt.tensor_reduce(st[:, 0, :], pr, AX.X, ALU.max))
                ordered(vt.tensor_tensor(st[:, 0, :], st[:, 0, :], sink, ALU.max))
                seq[0] += 1
                vt.tensor_tensor(st[:, 3, :], sink, st[:, 0, :], ALU.subtract).then_inc(s_seqV, 1)
                vt.tensor_scalar(st[:, 1, :], st[:, 0, :], -1.0, None, ALU.mult).then_inc(s_max, 1)

            def normalise(T):
                w = step_width(T)
                st = stat[:, T % 2]
                dve.wait_ge(s_exp, T + 1)
                ordered(vt.tensor_tensor(st[:, 5, :], st[:, 2, :], st[:, 4, :], ALU.add))
                ordered(vt.reciprocal(st[:, 6, :], st[:, 5, :]))
                for e in range(4):
                    ins = vt.tensor_scalar(probs[:, T % 2, e, 0:w], probs[:, T % 2, e, 0:w], st[:, 6, e:e + 1], None,
                                           ALU.mult)
                    if e < 3:
                        seq[0] += 1
                        ins.then_inc(s_seqV, 1)
                ins.then_inc(s_nrm, 1)

            mask_max(0)
            for T in range(17):
                if T < 16:
                    mask_max(T + 1)
                normalise(T)
                if T % 2 == 0 and T < 16:
                    split([oj + T // 2])
                dve.wait_ge(s_pt, T + 1)
                if T:
                    dve.wait_ge(s_pv, T)
                rows = NS if T == 16 else 128
                if step_width(T) > WIN:
                    vt.tensor_copy(probs_t[0:rows, 1, :], bank[0:rows, 5, :]).then_inc(s_ptV, 1)
                dve.wait_ge(s_ohi, T + 1)
                dst, src = mixed(T, x_lo)
                hi, _ = mixed(T, x_hi)
                vt.tensor_tensor(dst, src, hi.bitcast(F32), ALU.subtract).then_inc(s_olo, 1)
            project(1)
            mlp(1)
            norm_stats(3, 1)
            norm_apply(3, 1)

        @block.gpsimd
        def _(pool):
            pt = nc.gpsimd
            seq = [0]
            pool.wait_ge(s_vec, 16)
            def residual0(h):
                c0, n = HALF[h]
                for k in range(KT):
                    pool.wait_ge(s_xlo, 2 * h + k // 4 + 1)
                    ins = pt.tensor_scalar(acc[:, k, c0:c0 + n], acc[:, k, c0:c0 + n], ALPHA, V("b_out", k),
                                           ALU.mult, ALU.add)
                    if k < KT - 1:
                        ins.then_inc(s_seqP, 1)
                ins.then_inc(s_res0, 1)
            residual0(0)
            residual0(1)

            def low_product(s):
                p, (c0, n) = s // 2, HALF[s % 2]
                pool.wait_ge(s_phi, s + 1)
                pt.tensor_tensor(m_lo[:, 2 * p:2 * p + 2, c0:c0 + n], z[:, s % 2, :, :n],
                                 m_hi[:, 2 * p:2 * p + 2, c0:c0 + n].bitcast(F32), ALU.subtract).then_inc(s_plo, 1)

            for s in range(8):
                p, h = s // 2, s % 2
                c0, n = HALF[h]
                if s:
                    low_product(s - 1)
                pool.wait_ge(s_evA, read_by(mark[("x", s)] + 2, "A"))
                if s:
                    pool.wait_ge(s_gated, s)
                    pool.wait_ge(s_xclo, s)
                for t in range(2):
                    m = 2 * p + t
                    ins = pt.tensor_scalar(xc[:, t, 0:256], u[:, t, 0:256], V("conv_w", m), V("conv_b", m),
                                           ALU.mult, ALU.add)
                    if h == 1:
                        ins.then_inc(s_seqP, 1)
                        ins = pt.tensor_scalar(xc[:, t, 256:n].rearrange("p (b t) -> p b t", t=DEC_T),
                                               us[:, t, :, 0:DEC_T], V("conv_w", m), V("conv_b", m),
                                               ALU.mult, ALU.add)
                    if t == 0:
                        ins.then_inc(s_seqP, 1)
                ins.then_inc(s_conv0, 1)
                pool.wait_ge(s_xchi, s + 1)
                if s:
                    pool.wait_ge(s_unit, mark[("gate", s - 1)] + 4)
                pt.tensor_tensor(xc_lo[:, :, :n], xc[:, :, :n], xc_hi[:, :, :n].bitcast(F32), ALU.subtract)\
                  .then_inc(s_xclo, 1)

            def add_square(L, h, m):
                _, n = HALF[h]
                pos = tile_pos(L, h, m)
                s2 = sums[h][1]
                pool.wait_ge(s_sqt, pos + 1)
                if pos:
                    pool.wait_ge(s_s2, pos)
                pt.tensor_tensor(s2[:, :n], sqt[:, pos % 2, :n], zeros[:, :n] if m == 0 else s2[:, :n], ALU.add)\
                  .then_inc(s_s2, 1)

            def norm_apply(L, h):
                c0, n = HALF[h]
                idx = 2 * L + h
                for k in range(KT):
                    g, b = V("ln_g", L * KT + k), V("ln_b", L * KT + k)
                    a = acc[:, k, c0:c0 + n]
                    if L == 3:
                        if k % 2:
                            pool.wait_ge(s_xhat, 4 * idx + k // 2 + 1)
                            pt.tensor_scalar(a, a, g, b, ALU.mult, ALU.add).then_inc(s_yout[1], 1)
                        continue
                    pool.wait_ge(s_yhi, 8 * idx + k + 1)
                    if 8 * idx + k >= 2:
                        pool.wait_ge(s_ylo, 8 * idx + k - 1)
                    pt.tensor_scalar(y_tmp[:, k % 2, :n], a, g, b, ALU.mult, ALU.add).then_inc(s_y, 1)
                    pool.wait_ge(s_y, 8 * idx + k + 1)
                    pt.tensor_scalar(a, a, dv[:, 5 + L, k:k + 1], dv[:, 8 + L, k:k + 1], ALU.mult, ALU.add)\
                      .then_inc(s_res, 1)

            def project(l):
                L = 2 * l
                for m in range(4):
                    if l == 0 and m == 1:
                        low_product(7)
                    add_square(L, 0, m)
                for m in range(4):
                    add_square(L, 1, m)
                for m in range(4, 8):
                    add_square(L, 0, m)
                add_square(L, 1, 4)
                add_square(L, 1, 5)
                norm_apply(L, 0)
                add_square(L, 1, 6)
                add_square(L, 1, 7)
                norm_apply(L, 1)

            def mlp(l):
                L = 2 * l + 1
                for m in range(8):
                    add_square(L, 0, m)
                for m in range(8):
                    if m == 2:
                        norm_apply(L, 0)
                    add_square(L, 1, m)
                norm_apply(L, 1)

            project(0)
            pool.dma_start(kc_t[:, :, :], ck_t).then_inc(s_cache, 16)
            pool.dma_start(vc[:, :, :], cache_v.rearrange("b s c -> s b c")).then_inc(s_cache, 16)
            pool.dma_start(k_s[:, 0:WIN - DEC_T, :], cache_k[:, DEC_T:WIN, :]).then_inc(s_kept, 16)
            pool.dma_start(v_s[:, 0:WIN - DEC_T, :], cache_v[:, DEC_T:WIN, :]).then_inc(s_kept, 16)
            pool.dma_start(small, out_small[:, :, :]).then_inc(s_kept, 16)
            mlp(0)
            pool.wait_ge(s_tokc, 3)
            pool.dma_start(k_p, k_tok[:, :]).then_inc(s_kept, 16)
            pool.dma_start(v_p, v_tok[:, NB - 1, :]).then_inc(s_kept, 16)
            for n, dst in ((0, k_s), (1, v_s)):
                for b in range(DEC_B):
                    pool.dma_start(dst[b, WIN - DEC_T:WIN, :], kv_new[DEC_T * b:DEC_T * b + DEC_T, n, :])\
                        .then_inc(s_kept, 16)
            pool.wait_ge(s_kept, 16 * (5 + 2 * DEC_B))
            project(1)
            mlp(1)

        @block.tensor
        def _(pe):
            mm = nc.tensor.matmul

            def free_bank(n):
                prev = n - BANKS
                if prev >= floor[0]:
                    who = reader[prev]
                    pe.wait_ge(s_evA if who == "A" else s_evV, read_by(prev + 1, who))

            floor = [0]

            def product(n, width, pieces, done=None):
                out = bank[:, n % BANKS, :width]
                last = len(pieces) - 1
                for k, (wh, wl, xh, xl) in enumerate(pieces):
                    mm(out, wh, xh, start=(k == 0), stop=False)
                    mm(out, wh, xl, start=False, stop=False)
                    ins = mm(out, wl, xh, start=False, stop=(k == last))
                ins.then_inc(s_unit, 1)

            def slab(w0, k, off):
                s = (w0 + k) % SLOTS
                return w_hi[:, s, off:off + 128], w_lo[:, s, off:off + 128]

            def act_cols(hi, lo, k, h):
                c0, n = HALF[h]
                return hi[:, k, c0:c0 + n], lo[:, k, c0:c0 + n]

            def pair_unit(n, w0, t, h):
                free_bank(n)
                product(n, HALF[h][1], [(*slab(w0, k // 4, 256 * (k % 4) + 128 * t), *act_cols(x_hi, x_lo, k, h))
                                        for k in range(KT)])

            def quad_pieces(w0, t, h, hi=x_hi, lo=x_lo):
                return [(*slab(w0, k // 2, 512 * (k % 2) + 128 * t), *act_cols(hi, lo, k, h)) for k in range(KT)]

            def down_pieces(w0, m, h):
                return [(*slab(w0, k, 128 * m), *act_cols(m_hi, m_lo, k, h)) for k in range(4)]

            def gates(s):
                p, h = s // 2, s % 2
                n = HALF[h][1]
                pe.wait_ge(s_wlo, job_at[("gates", p)][0] + 1)
                pe.wait_ge(s_xclo, s + 1)
                for t in range(2):
                    for g in range(2):
                        n0 = mark[("gate", s)] + 2 * t + g
                        free_bank(n0)
                        off = 256 * t + 128 * g
                        product(n0, n, [(gate_hi[:, p % 2, off:off + 128], gate_lo[:, p % 2, off:off + 128],
                                         xc_hi[:, t, :n], xc_lo[:, t, :n])])

            def norm_sums(L, h):
                _, n = HALF[h]
                n0 = mark[("ln", L, h)]
                pe.wait_ge(s_s1, tile_pos(L, h, 7) + 1)
                free_bank(n0)
                mm(bank[:, n0 % BANKS, :n], ones[:, :], sums[h][0][:, :n], start=True, stop=True).then_inc(s_unit, 1)
                pe.wait_ge(s_s2, tile_pos(L, h, 7) + 1)
                free_bank(n0 + 1)
                mm(bank[:, (n0 + 1) % BANKS, :n], ones[:, :], sums[h][1][:, :n], start=True, stop=True)\
                    .then_inc(s_unit, 1)

            pe.wait_ge(s_const, 2)
            for s in range(8):
                p, h = s // 2, s % 2
                if s < 2:
                    pe.wait_ge(s_xlo, 2 * h + 2)
                j, w0 = job_at[("pair", p)]
                pe.wait_ge(s_wlo, j + 2)
                for t in range(2):
                    pair_unit(mark[("y", s)] + t, w0, t, h)
                if s:
                    gates(s - 1)
                pe.wait_ge(s_wlo, j + 4)
                for t in range(2):
                    pair_unit(mark[("x", s)] + t, w0 + 2, t, h)

            def project(l):
                L = 2 * l
                for g in range(2):
                    j, w0 = job_at[("o", l, g)]
                    pe.wait_ge(s_wlo, j + 4)
                    for h in range(2):
                        if l == 0 and g == 0 and h == 0:
                            pe.wait_ge(s_plo, 7)
                        if l == 0 and g == 0 and h == 1:
                            pe.wait_ge(s_plo, 8)
                        for t in range(4):
                            split_here = (g == 0 and h == 0) or (g == 1 and h == 1)
                            base = mark[("o", l, g, h, 2 if split_here and t >= 2 else 0)]
                            n0 = base + (t - 2 if split_here and t >= 2 else t)
                            if l == 0 and g == 0 and h == 0 and t == 2:
                                gates(7)
                            if g == 1 and h == 1 and t == 2:
                                norm_sums(L, 0)
                            free_bank(n0)
                            src = (m_hi, m_lo) if l == 0 else (x_hi, x_lo)
                            product(n0, HALF[h][1], quad_pieces(w0, t, h, *src))
                norm_sums(L, 1)

            def mlp(l):
                j0, w0 = job_at[("mlp", l)]
                n0 = mark[("mlp", l)]
                pe.wait_ge(s_evA, read_by(n0, "A"))
                pe.wait_ge(s_evV, read_by(n0, "V"))
                pe.wait_ge(s_ylo, 8 * (4 * l + 1))

                def chunk(i):
                    c = CHUNKS - 1 if i is None else 0
                    it = 0 if i is None else i
                    b0 = n0 + 24 * c
                    t0 = (CHUNKS * l + c) * 8
                    a0, v0 = read_by(b0, "A"), read_by(b0, "V")
                    pe.wait_ge(s_wlo, it * 8 + (j0 + 8 * c + 4))
                    for q in range(8):
                        if q == 4:
                            pe.wait_ge(s_ylo, 8 * (4 * l + 2))
                        pe.wait_ge(s_evV, it * 16 + (v0 - 7 + q))
                        product(b0 + q, HALF[q // 4][1], quad_pieces(w0, q % 4, q // 4))
                    pe.wait_ge(s_wlo, it * 8 + (j0 + 8 * c + 8))
                    for q in range(16):
                        h, m = q // 8, q % 8
                        if m == 0:
                            pe.wait_ge(s_hlo, it * 8 + (t0 + 4 * h + 6))
                        if q < 8:
                            pe.wait_ge(s_evA, it * 8 + (a0 + q + 1))
                        elif q < 10 or i is not None:
                            pe.wait_ge(s_evV, it * 16 + (v0 + q - 7))
                        extra = 0
                        if i is None and q >= 10:
                            extra = 2
                            free_bank(b0 + 8 + q + 2)
                        if i is None and q == 10:
                            norm_sums(2 * l + 1, 0)
                        product(b0 + 8 + q + extra, HALF[h][1], down_pieces(w0 + 4, m, h))

                with pe.Fori(0, CHUNKS - 1) as i:
                    chunk(i)
                chunk(None)

            project(0)
            mlp(0)
            for g in range(3):
                j, w0 = job_at[("qkv", g)]
                nu = 4 if g < 2 else 2
                pe.wait_ge(s_wlo, j + nu)
                for h in range(2):
                    if g == 0:
                        pe.wait_ge(s_ylo, 8 * (2 + h + 1))
                    for t in range(nu):
                        part = 2 if (g, h) == (0, 0) and t >= 2 else 0
                        if (g, h, t) == (0, 0, 2):
                            norm_sums(1, 1)
                        n0 = mark[("qkv", g, h, part)] + t - part
                        if g < 2:
                            free_bank(n0)
                            product(n0, HALF[h][1], quad_pieces(w0, t, h))
                        else:
                            pair_unit(n0, w0, t, h)
            ident = V("ident", 0, 128)
            pe.wait_ge(s_evA, read_by(mark["attention"], "A"))
            pe.wait_ge(s_evV, read_by(mark["attention"], "V"))
            pe.wait_ge(s_cache, 32)

            def scores(T):
                b0 = 2 * (T % 2)
                if T >= 2:
                    pe.wait_ge(s_sm, T - 1)
                if T < 16:
                    n = T % 4
                    lo = 0 if n == 0 else WIN * (n - 1)
                    w = step_width(T)
                    for v in range(2):
                        for e in range(2):
                            ins = mm(bank[:, b0 + v, 256 * e:256 * e + w],
                                     q_tile(2 * (T // 4) + e)[HD * v:HD * v + HD, WIN * n:WIN * n + WIN],
                                     k_t[HD * v:HD * v + HD, lo:lo + w], start=True, stop=True)
                else:
                    for v in range(2):
                        for bq in range(2):
                            for j in range(4):
                                b = 4 * bq + j
                                out = bank[32 * j:32 * j + 32, b0 + v, 256 * bq:256 * bq + WIN + NS]
                                qs = q_s[HD * v:HD * v + HD, b, :, :]
                                mm(out[:, 0:WIN], qs, kc_t[HD * v:HD * v + HD, b, :], start=True, stop=True)
                                ins = mm(out[:, WIN:WIN + NS], qs, k_t[HD * v:HD * v + HD, SEQ:TOK],
                                         start=True, stop=True)
                ins.then_inc(s_sc, 1)

            for n in range(NB):
                ins = nc.tensor.transpose(bank[:, 4, 128 * n:128 * n + 128], v_t[:, 128 * n:128 * n + 128], ident)
            ins.then_inc(s_tok, 1)
            nc.tensor.transpose(bank[:, 5, 0:128], k_t[:, SEQ - 128:SEQ], ident)
            nc.tensor.transpose(bank[0:NS, 5, 128:256], k_t[:, SEQ:TOK], ident)
            nc.tensor.transpose(bank[0:NS, 5, 256:384], v_t[:, SEQ:TOK], ident).then_inc(s_tok, 1)
            pe.wait_ge(s_tokc, 3)
            scores(0)
            scores(1)
            for T in range(17):
                w = step_width(T)
                pe.wait_ge(s_nrm, T + 1)
                if T:
                    pe.wait_ge(s_ptA, T)
                    if wide_steps(T):
                        pe.wait_ge(s_ptV, wide_steps(T))
                for kb in range(2 if w > WIN else 1):
                    wk = min(WIN, w - WIN * kb)
                    for e in range(4):
                        ins = nc.tensor.transpose(bank[0:wk, 4 + kb, 128 * e:128 * e + 128],
                                                  probs[:, T % 2, e, WIN * kb:WIN * kb + wk], ident)
                ins.then_inc(s_pt, 1)
                if T + 2 < 17:
                    scores(T + 2)
                pe.wait_ge(s_ptA, T + 1)
                if wide_steps(T + 1):
                    pe.wait_ge(s_ptV, wide_steps(T + 1))
                if T >= 2:
                    pe.wait_ge(s_olo, T - 1)
                for v in range(2):
                    out = bank[HD * v:HD * v + HD, 6 + T % 2, 0:256]
                    if T < 16:
                        n = T % 4
                        blocks = [n] if n == 0 else [n - 1, n]
                        for kb, blk in enumerate(blocks):
                            ins = mm(out, v_tok[:, blk, HD * v:HD * v + HD], probs_t[:, kb, 256 * v:256 * v + 256],
                                     start=(kb == 0), stop=(kb == len(blocks) - 1))
                    else:
                        for b in range(DEC_B):
                            at = 128 * (2 * v + b // 4) + 32 * (b % 4)
                            mm(out[:, 32 * b:32 * b + 32], vc[:, b, HD * v:HD * v + HD], probs_t[:, 0, at:at + 32],
                               start=True, stop=False)
                            ins = mm(out[:, 32 * b:32 * b + 32], kv_new[:, 1, HD * v:HD * v + HD],
                                     probs_t[0:NS, 1, at:at + 32], start=False, stop=True)
                ins.then_inc(s_pv, 1)
            pe.wait_ge(s_olo, 17)
            floor[0] = mark["attention"]
            project(1)
            mlp(1)
            norm_sums(3, 1)


def kernel(x_prompt, x_sample, state_lru_h, state_lru_conv, cache_swa_k, cache_swa_v,
           lru_w_x, lru_b_x, lru_w_y, lru_b_y, lru_conv_w, lru_conv_b,
           lru_w_ga, lru_b_ga, lru_w_gi, lru_b_gi, lru_lam, lru_w_out, lru_b_out,
           swa_w_qkv, swa_b_qkv, swa_sinks, swa_w_o, swa_b_o,
           mlp_w_up, mlp_w_down, ln1_g, ln1_b, ln2_g, ln2_b):
    import concourse.bacc as bacc
    from concourse.bass_utils import run_bass_kernel_spmd

    (x_prompt, x_sample, state_lru_h, state_lru_conv, cache_swa_k, cache_swa_v, lru_w_x, lru_b_x, lru_w_y, lru_b_y,
     lru_conv_w, lru_conv_b, lru_w_ga, lru_b_ga, lru_w_gi, lru_b_gi, lru_lam, lru_w_out, lru_b_out, swa_w_qkv,
     swa_b_qkv, swa_sinks, swa_w_o, swa_b_o, mlp_w_up, mlp_w_down, ln1_g, ln1_b, ln2_g, ln2_b) = map(np.asarray, (
         x_prompt, x_sample, state_lru_h, state_lru_conv, cache_swa_k, cache_swa_v, lru_w_x, lru_b_x, lru_w_y,
         lru_b_y, lru_conv_w, lru_conv_b, lru_w_ga, lru_b_ga, lru_w_gi, lru_b_gi, lru_lam, lru_w_out, lru_b_out,
         swa_w_qkv, swa_b_qkv, swa_sinks, swa_w_o, swa_b_o, mlp_w_up, mlp_w_down, ln1_g, ln1_b, ln2_g, ln2_b))

    nq = NKV * GRP * HD
    q_cols = np.arange(nq).reshape(NKV, GRP, HD).transpose(1, 0, 2).reshape(-1)
    cols = np.concatenate([np.arange(nq, nq + 2 * NKV * HD), q_cols])

    def tiles(a):
        a = a.reshape(-1, a.shape[-1] // 128, 128)
        return a.transpose(2, 0, 1).reshape(128, -1)

    def tiles_first(a):
        return a.reshape(-1, KT, 128).transpose(2, 1, 0).reshape(128, -1)

    row, col = np.arange(WIN)[:, None], np.arange(2 * WIN)[None, :]
    mask = np.where((col > row) & (col <= row + WIN), 0.0, NEG).astype(np.float32)
    j, t = np.arange(128) // 32, np.arange(128) % DEC_T
    rows = np.full((128, 2, WIN + NS), NEG, np.float32)
    for bq in range(2):
        rows[:, bq, :WIN][np.arange(WIN)[None, :] > t[:, None]] = 0.0
        c = np.arange(NS)[None, :]
        rows[:, bq, WIN:][(c // DEC_T == 4 * bq + j[:, None]) & (c % DEC_T <= t[:, None])] = 0.0
    sinks = swa_sinks.reshape(NKV, GRP)
    head_of_row = (np.arange(128) % 32) // DEC_T
    parts = {
        "b_y": tiles(lru_b_y), "b_x": tiles(lru_b_x), "conv_w": tiles(lru_conv_w[0]), "conv_b": tiles(lru_conv_b),
        "b_ga": tiles(lru_b_ga.reshape(1, D)), "b_gi": tiles(lru_b_gi.reshape(1, D)), "lam": tiles(lru_lam),
        "b_out": tiles(lru_b_out), "b_o": tiles(swa_b_o),
        "ln_g": tiles(np.stack([ln1_g[0], ln2_g[0], ln1_g[1], ln2_g[1]])),
        "ln_b": tiles(np.stack([ln1_b[0], ln2_b[0], ln1_b[1], ln2_b[1]])),
        "b_qkv": tiles(swa_b_qkv[:, cols]), "h0": tiles_first(state_lru_h[0]),
        "conv_state": tiles_first(state_lru_conv[0].reshape(-1, D)),
        "sinks": np.broadcast_to(sinks.reshape(NKV, GRP // 2, 2).transpose(1, 0, 2).reshape(1, 16), (128, 16)),
        "sink_rows": np.stack([sinks[v][head_of_row] for v in (0, 0, 1, 1)], axis=1),
        "mask": mask, "mask_rows": rows.reshape(128, -1), "ident": np.eye(128, dtype=np.float32),
    }
    vec = np.ascontiguousarray(np.concatenate([parts[n] for n in VEC], axis=1))
    kv = NKV * HD
    arrays = {
        "xp_t": x_prompt[0].T, "xs_t": x_sample.reshape(NS, D).T, "vec": vec,
        "w_y": lru_w_y[0], "w_x": lru_w_x[0], "w_ga": lru_w_ga[0], "w_gi": lru_w_gi[0], "w_out": lru_w_out[0],
        "w_qkv": swa_w_qkv[0][:, cols], "w_o": swa_w_o[0][q_cols], "w_up": mlp_w_up, "w_down": mlp_w_down,
        "ck_t": cache_swa_k[0].reshape(DEC_B, WIN, kv).transpose(2, 0, 1),
        "cache_k": cache_swa_k[0].reshape(DEC_B, WIN, kv), "cache_v": cache_swa_v[0].reshape(DEC_B, WIN, kv),
    }
    arrays = {k: np.ascontiguousarray(v) for k, v in arrays.items()}
    outs = {"y_t": (D, TOK), "small": (128, KT, 36), "k_p": (WIN, kv), "v_p": (WIN, kv),
            "k_s": (DEC_B, WIN, kv), "v_s": (DEC_B, WIN, kv)}

    nc = bacc.Bacc("TRN2", target_bir_lowering=False, num_devices=1)
    args = [nc.dram_tensor(k, v.shape, mybir.dt.from_np(v.dtype), kind="ExternalInput").ap()
            for k, v in arrays.items()]
    args += [nc.dram_tensor(k, s, F32, kind="ExternalOutput").ap() for k, s in outs.items()]
    build(nc, *args)
    got = run_bass_kernel_spmd(nc, [arrays], core_ids=[0]).results[0]

    y = got["y_t"].T
    small = got["small"].transpose(1, 0, 2).reshape(D, 36)
    h, conv = small[:, 0:9].T, small[:, 9:36].reshape(D, 9, CONV - 1).transpose(1, 2, 0)
    heads = (NKV, HD)
    return (y[:SEQ].reshape(1, SEQ, D), y[SEQ:].reshape(DEC_B, DEC_T, D),
            h[0:1].reshape(1, 1, D), conv[0:1][None],
            got["k_p"].reshape(1, 1, WIN, *heads), got["v_p"].reshape(1, 1, WIN, *heads),
            h[1:9].reshape(1, DEC_B, D), conv[1:9][None],
            got["k_s"].reshape(1, DEC_B, WIN, *heads), got["v_s"].reshape(1, DEC_B, WIN, *heads))
```

```python
import numpy as np
import concourse.bass as bass
from concourse import mybir
from contextlib import ExitStack

F32 = mybir.dt.float32
F32R = mybir.dt.float32r
ALU = mybir.AluOpType
ACT = mybir.ActivationFunctionType
AX = mybir.AxisListType

D = 1024
SEQ, DEC_B, DEC_T = 512, 8, 4
NS = DEC_B * DEC_T
TOK = SEQ + NS
KT = D // 128
DFF = 4 * D
CHUNKS = DFF // 512
WIN = 128
NB = SEQ // WIN
NKV, GRP, HD = 2, 8, 64
CONV = 4
ALPHA = float(4.0 ** 0.25)
EPS = 1e-5
GELU_IN = 1.0 / 0.044715
GELU_OUT = 0.044715 * float(np.sqrt(2.0 / np.pi))
NEG = -1.0e30

HALF = [(0, 256), (256, TOK - 256)]
HW = TOK - 256

VEC = {}
_at = 0
for _name, _cols in [("b_y", KT), ("b_x", KT), ("conv_w", CONV * KT), ("conv_b", KT), ("b_ga", KT), ("b_gi", KT),
                     ("lam", KT), ("b_out", KT), ("b_o", KT), ("ln_g", 4 * KT), ("ln_b", 4 * KT), ("b_qkv", KT + 2),
                     ("h0", KT * DEC_B), ("conv_state", KT * DEC_B * (CONV - 1)), ("sinks", 16), ("sink_rows", 4),
                     ("mask", 2 * WIN), ("mask_rows", 2 * (WIN + NS)), ("ident", 128)]:
    VEC[_name] = (_at, _cols)
    _at += _cols
NVEC = _at



def step_width(T):
    return WIN + NS if T == 16 else (WIN if T < 4 else 2 * WIN)


def wide_steps(T):
    return sum(step_width(t) > WIN for t in range(T))


def tile_pos(L, h, m):
    return 16 * L + 8 * h + m


STAGES = 4
SLOTS = 8
BANKS = 8


def build(nc, xp_t, xs_t, vec, w_y, w_x, w_ga, w_gi, w_out, w_qkv, w_o, w_up, w_down,
          ck_t, cache_k, cache_v, y_t, small, k_p, v_p, k_s, v_s):
    ctx = ExitStack()
    with ctx:
        top = [nc.sbuf_base]

        def place(name, shape, dt, at=None):
            size = int(np.prod(shape[1:])) * 4
            if at is None:
                at = (top[0] + 31) // 32 * 32
                top[0] = at + size
            t = nc.alloc_sbuf_tensor_at(name, shape, dt, offset=at)
            t_at[name] = at
            return t

        t_at = {}
        w_hi = place("w_hi", [128, SLOTS, 1024], F32R)
        w_lo = place("w_lo", [128, SLOTS, 1024], F32R)
        stage = place("stage", [128, STAGES, 1024], F32)
        x_hi = place("x_hi", [128, KT, TOK], F32R)
        x_lo = place("x_lo", [128, KT, TOK], F32R)
        m_hi = place("m_hi", [128, KT, TOK], F32R)
        m_lo = place("m_lo", [128, KT, TOK], F32R)
        acc = place("acc", [128, KT, TOK], F32)
        vecs = place("vecs", [128, NVEC], F32)
        gate_hi = place("gate_hi", [128, 2, 512], F32R)
        gate_lo = place("gate_lo", [128, 2, 512], F32R)
        xc_hi = place("xc_hi", [128, 2, HW], F32R)
        xc_lo = place("xc_lo", [128, 2, HW], F32R)
        ones = place("ones", [128, 128], F32)
        zeros = place("zeros", [128, HW], F32)
        dv = place("dv", [128, 12, KT], F32)
        tiny = place("tiny", [128, 8, KT], F32)
        out_small = place("out_small", [128, KT, 9 * 4], F32)
        scratch = (top[0] + 31) // 32 * 32
        z = place("z", [128, 2, 2, HW], F32)
        sq = place("sq", [128, 2, HW], F32)
        xc_at = place("xc_even", [128, 2, HW], F32)
        th_r = place("th_r", [128, 2, HW], F32)
        th_g = place("th_g", [128, 2, HW], F32)
        decay = place("decay", [128, 2, HW], F32)
        u = place("u", [128, 2, 3 + 256], F32)
        us = place("us", [128, 2, DEC_B, 3 + DEC_T], F32)
        sums = [[place("sum_a", [128, HW], F32, t_at["z"]), place("sumsq_a", [128, HW], F32, t_at["z"] + 4 * HW)],
                [place("sum_b", [128, HW], F32), place("sumsq_b", [128, HW], F32)]]
        sqt = place("sqt", [128, 2, HW], F32, t_at["sq"])
        xc = [xc_at, place("xc_odd", [128, 2, HW], F32, t_at["sum_b"])]
        mean = place("mean", [128, HW], F32, t_at["th_r"])
        rstd = place("rstd", [128, HW], F32, t_at["th_r"] + 4 * HW)
        msq = place("msq", [128, HW], F32, t_at["decay"])
        y_tmp = place("y_tmp", [128, 2, HW], F32, t_at["th_g"])
        relu = place("relu", [128, 2, HW], F32, t_at["xc_even"])
        h_sq = place("h_sq", [128, 2, HW], F32, t_at["z"] + 8 * HW)
        assert top[0] <= nc.sbuf_usable_end, (top[0], nc.sbuf_usable_end)
        m_half = 4 * TOK * 4
        kc_t = place("kc_t", [128, DEC_B, WIN], F32, t_at["m_hi"] + m_half)
        vc = place("vc", [128, DEC_B, WIN], F32, t_at["m_hi"] + m_half + 4096)
        v_t = place("v_t", [128, TOK], F32, t_at["m_lo"] + m_half)
        k_t = place("k_t", [128, TOK], F32, t_at["m_lo"] + m_half + 4 * TOK)
        v_tok = place("v_tok", [128, NB, 128], F32, t_at["m_lo"] + m_half + 8 * TOK)
        k_tok = place("k_tok", [128, 128], F32, t_at["m_lo"] + m_half + 8 * TOK + 2048)
        kv_new = place("kv_new", [NS, 2, 128], F32, t_at["m_lo"] + m_half + 8 * TOK + 2560)
        q_a = place("q_a", [128, 4, SEQ], F32, t_at["m_hi"])
        q_b = place("q_b", [128, 4, SEQ], F32, t_at["m_lo"])
        probs = place("probs", [128, 3, 4, 256], F32, scratch)
        scale_by = place("scale_by", [128, 2, 4, 128], F32, scratch + 3 * 4096)
        probs_t = place("probs_t", [128, 2, 2, 512], F32, t_at["gate_hi"])
        stat = place("stat", [128, 2, 8, 4], F32, t_at["xc_lo"])
        q_s = place("q_s", [128, DEC_B, KT, DEC_T], F32, t_at["xc_hi"])
        assert scratch + 16384 <= top[0]

        def q_tile(i):
            return (q_a if i < 4 else q_b)[:, i % 4, :]

        bank = ctx.enter_context(nc.psum_tensor("bank", [128, BANKS, 512], F32))

        def sem(name):
            return ctx.enter_context(nc.semaphore(name))

        s_vec = sem("vec_loaded")
        s_xa = [sem(f"x_half_a_loaded_{k}") for k in range(4)]
        s_xb = sem("x_half_b_loaded")
        s_arrived = [sem(f"slab_arrived_{i}") for i in range(STAGES)]
        s_whi, s_wlo = sem("slab_hi_done"), sem("slab_lo_done")
        s_unit = sem("unit_done")
        s_evA, s_evV = sem("read_by_scalar"), sem("read_by_vector")
        s_xhi, s_xlo, s_res0 = sem("x_hi_done"), sem("x_lo_done"), sem("residual_ready")
        s_const = sem("constants_ready")
        s_sp, s_spe = sem("softplus_in"), sem("softplus_exp")
        s_dv = sem("derived_ready")
        s_gsq, s_gin, s_gth, s_gy = sem("gelu_sq"), sem("gelu_in"), sem("gelu_tanh"), sem("gelu_y")
        s_halo, s_conv0, s_conv = sem("halo_ready"), sem("conv_first"), sem("conv_done")
        s_xchi, s_xclo = sem("xc_hi_done"), sem("xc_lo_done")
        s_dec, s_root, s_gated = sem("decay_ready"), sem("root_ready"), sem("gated_ready")
        s_drive, s_scan, s_p = sem("drive_ready"), sem("scan_done"), sem("product_ready")
        s_phi, s_plo = sem("product_hi_done"), sem("product_lo_done")
        s_sqt, s_s1, s_s2 = sem("square_ready"), sem("sum_added"), sem("square_added")
        s_var, s_std = sem("variance_ready"), sem("deviation_ready")
        s_xhat, s_yhi, s_y, s_ylo, s_res = (sem("normed"), sem("y_hi_done"), sem("y_ready"), sem("y_lo_done"),
                                            sem("residual_done"))
        s_yout = [sem("y_out_even"), sem("y_out_odd")]
        s_hhi, s_hsq, s_hlo = sem("hidden_hi"), sem("hidden_sq"), sem("hidden_lo")
        s_cache = sem("cache_loaded")
        s_tok = sem("token_major_transposed")
        s_tokc = sem("token_major_copied")
        s_sc, s_sm, s_max = sem("scores_done"), sem("scores_masked"), sem("max_ready")
        s_cent = sem("centred")
        s_exp, s_diag = sem("exp_done"), sem("diagonals_ready")
        s_pt, s_ptA, s_ptV = sem("probs_transposed"), sem("probs_t_by_scalar"), sem("probs_t_by_vector")
        s_pv, s_ohi, s_olo = sem("values_done"), sem("mixed_hi"), sem("mixed_lo")
        s_out, s_kept = sem("trunk_written"), sem("states_written")
        s_seqA, s_seqV, s_seqP = sem("scalar_order"), sem("vector_order"), sem("pool_order")

        block = ctx.enter_context(nc.Block())

        def V(name, a=0, n=1):
            at = VEC[name][0]
            return vecs[:, at + a:at + a + n]

        reader = []
        mark = {}

        def plan(name, who):
            mark[name] = len(reader)
            reader.extend(who)

        for s in range(8):
            plan(("x", s), "AA")
            if s:
                plan(("gate", s - 1), "AAAA")
            plan(("y", s), "AA")
        plan(("gate", 7), "AAAA")

        def plan_tiles(name, L):
            plan((name, L, 0, 0), "V" * 2)
            plan((name, L, 0, 2), "V" * 6)
            plan((name, L, 1, 0), "V" * 2)
            plan(("ln", L, 0), "AV")
            plan((name, L, 1, 2), "V" * 6)

        def plan_mlp(l):
            plan(("ln", 2 * l, 1), "AV")
            plan(("up", l), "A" * 8)
            plan(("loop", l), ("V" * 16 + "A" * 8) * (CHUNKS - 1))
            plan_tiles("down", 2 * l + 1)

        def unit_of(name, L, h, m):
            return mark[(name, L, h, 0 if m < 2 else 2)] + (m if m < 2 else m - 2)

        plan_tiles("o", 0)
        plan_mlp(0)
        plan(("ln", 1, 1), "AV")
        for g in range(3):
            for h in (0, 1):
                plan(("qkv", g, h), "AAAA" if g < 2 else "AA")
        mark["attention"] = len(reader)
        plan_tiles("o", 2)
        plan_mlp(1)
        plan(("ln", 3, 1), "AV")

        def read_by(n, who):
            return sum(1 for r in reader[:n] if r == who)

        yv, xv, ov, qv, pv = (w.rearrange("(k p) c -> p k c", p=128) for w in (w_y, w_x, w_out, w_qkv, w_o))
        uv = [w_up[l].rearrange("(k p) c -> p k c", p=128) for l in range(2)]
        dwv = [w_down[l].rearrange("(k p) c -> p k c", p=128) for l in range(2)]

        def quad(view, g, j):
            return view[:, 2 * j:2 * j + 2, 512 * g:512 * g + 512]

        job_at = {}
        jobs = []
        ring = [0]

        def plan_jobs(name, kinds):
            job_at[name] = (len(jobs), ring[0])
            for k in kinds:
                jobs.append((k, ring[0]))
                ring[0] += k == "w"

        for p in range(4):
            plan_jobs(("pair", p), "wwww")
            plan_jobs(("gates", p), "g")
        for g in range(2):
            plan_jobs(("o", 0, g), "wwww")
        plan_jobs(("mlp", 0), "w" * 8 * CHUNKS)
        for g, k in enumerate(["wwww", "wwww", "ww"]):
            plan_jobs(("qkv", g), k)
        for g in range(2):
            plan_jobs(("o", 1, g), "wwww")
        plan_jobs(("mlp", 1), "w" * 8 * CHUNKS)

        free_at = {}

        def frees(name, end, n=4):
            w = job_at[name][1]
            for k in range(n):
                free_at[w + k] = end

        for p in range(4):
            frees(("pair", p), mark[("y", 2 * p + 1)] + 2)
        for l in range(2):
            frees(("o", l, 0), unit_of("o", 2 * l, 1, 3) + 1)
            frees(("o", l, 1), unit_of("o", 2 * l, 1, 7) + 1)
            w0 = job_at[("mlp", l)][1]
            for c in range(CHUNKS):
                for k in range(4):
                    free_at[w0 + 8 * c + k] = mark[("up", l)] + 24 * c + 8
                    free_at[w0 + 8 * c + 4 + k] = mark[("loop", l)] + 24 * c + 16 + (2 if c == CHUNKS - 1 else 0)
        for g, n in enumerate((4, 4, 2)):
            frees(("qkv", g), mark[("qkv", g, 1)] + n, n)

        def next_jobs(s):
            p, h = s // 2, s % 2
            j = (job_at[("pair", p + 1)] if p < 3 else job_at[("o", 0, 0)])[0]
            return range(j, j + 2) if h == 0 else range(j + 2, j + (5 if p < 3 else 4))

        def score_bank(T):
            return (mark["attention"] + 2 * (T % 2)) % BANKS

        def trans_bank(kb):
            return (mark["attention"] + 4 + kb) % BANKS

        def pv_bank(T):
            return (mark["attention"] + 6 + T % 2) % BANKS

        def mixed(T, dst):
            src = bank[:, pv_bank(T), 0:256]
            if T < 16:
                n, i = T // 4, 2 * (T % 4)
                return (dst[:, i:i + 2, WIN * n:WIN * n + WIN],
                        src.rearrange("p (i q) -> p i q", i=2))
            return (dst[:, :, SEQ:TOK].rearrange("p i (b t) -> p b i t", t=DEC_T),
                    src.rearrange("p (b i t) -> p b i t", b=DEC_B, i=KT))

        @block.sync
        def _(sp):
            def load(j, src, i=None, per=0):
                if i is None:
                    if j >= STAGES:
                        sp.wait_ge(s_wlo, j - STAGES + 1)
                else:
                    sp.wait_ge(s_wlo, i * per + (j - STAGES + 1))
                n = int(np.prod(src.shape[1:]))
                dst = stage[:, j % STAGES, 0:n]
                if len(src.shape) == 3:
                    dst = dst.rearrange("p (k c) -> p k c", k=src.shape[1])
                sp.dma_start(dst, src).then_inc(s_arrived[j % STAGES], 16)

            def load_pair(name, view, c, jj=0):
                for k in range(2):
                    load(job_at[name][0] + jj + k, view[:, 4 * k:4 * k + 4, c:c + 256])

            def load_quad(name, view, g):
                for k in range(4):
                    load(job_at[name][0] + k, quad(view, g, k))

            def load_mlp(l):
                j0 = job_at[("mlp", l)][0]
                for k in range(4):
                    load(j0 + k, quad(uv[l], 0, k))
                with sp.Fori(0, CHUNKS - 1) as i:
                    for k in range(4):
                        load(j0 + 4 + k, dwv[l][:, bass.ds(i * 4 + k, 1), :], i, 8)
                    for k in range(4):
                        load(j0 + 8 + k, uv[l][:, 2 * k:2 * k + 2, bass.ds(i * 512 + 512, 512)], i, 8)
                for k in range(4):
                    load(j0 + 8 * (CHUNKS - 1) + 4 + k, dwv[l][:, 4 * (CHUNKS - 1) + k, :])

            def load_x(k):
                sp.dma_start(acc[:, 2 * k:2 * k + 2, 0:256],
                             xp_t[256 * k:256 * k + 256, 0:256].rearrange("(k p) t -> p k t", p=128))\
                    .then_inc(s_xa[k], 16)

            load_x(0)
            load(0, xv[:, 0:4, 0:256])
            for k in (1, 2):
                load_x(k)
            load(1, xv[:, 4:8, 0:256])
            load_x(3)
            load_pair(("pair", 0), yv, 0, 2)
            for p in range(4):
                if p == 0:
                    sp.dma_start(acc[:, :, 256:512],
                                 xp_t[:, 256:512].rearrange("(k p) t -> p k t", p=128)).then_inc(s_xb, 16)
                    sp.dma_start(acc[:, :, 512:TOK], xs_t.rearrange("(k p) t -> p k t", p=128)).then_inc(s_xb, 16)
                else:
                    load_pair(("pair", p), xv, 256 * p)
                    load_pair(("pair", p), yv, 256 * p, 2)
                j = job_at[("gates", p)][0]
                sp.wait_ge(s_wlo, j - STAGES + 1)
                dst = stage[:, j % STAGES, 0:512].rearrange("p (b g c) -> p b g c", b=2, g=2)
                for n, w in enumerate((w_ga, w_gi)):
                    sp.dma_start(dst[:, :, n, :], w[2 * p:2 * p + 2].rearrange("b i j -> i b j"))\
                      .then_inc(s_arrived[j % STAGES], 16)
            for g in range(2):
                load_quad(("o", 0, g), ov, g)
            load_mlp(0)
            for g in range(2):
                load_quad(("qkv", g), qv, g)
            load_pair(("qkv", 2), qv, 1024)
            for g in range(2):
                load_quad(("o", 1, g), pv, g)
            load_mlp(1)
            for h, (c0, n) in enumerate(HALF):
                for k in range(KT):
                    sp.wait_ge(s_yout[k % 2], 4 * h + k // 2 + 1)
                    sp.dma_start(y_t[128 * k:128 * k + 128, c0:c0 + n], acc[:, k, c0:c0 + n]).then_inc(s_out, 16)
            sp.wait_ge(s_out, 16 * 2 * KT)
            sp.wait_ge(s_kept, 16 * (5 + 2 * DEC_B))

        arrivals = []
        count = [0] * STAGES
        for j, (kind, _) in enumerate(jobs):
            count[j % STAGES] += 32 if kind == "g" else 16
            arrivals.append(count[j % STAGES])

        def split_targets(j):
            kind, w = jobs[j]
            if kind == "g":
                p = (j - 4) // 5
                return gate_hi[:, p % 2, :], gate_lo[:, p % 2, :], stage[:, j % STAGES, 0:512]
            return w_hi[:, w % SLOTS, :], w_lo[:, w % SLOTS, :], stage[:, j % STAGES, :]

        @block.scalar
        def _(act):
            A = nc.scalar.activation
            seq = [0]

            def ordered(ins):
                seq[0] += 1
                ins.then_inc(s_seqA, 1)
                return seq[0]

            def split(js, i=None, per=0, per_units=0, freed=0):
                for j in js:
                    hi, _, raw = split_targets(j)
                    kind, w = jobs[j]
                    if i is None:
                        act.wait_ge(s_arrived[j % STAGES], arrivals[j])
                        if kind == "w" and w >= SLOTS:
                            act.wait_ge(s_unit, free_at[w - SLOTS])
                        if kind == "g" and j >= 14:
                            act.wait_ge(s_unit, mark[("gate", 2 * ((j - 4) // 5) - 3)] + 4)
                    else:
                        act.wait_ge(s_arrived[j % STAGES], i * (16 * per // STAGES) + arrivals[j])
                        act.wait_ge(s_unit, i * per_units + freed)
                    A(hi, raw, ACT.Copy).then_inc(s_whi, 1)

            def unit(n):
                act.wait_ge(s_unit, n + 1)
                return bank[:, n % BANKS, :]

            def x_split(h, ks=range(4)):
                c0, n = HALF[h]
                for k in ks:
                    if h == 0:
                        act.wait_ge(s_xa[k], 16)
                    elif k == 0:
                        act.wait_ge(s_xb, 32)
                    A(x_hi[:, 2 * k:2 * k + 2, c0:c0 + n], acc[:, 2 * k:2 * k + 2, c0:c0 + n], ACT.Copy)\
                        .then_inc(s_xhi, 1)

            act.dma_start(vecs[:, :], vec).then_inc(s_vec, 16)
            x_split(0, [0])
            split([0])
            x_split(0, [1, 2])
            split([1])
            x_split(0, [3])
            split([2, 3])
            act.wait_ge(s_sp, 1)
            A(tiny[:, 2, :], tiny[:, 1, :], ACT.Exp, scale=-1.0).then_inc(s_spe, 1)
            act.wait_ge(s_dv, 1)

            def chain(s):
                p, (_, n) = s // 2, HALF[s % 2]
                m0 = mark[("gate", s)]
                if s >= 1:
                    act.wait_ge(s_p, s)
                for t in range(2):
                    m = 2 * p + t
                    A(th_r[:, t, :n], unit(m0 + 2 * t)[:, :n], ACT.Tanh, bias=dv[:, 0, m:m + 1], scale=0.5)\
                        .then_inc(s_evA, 1)
                    A(th_g[:, t, :n], unit(m0 + 2 * t + 1)[:, :n], ACT.Tanh, bias=dv[:, 1, m:m + 1], scale=0.5)\
                        .then_inc(s_evA, 1)
                act.wait_ge(s_evA, read_by(m0 + 4, "A"))
                for t in range(2):
                    m = 2 * p + t
                    last = ordered(A(decay[:, t, :n], th_r[:, t, :n], ACT.Exp, bias=dv[:, 2, m:m + 1],
                                     scale=dv[:, 2, m:m + 1]))
                act.wait_ge(s_seqA, last)
                for t in range(2):
                    m = 2 * p + t
                    last = ordered(A(th_r[:, t, :n], th_r[:, t, :n], ACT.Tanh, bias=dv[:, 3, m:m + 1],
                                     scale=dv[:, 3, m:m + 1]))
                return last

            def chain_root(s, last):
                _, n = HALF[s % 2]
                act.wait_ge(s_seqA, last)
                A(th_r[:, :, :n], th_r[:, :, :n], ACT.Sqrt).then_inc(s_root, 1)

            def chain_hi(s):
                p, (c0, n) = s // 2, HALF[s % 2]
                act.wait_ge(s_p, s + 1)
                A(m_hi[:, 2 * p:2 * p + 2, c0:c0 + n], z[:, s % 2, :, :n], ACT.Copy).then_inc(s_phi, 1)

            def copy_u(s, t):
                p, h = s // 2, s % 2
                n = HALF[h][1]
                src = unit(mark[("x", s)] + t)
                if h == 1:
                    ordered(A(us[:, t, :, 3:], src[:, 256:n].rearrange("p (b t) -> p b t", t=DEC_T),
                              ACT.Identity, bias=V("b_x", 2 * p + t)))
                A(u[:, t, 3:3 + 256], src[:, 0:256], ACT.Identity, bias=V("b_x", 2 * p + t)).then_inc(s_evA, 1)

            def gelu_in(s, t):
                p, (_, n) = s // 2, HALF[s % 2]
                A(z[:, s % 2, t, :n], unit(mark[("y", s)] + t)[:, :n], ACT.Identity,
                  bias=V("b_y", 2 * p + t)).then_inc(s_evA, 1)
                if t:
                    act.wait_ge(s_evA, read_by(mark[("y", s)] + 2, "A"))
                    if s >= 1:
                        act.wait_ge(s_gy, s)
                    A(sq[:, :, :n], z[:, s % 2, :, :n], ACT.Square).then_inc(s_gsq, 1)

            def gelu_tanh(s):
                _, n = HALF[s % 2]
                act.wait_ge(s_gin, s + 1)
                A(sq[:, :, :n], sq[:, :, :n], ACT.Tanh, scale=GELU_OUT).then_inc(s_gth, 1)

            for s in range(8):
                _, n = HALF[s % 2]
                act.wait_ge(s_halo, s + 1)
                copy_u(s, 0)
                if s:
                    split(next_jobs(s)[:1])
                copy_u(s, 1)
                if s == 0:
                    x_split(1)
                    split([4])
                    act.wait_ge(s_dv, 1)
                    split(next_jobs(s)[:1])
                if s >= 1:
                    gelu_tanh(s - 1)
                if s >= 2:
                    chain_hi(s - 2)
                if s >= 1:
                    last = chain(s - 1)
                act.wait_ge(s_conv, s + 1)
                if s >= 1:
                    act.wait_ge(s_unit, mark[("gate", s - 1)] + 4)
                A(xc_hi[:, :, :n], xc[s % 2][:, :, :n], ACT.Copy).then_inc(s_xchi, 1)
                if s >= 2:
                    act.wait_ge(s_plo, s - 1)
                gelu_in(s, 0)
                if s >= 1:
                    chain_root(s - 1, last)
                gelu_in(s, 1)
                split(next_jobs(s)[1:])
            chain_hi(6)
            split(range(job_at[("o", 0, 1)][0], job_at[("o", 0, 1)][0] + 4))
            gelu_tanh(7)
            chain_root(7, chain(7))
            chain_hi(7)

            def square(L, h, m):
                c0, n = HALF[h]
                pos = tile_pos(L, h, m)
                act.wait_ge(s_s1, pos + 1)
                if pos >= 2:
                    act.wait_ge(s_s2, pos - 1)
                A(sqt[:, pos % 2, :n], acc[:, m, c0:c0 + n], ACT.Square).then_inc(s_sqt, 1)

            def norm_stats(L, h):
                _, n = HALF[h]
                m0 = mark[("ln", L, h)]
                idx = 2 * L + h
                if idx:
                    act.wait_ge(s_xhat, 4 * idx)
                A(mean[:, :n], unit(m0)[:, :n], ACT.Copy).then_inc(s_evA, 1)
                act.wait_ge(s_var, idx + 1)
                A(rstd[:, :n], msq[:, :n], ACT.Sqrt).then_inc(s_std, 1)

            def norm_apply(L, h):
                c0, n = HALF[h]
                idx = 2 * L + h
                for k in range(KT):
                    act.wait_ge(s_xhat, 4 * idx + k // 2 + 1)
                    g, b = V("ln_g", L * KT + k), V("ln_b", L * KT + k)
                    xhat = acc[:, k, c0:c0 + n]
                    if L < 3:
                        A(x_hi[:, k, c0:c0 + n], xhat, ACT.Identity, bias=b, scale=g).then_inc(s_yhi, 1)
                        if 8 * idx + k >= 2:
                            act.wait_ge(s_ylo, 8 * idx + k - 1)
                        A(y_tmp[:, k % 2, :n], xhat, ACT.Identity, bias=b, scale=g).then_inc(s_y, 1)
                    elif k % 2 == 0:
                        A(xhat, xhat, ACT.Identity, bias=b, scale=g).then_inc(s_yout[0], 1)

            def tiles(L, jobs_at):
                for h in range(2):
                    for m in range(KT):
                        split(jobs_at.get((h, m), ()))
                        square(L, h, m)
                        if (h, m) == (1, 1):
                            norm_stats(L, 0)
                            norm_apply(L, 0)

            def up(l, q, c=0, i=0):
                c0, n = HALF[q // 4]
                n0 = mark[("up", l)] + 24 * c + q
                t0 = (CHUNKS * l + c) * 8 + q
                act.wait_ge(s_unit, i * 24 + (n0 + 1))
                act.wait_ge(s_hsq, i * 8 + (t0 + 1))
                A(relu[:, q % 2, :n], bank[:, n0 % BANKS, :n], ACT.Relu).then_inc(s_evA, 1)
                act.wait_ge(s_evA, i * 8 + read_by(n0 + 1, "A"))
                A(m_hi[:, q % 4, c0:c0 + n], relu[:, q % 2, :n], ACT.Square).then_inc(s_hhi, 1)

            def mlp(l):
                j0 = job_at[("mlp", l)][0]
                norm_stats(2 * l, 1)
                norm_apply(2 * l, 1)
                for q in range(8):
                    if q % 2 == 0:
                        split([j0 + 4 + q // 2])
                    up(l, q)
                with act.Fori(0, CHUNKS - 1) as i:
                    split(range(j0 + 8, j0 + 12), i, 8, 24, mark[("loop", l)])
                    for q in range(8):
                        if q % 2 == 0:
                            split([j0 + 12 + q // 2], i, 8, 24, mark[("loop", l)] + 16)
                        up(l, q, 1, i)
                nxt = job_at[("qkv", 0)][0]
                tiles(2 * l + 1, {(0, 2 * k + 1): [nxt + k] for k in range(4)} if l == 0 else {})

            def o_jobs(l):
                j = job_at[("mlp", l)][0]
                return {(1, m): [j + m - 4] for m in range(4, 8)}

            tiles(0, o_jobs(0))
            mlp(0)
            def qkv(g, h):
                c0, n = HALF[h]
                for t in range(4 if g < 2 else 2):
                    i = 4 * g + t
                    src = unit(mark[("qkv", g, h)] + t)[:, :n]
                    if i < 2:
                        A((k_t if i == 0 else v_t)[:, c0:c0 + n], src, ACT.Identity, bias=V("b_qkv", i))\
                            .then_inc(s_evA, 1)
                    else:
                        bq = dv[:, 4, i - 2:i - 1]
                        if h == 1:
                            ordered(A(q_s[:, :, i - 2, :], src[:, 256:n].rearrange("p (b t) -> p b t", t=DEC_T),
                                      ACT.Identity, bias=bq, scale=HD ** -0.5))
                        A(q_tile(i - 2)[:, c0:c0 + 256], src[:, 0:256], ACT.Identity, bias=bq, scale=HD ** -0.5)\
                            .then_inc(s_evA, 1)
            qj = [job_at[("qkv", g)][0] for g in range(3)]
            norm_stats(1, 1)
            norm_apply(1, 1)
            qkv(0, 0)
            split([qj[1], qj[1] + 1])
            qkv(0, 1)
            split([qj[1] + 2, qj[1] + 3])
            qkv(1, 0)
            split([qj[2], qj[2] + 1])
            qkv(1, 1)
            act.wait_ge(s_tok, 1)
            A(v_tok[:, :, :], bank[:, score_bank(1), :].rearrange("p (n d) -> p n d", n=NB), ACT.Copy)\
                .then_inc(s_tokc, 1)
            act.wait_ge(s_tok, 2)
            A(k_tok[:, :], bank[:, score_bank(1) + 1, 0:128], ACT.Copy).then_inc(s_tokc, 1)
            A(kv_new[:, :, :], bank[0:NS, score_bank(1) + 1, 128:384].rearrange("p (n d) -> p n d", n=2), ACT.Copy)\
                .then_inc(s_tokc, 1)
            oj = job_at[("o", 1, 0)][0]

            def exponentials(T):
                w = step_width(T)
                act.wait_ge(s_max, T + 1)
                for e in range(4):
                    pr = probs[:, T % 3, e, 0:w]
                    ordered(A(pr, pr, ACT.Exp, bias=stat[:, T % 2, 1, e:e + 1], accum_out=stat[:, T % 2, 2, e:e + 1]))
                A(stat[:, T % 2, 4, :], stat[:, T % 2, 3, :], ACT.Exp).then_inc(s_exp, 1)

            exponentials(0)
            qkv(2, 0)
            qkv(2, 1)
            for it in range(17 + 1):
                if it + 1 < 17:
                    exponentials(it + 1)
                if it < 17:
                    act.wait_ge(s_pt, it + 1)
                    if it >= 2:
                        act.wait_ge(s_pv, it - 1)
                    A(probs_t[:, it % 2, 0, :], bank[:, trans_bank(0), :], ACT.Copy).then_inc(s_ptA, 1)
                if it >= 1:
                    act.wait_ge(s_pv, it)
                    dst, src = mixed(it - 1, x_hi)
                    A(dst, src, ACT.Copy).then_inc(s_ohi, 1)
                if it % 2 == 0 and it < 16:
                    split([oj + it // 2])
            tiles(2, o_jobs(1))
            mlp(1)
            norm_stats(3, 1)
            norm_apply(3, 1)

        @block.vector
        def _(dve):
            vt = nc.vector
            seq = [0]

            def ordered(ins):
                seq[0] += 1
                ins.then_inc(s_seqV, 1)
                dve.wait_ge(s_seqV, seq[0])

            def split(js, i=None, per=0):
                for j in js:
                    hi, lo, raw = split_targets(j)
                    dve.wait_ge(s_whi, j + 1 if i is None else i * per + (j + 1))
                    vt.tensor_tensor(lo, raw, hi.bitcast(F32), ALU.subtract).then_inc(s_wlo, 1)

            def unit(n):
                dve.wait_ge(s_unit, n + 1)
                return bank[:, n % BANKS, :]

            def x_split(h, ks=range(4)):
                c0, n = HALF[h]
                for k in ks:
                    dve.wait_ge(s_xhi, 4 * h + k + 1)
                    vt.tensor_tensor(x_lo[:, 2 * k:2 * k + 2, c0:c0 + n], acc[:, 2 * k:2 * k + 2, c0:c0 + n],
                                     x_hi[:, 2 * k:2 * k + 2, c0:c0 + n].bitcast(F32), ALU.subtract).then_inc(s_xlo, 1)

            vt.memset(ones[:, :], 1.0 / D).then_inc(s_const, 1)
            vt.memset(zeros[:, :], 0.0).then_inc(s_const, 1)
            vt.memset(tiny[:, 6, :], 0.0).then_inc(s_hsq, 2)
            vt.memset(tiny[:, 7, :], 0.0).then_inc(s_hlo, 2)
            dve.wait_ge(s_vec, 16)
            lam = V("lam", 0, KT)
            ordered(vt.tensor_scalar(tiny[:, 0, :], lam, -1.0, None, ALU.mult))
            vt.tensor_tensor(tiny[:, 1, :], tiny[:, 0, :], lam, ALU.max).then_inc(s_sp, 1)
            vt.tensor_scalar(dv[:, 0, :], V("b_ga", 0, KT), 0.5, None, ALU.mult)
            vt.tensor_scalar(dv[:, 1, :], V("b_gi", 0, KT), 0.5, None, ALU.mult)
            vt.tensor_scalar(dv[:, 4, :], V("b_qkv", 2, KT), HD ** -0.5, None, ALU.mult)
            for L in range(3):
                vt.tensor_scalar(dv[:, 5 + L, :], V("ln_g", L * KT, KT), ALPHA, None, ALU.mult)
                if L == 1:
                    vt.scalar_tensor_tensor(dv[:, 8 + L, :], V("ln_b", L * KT, KT), ALPHA, V("b_o", 0, KT),
                                            ALU.mult, ALU.add)
                else:
                    vt.tensor_scalar(dv[:, 8 + L, :], V("ln_b", L * KT, KT), ALPHA, None, ALU.mult)
            x_split(0, [0])
            split([0])
            x_split(0, [1, 2])
            split([1])
            x_split(0, [3])
            split([2, 3])
            dve.wait_ge(s_spe, 1)
            e, zz, z2, f = (tiny[:, k, :] for k in (2, 3, 4, 5))
            ordered(vt.tensor_scalar(zz, e, 2.0, None, ALU.add))
            ordered(vt.reciprocal(z2, zz))
            ordered(vt.tensor_tensor(zz, e, z2, ALU.mult))
            ordered(vt.tensor_tensor(z2, zz, zz, ALU.mult))
            ordered(vt.tensor_scalar(f, z2, 1.0 / 15.0, None, ALU.mult))
            for k in (13, 11, 9, 7, 5, 3):
                ordered(vt.scalar_tensor_tensor(f, f, 1.0 / k, z2, ALU.add, ALU.mult))
            ordered(vt.scalar_tensor_tensor(f, f, 1.0, zz, ALU.add, ALU.mult))
            ordered(vt.tensor_scalar(f, f, 2.0, None, ALU.mult))
            ordered(vt.tensor_scalar(tiny[:, 0, :], tiny[:, 0, :], 0.0, None, ALU.max))
            ordered(vt.tensor_tensor(f, f, tiny[:, 0, :], ALU.add))
            ordered(vt.tensor_scalar(dv[:, 3, :], f, 2.0, None, ALU.mult))
            vt.tensor_scalar(dv[:, 2, :], f, -4.0, None, ALU.mult).then_inc(s_dv, 1)

            def halo(s):
                p, h = s // 2, s % 2
                if s:
                    dve.wait_ge(s_conv, s)
                if h == 0:
                    vt.memset(u[:, :, 0:3], 0.0).then_inc(s_halo, 1)
                else:
                    at = VEC["conv_state"][0] + 2 * p * DEC_B * 3
                    state = vecs[:, at:at + 2 * DEC_B * 3].rearrange("p (t b k) -> p t b k", t=2, b=DEC_B)
                    for t in range(2):
                        seq[0] += 1
                        vt.tensor_copy(us[:, t, :, 0:3], state[:, t]).then_inc(s_seqV, 1)
                    vt.tensor_copy(u[:, :, 0:3], u[:, :, 256:259]).then_inc(s_halo, 1)

            def gated(s):
                _, n = HALF[s % 2]
                dve.wait_ge(s_evA, read_by(mark[("gate", s)] + 4, "A"))
                vt.scalar_tensor_tensor(th_g[:, :, :n], th_g[:, :, :n], 1.0, xc[s % 2][:, :, :n], ALU.add, ALU.mult)\
                    .then_inc(s_gated, 1)

            def recur(s):
                p, h = s // 2, s % 2
                c0, n = HALF[h]
                dve.wait_ge(s_root, s + 1)
                dve.wait_ge(s_gated, s + 1)
                ordered(vt.scalar_tensor_tensor(th_r[:, :, :n], decay[:, :, :n], 1.0, th_r[:, :, :n],
                                                ALU.add, ALU.mult))
                ordered(vt.scalar_tensor_tensor(th_g[:, :, :n], th_r[:, :, :n], 0.5, th_g[:, :, :n],
                                                ALU.mult, ALU.mult))
                if h == 1:
                    first = slice(256, n, DEC_T)
                    h0 = V("h0", 2 * p * DEC_B, 2 * DEC_B).rearrange("p (t b) -> p t b", t=2)
                    t3 = tiny[:, 6:8, :]
                    ordered(vt.tensor_tensor(t3, decay[:, :, first], h0, ALU.mult))
                    ordered(vt.tensor_tensor(th_g[:, :, first], th_g[:, :, first], t3, ALU.add))
                    ordered(vt.memset(decay[:, :, first], 0.0))
                for t in range(2):
                    m = 2 * p + t
                    init = 0.0 if h == 0 else out_small[:, m, 0:1]
                    ins = vt.tensor_tensor_scan(th_r[:, t, :n], decay[:, t, :n], th_g[:, t, :n], init,
                                                ALU.mult, ALU.add)
                    ins.then_inc(s_scan, 1)
                dve.wait_ge(s_scan, 2 * s + 2)
                for t in range(2):
                    m = 2 * p + t
                    seq[0] += 1
                    vt.tensor_copy(out_small[:, m, 0:1], th_r[:, t, 255:256]).then_inc(s_seqV, 1)
                    if h == 1:
                        seq[0] += 1
                        vt.tensor_copy(out_small[:, m, 1:9], th_r[:, t, 256 + DEC_T - 1:n:DEC_T]).then_inc(s_seqV, 1)
                dve.wait_ge(s_gy, s + 1)
                vt.scalar_tensor_tensor(z[:, s % 2, :, :n], th_r[:, :, :n], 0.5, z[:, s % 2, :, :n],
                                        ALU.mult, ALU.mult).then_inc(s_p, 1)

            def gelu_out(s):
                _, n = HALF[s % 2]
                dve.wait_ge(s_gth, s + 1)
                vt.scalar_tensor_tensor(z[:, s % 2, :, :n], sq[:, :, :n], 1.0, z[:, s % 2, :, :n], ALU.add, ALU.mult)\
                    .then_inc(s_gy, 1)

            halo(0)
            for s in range(8):
                p, h = s // 2, s % 2
                c0, n = HALF[h]
                if s == 0:
                    x_split(1)
                    split([4])
                split(next_jobs(s)[:1])
                if s:
                    gelu_out(s - 1)
                xcs = xc[s % 2]
                dve.wait_ge(s_conv0, s + 1)
                for k in range(1, CONV):
                    for t in range(2):
                        m = 2 * p + t
                        wk = V("conv_w", k * KT + m)
                        ins = vt.scalar_tensor_tensor(xcs[:, t, 0:256], u[:, t, k:k + 256], wk, xcs[:, t, 0:256],
                                                      ALU.mult, ALU.add)
                        if h == 1:
                            seq[0] += 1
                            ins.then_inc(s_seqV, 1)
                            xs = xcs[:, t, 256:n].rearrange("p (b t) -> p b t", t=DEC_T)
                            ins = vt.scalar_tensor_tensor(xs, us[:, t, :, k:k + DEC_T], wk, xs, ALU.mult, ALU.add)
                        if k == CONV - 1 and t == 1:
                            ins.then_inc(s_conv, 1)
                        else:
                            seq[0] += 1
                            ins.then_inc(s_seqV, 1)
                    if k < CONV - 1:
                        dve.wait_ge(s_seqV, seq[0])
                if h == 1:
                    for t in range(2):
                        m = 2 * p + t
                        rows = out_small[:, m, 9:36].rearrange("p (b k) -> p b k", k=3)
                        seq[0] += 2
                        vt.tensor_copy(rows[:, 0, :], u[:, t, 256:259]).then_inc(s_seqV, 1)
                        vt.tensor_copy(rows[:, 1:9, :], us[:, t, :, DEC_T:DEC_T + 3]).then_inc(s_seqV, 1)
                if s < 7:
                    halo(s + 1)
                if s:
                    gated(s - 1)
                    recur(s - 1)
                dve.wait_ge(s_gsq, s + 1)
                vt.scalar_tensor_tensor(sq[:, :, :n], sq[:, :, :n], GELU_IN, z[:, s % 2, :, :n], ALU.add, ALU.mult)\
                    .then_inc(s_gin, 1)
                split(next_jobs(s)[1:])
            split(range(job_at[("o", 0, 1)][0], job_at[("o", 0, 1)][0] + 4))
            gelu_out(7)
            gated(7)
            recur(7)

            def tile_done(L, h, m, src, n_read):
                c0, n = HALF[h]
                if n_read > 8:
                    dve.wait_ge(s_evV, n_read - 8)
                vt.tensor_tensor(acc[:, m, c0:c0 + n], src[:, :n], acc[:, m, c0:c0 + n], ALU.add)\
                    .then_inc(s_evV, 1)
                pos = tile_pos(L, h, m)
                dve.wait_ge(s_evV, n_read)
                if pos:
                    dve.wait_ge(s_s1, pos)
                s1 = sums[h][0]
                vt.tensor_tensor(s1[:, :n], acc[:, m, c0:c0 + n], zeros[:, :n] if m == 0 else s1[:, :n], ALU.add)\
                    .then_inc(s_s1, 1)

            def norm_stats(L, h):
                _, n = HALF[h]
                m0 = mark[("ln", L, h)]
                idx = 2 * L + h
                dve.wait_ge(s_evA, read_by(m0 + 1, "A"))
                ordered(vt.tensor_tensor(msq[:, :n], mean[:, :n], mean[:, :n], ALU.mult))
                vt.tensor_tensor(msq[:, :n], unit(m0 + 1)[:, :n], msq[:, :n], ALU.subtract).then_inc(s_evV, 1)
                dve.wait_ge(s_evV, read_by(m0 + 2, "V"))
                vt.tensor_scalar(msq[:, :n], msq[:, :n], 0.0, EPS, ALU.max, ALU.add).then_inc(s_var, 1)

            def norm_apply(L, h, between=()):
                c0, n = HALF[h]
                idx = 2 * L + h

                def pair(a, t):
                    return a[:, 2 * t:2 * t + 2, c0:c0 + n]

                def wide(a):
                    return a[:, 0:n].rearrange("p (o n) -> p o n", o=1).broadcast_to([128, 2, n])

                def low(k):
                    if L == 3:
                        return
                    dve.wait_ge(s_y, 8 * idx + k + 1)
                    vt.tensor_tensor(x_lo[:, k, c0:c0 + n], y_tmp[:, k % 2, :n],
                                     x_hi[:, k, c0:c0 + n].bitcast(F32), ALU.subtract).then_inc(s_ylo, 1)

                for t in range(2):
                    seq[0] += 1
                    vt.tensor_tensor(pair(acc, t), pair(acc, t), wide(mean), ALU.subtract).then_inc(s_seqV, 1)
                dve.wait_ge(s_std, idx + 1)
                ordered(vt.reciprocal(rstd[:, :n], rstd[:, :n]))
                for t in range(4):
                    if t >= 2:
                        dve.wait_ge(s_cent, 2 * idx + t - 1)
                    vt.tensor_tensor(pair(acc, t), pair(acc, t), wide(rstd), ALU.mult).then_inc(s_xhat, 1)
                    if t:
                        low(2 * t - 2)
                        low(2 * t - 1)
                    for work in between[2 * t:2 * t + 2]:
                        add_tile(*work)
                low(6)
                low(7)

            def add_tile(name, L, h, m):
                n0 = unit_of(name, L, h, m)
                tile_done(L, h, m, unit(n0), read_by(n0 + 1, "V"))

            def tiles(name, L, jobs_at):
                for m in range(KT):
                    split(jobs_at.get((0, m), ()))
                    add_tile(name, L, 0, m)
                add_tile(name, L, 1, 0)
                add_tile(name, L, 1, 1)
                norm_stats(L, 0)
                norm_apply(L, 0, [(name, L, 1, m) for m in range(2, 4)])
                for m in range(4, KT):
                    split(jobs_at.get((1, m), ()))
                    add_tile(name, L, 1, m)

            def up(l, q, c=0, i=0):
                c0, n = HALF[q // 4]
                n0 = mark[("up", l)] + 24 * c + q
                t0 = (CHUNKS * l + c) * 8 + q
                dve.wait_ge(s_evA, i * 8 + read_by(n0 + 1, "A"))
                dve.wait_ge(s_hlo, i * 8 + (t0 + 1))
                vt.tensor_tensor(h_sq[:, q % 2, :n], relu[:, q % 2, :n], relu[:, q % 2, :n], ALU.mult)\
                    .then_inc(s_hsq, 1)
                dve.wait_ge(s_hhi, i * 8 + (t0 + 1))
                dve.wait_ge(s_hsq, i * 8 + (t0 + 3))
                vt.tensor_tensor(m_lo[:, q % 4, c0:c0 + n], h_sq[:, q % 2, :n],
                                 m_hi[:, q % 4, c0:c0 + n].bitcast(F32), ALU.subtract).then_inc(s_hlo, 1)

            def mlp(l):
                j0 = job_at[("mlp", l)][0]
                norm_stats(2 * l, 1)
                norm_apply(2 * l, 1)
                for q in range(8):
                    if q % 2 == 0:
                        split([j0 + 4 + q // 2])
                    up(l, q)
                dve.wait_ge(s_res, 8 * (4 * l + 2))
                with dve.Fori(0, CHUNKS - 1) as i:
                    for q in range(16):
                        c0, n = HALF[q // 8]
                        n0 = mark[("loop", l)] + q
                        if q % 4 == 0:
                            split([j0 + 8 + q // 4], i, 8)
                        dve.wait_ge(s_unit, i * 24 + (n0 + 1))
                        dve.wait_ge(s_evV, i * 16 + (read_by(n0, "V") - 8))
                        vt.tensor_tensor(acc[:, q % 8, c0:c0 + n], bank[:, n0 % BANKS, :n],
                                         acc[:, q % 8, c0:c0 + n], ALU.add).then_inc(s_evV, 1)
                    for q in range(8):
                        if q % 2 == 0:
                            split([j0 + 12 + q // 2], i, 8)
                        up(l, q, 1, i)
                nxt = job_at[("qkv", 0)][0]
                tiles("down", 2 * l + 1, {(0, 2 * k + 1): [nxt + k] for k in range(4)} if l == 0 else {})

            def o_jobs(l):
                j = job_at[("mlp", l)][0]
                return {(1, m): [j + m - 4] for m in range(4, 8)}

            dve.wait_ge(s_res0, 2)
            tiles("o", 0, o_jobs(0))
            mlp(0)
            norm_stats(1, 1)
            norm_apply(1, 1)
            split(range(job_at[("qkv", 1)][0], job_at[("qkv", 1)][0] + 6))
            oj = job_at[("o", 1, 0)][0]

            def mask_max(T):
                w = step_width(T)
                st = stat[:, T % 2]
                dve.wait_ge(s_sc, T + 1)
                if T >= 3:
                    dve.wait_ge(s_pt, T - 2)
                pr = probs[:, T % 3, :, 0:w]
                src = bank[:, score_bank(T):score_bank(T) + 2, :].rearrange("p v (i c) -> p (v i) c", i=2)[:, :, 0:w]
                if T < 16:
                    mk = V("mask", 2 * WIN - w, w).rearrange("p (o c) -> p o c", o=1).broadcast_to([128, 4, w])
                    vt.tensor_tensor(pr, src, mk, ALU.add).then_inc(s_sm, 1)
                else:
                    mk = V("mask_rows", 0, 2 * w).rearrange("p (b c) -> p b c", b=2)
                    for v in range(2):
                        ins = vt.tensor_tensor(pr[:, 2 * v:2 * v + 2, :], src[:, 2 * v:2 * v + 2, :], mk, ALU.add)
                        if v == 0:
                            seq[0] += 1
                            ins.then_inc(s_seqV, 1)
                    ins.then_inc(s_sm, 1)
                sink = V("sinks", 4 * (T % 4), 4) if T < 16 else V("sink_rows", 0, 4)
                dve.wait_ge(s_sm, T + 1)
                ordered(vt.tensor_reduce(st[:, 0, :], pr, AX.X, ALU.max))
                ordered(vt.tensor_tensor(st[:, 0, :], st[:, 0, :], sink, ALU.max))
                seq[0] += 1
                vt.tensor_tensor(st[:, 3, :], sink, st[:, 0, :], ALU.subtract).then_inc(s_seqV, 1)
                vt.tensor_scalar(st[:, 1, :], st[:, 0, :], -1.0, None, ALU.mult).then_inc(s_max, 1)

            def denominators(T):
                st = stat[:, T % 2]
                dve.wait_ge(s_exp, T + 1)
                ordered(vt.tensor_tensor(st[:, 5, :], st[:, 2, :], st[:, 4, :], ALU.add))
                ordered(vt.reciprocal(st[:, 6, :], st[:, 5, :]))
                if T >= 2:
                    dve.wait_ge(s_pt, T - 1)
                for e in range(4):
                    ins = vt.tensor_scalar(scale_by[:, T % 2, e, :], V("ident", 0, 128), st[:, 6, e:e + 1], None,
                                           ALU.mult)
                    if e < 3:
                        seq[0] += 1
                        ins.then_inc(s_seqV, 1)
                ins.then_inc(s_diag, 1)

            mask_max(0)
            mask_max(1)
            denominators(0)
            for it in range(17 + 1):
                if it + 2 < 17:
                    mask_max(it + 2)
                if it + 1 < 17:
                    denominators(it + 1)
                if it < 17 and step_width(it) > WIN:
                    dve.wait_ge(s_pt, it + 1)
                    if it >= 2:
                        dve.wait_ge(s_pv, it - 1)
                    rows = NS if it == 16 else 128
                    vt.tensor_copy(probs_t[0:rows, it % 2, 1, :], bank[0:rows, trans_bank(1), :]).then_inc(s_ptV, 1)
                if it >= 1:
                    dve.wait_ge(s_ohi, it)
                    dst, src = mixed(it - 1, x_lo)
                    hi, _ = mixed(it - 1, x_hi)
                    vt.tensor_tensor(dst, src, hi.bitcast(F32), ALU.subtract).then_inc(s_olo, 1)
                if it % 2 == 0 and it < 16:
                    split([oj + it // 2])
            dve.wait_ge(s_res, 8 * 4)
            tiles("o", 2, o_jobs(1))
            mlp(1)
            norm_stats(3, 1)
            norm_apply(3, 1)

        @block.gpsimd
        def _(pool):
            pt = nc.gpsimd
            seq = [0]
            pool.wait_ge(s_vec, 16)
            def residual0(h):
                c0, n = HALF[h]
                for k in range(KT):
                    pool.wait_ge(s_xlo, 4 * h + k // 2 + 1)
                    ins = pt.tensor_scalar(acc[:, k, c0:c0 + n], acc[:, k, c0:c0 + n], ALPHA, V("b_out", k),
                                           ALU.mult, ALU.add)
                    if k < KT - 1:
                        ins.then_inc(s_seqP, 1)
                ins.then_inc(s_res0, 1)
            residual0(0)
            residual0(1)

            def low_product(s):
                p, (c0, n) = s // 2, HALF[s % 2]
                pool.wait_ge(s_phi, s + 1)
                pt.tensor_tensor(m_lo[:, 2 * p:2 * p + 2, c0:c0 + n], z[:, s % 2, :, :n],
                                 m_hi[:, 2 * p:2 * p + 2, c0:c0 + n].bitcast(F32), ALU.subtract).then_inc(s_plo, 1)

            for s in range(8):
                p, h = s // 2, s % 2
                c0, n = HALF[h]
                pool.wait_ge(s_evA, read_by(mark[("x", s)] + 2, "A"))
                if s >= 2:
                    pool.wait_ge(s_gated, s - 1)
                    pool.wait_ge(s_xclo, s - 1)
                xcs = xc[s % 2]
                for t in range(2):
                    m = 2 * p + t
                    ins = pt.tensor_scalar(xcs[:, t, 0:256], u[:, t, 0:256], V("conv_w", m), V("conv_b", m),
                                           ALU.mult, ALU.add)
                    if h == 1:
                        ins.then_inc(s_seqP, 1)
                        ins = pt.tensor_scalar(xcs[:, t, 256:n].rearrange("p (b t) -> p b t", t=DEC_T),
                                               us[:, t, :, 0:DEC_T], V("conv_w", m), V("conv_b", m),
                                               ALU.mult, ALU.add)
                    if t == 0:
                        ins.then_inc(s_seqP, 1)
                ins.then_inc(s_conv0, 1)
                if s >= 2:
                    low_product(s - 2)
                pool.wait_ge(s_xchi, s + 1)
                if s:
                    pool.wait_ge(s_unit, mark[("gate", s - 1)] + 4)
                pt.tensor_tensor(xc_lo[:, :, :n], xcs[:, :, :n], xc_hi[:, :, :n].bitcast(F32), ALU.subtract)\
                  .then_inc(s_xclo, 1)
            low_product(6)
            low_product(7)

            def add_square(L, h, m):
                _, n = HALF[h]
                pos = tile_pos(L, h, m)
                s2 = sums[h][1]
                pool.wait_ge(s_sqt, pos + 1)
                if pos:
                    pool.wait_ge(s_s2, pos)
                pt.tensor_tensor(s2[:, :n], sqt[:, pos % 2, :n], zeros[:, :n] if m == 0 else s2[:, :n], ALU.add)\
                  .then_inc(s_s2, 1)

            def norm_apply(L, h):
                c0, n = HALF[h]
                idx = 2 * L + h
                pool.wait_ge(s_evA, read_by(mark[("ln", L, h)] + 1, "A"))
                for t in (2, 3):
                    pair = acc[:, 2 * t:2 * t + 2, c0:c0 + n]
                    wide = mean[:, 0:n].rearrange("p (o n) -> p o n", o=1).broadcast_to([128, 2, n])
                    pt.tensor_tensor(pair, pair, wide, ALU.subtract).then_inc(s_cent, 1)
                for k in range(KT):
                    a = acc[:, k, c0:c0 + n]
                    if L == 3:
                        if k % 2:
                            pool.wait_ge(s_xhat, 4 * idx + k // 2 + 1)
                            pt.tensor_scalar(a, a, V("ln_g", L * KT + k), V("ln_b", L * KT + k), ALU.mult, ALU.add)\
                              .then_inc(s_yout[1], 1)
                        continue
                    pool.wait_ge(s_y, 8 * idx + k + 1)
                    pt.tensor_scalar(a, a, dv[:, 5 + L, k:k + 1], dv[:, 8 + L, k:k + 1], ALU.mult, ALU.add)\
                      .then_inc(s_res, 1)

            def tiles(L):
                for h in range(2):
                    for m in range(KT):
                        add_square(L, h, m)
                        if (h, m) == (1, 1):
                            norm_apply(L, 0)

            def mlp(l):
                norm_apply(2 * l, 1)
                tiles(2 * l + 1)
                if l == 0:
                    norm_apply(1, 1)

            tiles(0)
            pool.dma_start(kc_t[:, :, :], ck_t).then_inc(s_cache, 16)
            pool.dma_start(vc[:, :, :], cache_v.rearrange("b s c -> s b c")).then_inc(s_cache, 16)
            pool.dma_start(k_s[:, 0:WIN - DEC_T, :], cache_k[:, DEC_T:WIN, :]).then_inc(s_kept, 16)
            pool.dma_start(v_s[:, 0:WIN - DEC_T, :], cache_v[:, DEC_T:WIN, :]).then_inc(s_kept, 16)
            pool.dma_start(small, out_small[:, :, :]).then_inc(s_kept, 16)
            mlp(0)
            pool.wait_ge(s_tokc, 3)
            pool.dma_start(k_p, k_tok[:, :]).then_inc(s_kept, 16)
            pool.dma_start(v_p, v_tok[:, NB - 1, :]).then_inc(s_kept, 16)
            for n, dst in ((0, k_s), (1, v_s)):
                for b in range(DEC_B):
                    pool.dma_start(dst[b, WIN - DEC_T:WIN, :], kv_new[DEC_T * b:DEC_T * b + DEC_T, n, :])\
                        .then_inc(s_kept, 16)
            tiles(2)
            mlp(1)
            norm_apply(3, 1)

        @block.tensor
        def _(pe):
            mm = nc.tensor.matmul

            def free_bank(n):
                prev = n - BANKS
                if prev >= floor[0]:
                    who = reader[prev]
                    pe.wait_ge(s_evA if who == "A" else s_evV, read_by(prev + 1, who))

            floor = [0]

            def product(n, width, pieces):
                out = bank[:, n % BANKS, :width]
                last = len(pieces) - 1
                for k, (wh, wl, xh, xl) in enumerate(pieces):
                    mm(out, wh, xh, start=(k == 0), stop=False)
                    mm(out, wh, xl, start=False, stop=False)
                    ins = mm(out, wl, xh, start=False, stop=(k == last))
                ins.then_inc(s_unit, 1)

            def slab(w0, k, off):
                s = (w0 + k) % SLOTS
                return w_hi[:, s, off:off + 128], w_lo[:, s, off:off + 128]

            def act_cols(hi, lo, k, h):
                c0, n = HALF[h]
                return hi[:, k, c0:c0 + n], lo[:, k, c0:c0 + n]

            def pair_unit(n, w0, t, h):
                free_bank(n)
                product(n, HALF[h][1], [(*slab(w0, k // 4, 256 * (k % 4) + 128 * t), *act_cols(x_hi, x_lo, k, h))
                                        for k in range(KT)])

            def quad_pieces(w0, t, h, hi=x_hi, lo=x_lo):
                return [(*slab(w0, k // 2, 512 * (k % 2) + 128 * t), *act_cols(hi, lo, k, h)) for k in range(KT)]

            def down_pieces(w0, m, h):
                return [(*slab(w0, k, 128 * m), *act_cols(m_hi, m_lo, k, h)) for k in range(4)]

            def gates(s):
                p, h = s // 2, s % 2
                n = HALF[h][1]
                pe.wait_ge(s_wlo, job_at[("gates", p)][0] + 1)
                pe.wait_ge(s_xclo, s + 1)
                for t in range(2):
                    for g in range(2):
                        n0 = mark[("gate", s)] + 2 * t + g
                        free_bank(n0)
                        off = 256 * t + 128 * g
                        product(n0, n, [(gate_hi[:, p % 2, off:off + 128], gate_lo[:, p % 2, off:off + 128],
                                         xc_hi[:, t, :n], xc_lo[:, t, :n])])

            def norm_sums(L, h):
                _, n = HALF[h]
                n0 = mark[("ln", L, h)]
                pe.wait_ge(s_s1, tile_pos(L, h, 7) + 1)
                free_bank(n0)
                mm(bank[:, n0 % BANKS, :n], ones[:, :], sums[h][0][:, :n], start=True, stop=True).then_inc(s_unit, 1)
                pe.wait_ge(s_s2, tile_pos(L, h, 7) + 1)
                free_bank(n0 + 1)
                mm(bank[:, (n0 + 1) % BANKS, :n], ones[:, :], sums[h][1][:, :n], start=True, stop=True)\
                    .then_inc(s_unit, 1)

            def group_by_k(ns, h, pieces_of, ready, middle=None):
                width = HALF[h][1]
                for n in ns:
                    free_bank(n)
                for k in range(KT):
                    for on in ready(k):
                        pe.wait_ge(*on)
                    for t, n in enumerate(ns):
                        wh, wl, xh, xl = pieces_of(t)[k]
                        out = bank[:, n % BANKS, :width]
                        mm(out, wh, xh, start=(k == 0), stop=False)
                        mm(out, wh, xl, start=False, stop=False)
                        ins = mm(out, wl, xh, start=False, stop=(k == KT - 1))
                        if k == KT - 1:
                            ins.then_inc(s_unit, 1)
                    if k == KT // 2 - 1 and middle:
                        middle()

            pe.wait_ge(s_const, 2)
            for s in range(8):
                p, h = s // 2, s % 2
                j, w0 = job_at[("pair", p)]
                if s == 0:
                    def pieces0(t):
                        return [(*slab(w0, k // 4, 256 * (k % 4) + 128 * t), *act_cols(x_hi, x_lo, k, 0))
                                for k in range(KT)]

                    group_by_k(range(2), 0, pieces0,
                               lambda k: ((s_xlo, k // 2 + 1), (s_wlo, k // 4 + 1)))
                else:
                    if s == 1:
                        pe.wait_ge(s_xlo, 8)
                    pe.wait_ge(s_wlo, j + 2)
                    for t in range(2):
                        pair_unit(mark[("x", s)] + t, w0, t, h)
                if s:
                    gates(s - 1)
                pe.wait_ge(s_wlo, j + 4)
                for t in range(2):
                    pair_unit(mark[("y", s)] + t, w0 + 2, t, h)
            gates(7)

            def project(l, between={}):
                L = 2 * l
                src = (m_hi, m_lo) if l == 0 else (x_hi, x_lo)
                for h in range(2):
                    for m in range(KT):
                        j, w0 = job_at[("o", l, m // 4)]
                        if l == 0 and h == 0 and m < 4:
                            if m == 0:
                                pe.wait_ge(s_wlo, j + 4)
                                n0 = unit_of("o", L, 0, 0)
                                group_by_k(range(n0, n0 + 4), 0, lambda t: quad_pieces(w0, t, 0, *src),
                                           lambda k: ((s_plo, (1, 3, 5, 7)[k // 2]),))
                            continue
                        if h == 0 and m % 4 == 0:
                            pe.wait_ge(s_wlo, j + 4)
                        if (h, m) == (1, 2):
                            norm_sums(L, 0)
                        if l == 0 and m == 0 and h == 1:
                            pe.wait_ge(s_plo, 8)
                        if l == 1 and h == 0 and m in (0, 4, 6):
                            pe.wait_ge(*((s_sm, 17) if m == 0 else (s_ptA, 17) if m == 4 else (s_olo, 17)))
                            if m == 4:
                                pe.wait_ge(s_ptV, wide_steps(17))
                        n0 = unit_of("o", L, h, m)
                        free_bank(n0)
                        pieces = quad_pieces(w0, m % 4, h, *src)
                        product(n0, HALF[h][1], pieces)
                        if h == 0 and m in between:
                            between[m]()

            def mlp(l):
                j0, w0 = job_at[("mlp", l)]
                u0, loop0 = mark[("up", l)], mark[("loop", l)]
                v0, a0 = read_by(loop0, "V"), read_by(loop0, "A")
                t0 = 8 * CHUNKS * l
                idx = 4 * l
                pe.wait_ge(s_wlo, j0 + 4)
                for h in range(2):
                    group_by_k(range(u0 + 4 * h, u0 + 4 * h + 4), h, lambda t: quad_pieces(w0, t, h),
                               lambda k: ((s_ylo, 8 * (idx + h) + k + 1),),
                               (lambda: norm_sums(2 * l, 1)) if h == 0 else None)
                with pe.Fori(0, CHUNKS - 1) as i:
                    pe.wait_ge(s_wlo, i * 8 + (j0 + 8))
                    for q in range(16):
                        h, m = q // 8, q % 8
                        if m == 0:
                            pe.wait_ge(s_hlo, i * 8 + (t0 + 4 * h + 6))
                        if q < 8:
                            pe.wait_ge(s_evA, i * 8 + (a0 - 7 + q))
                        else:
                            pe.wait_ge(s_evV, i * 16 + (v0 + q - 7))
                        product(loop0 + q, HALF[h][1], down_pieces(w0 + 4, m, h))
                    pe.wait_ge(s_wlo, i * 8 + (j0 + 12))
                    for q in range(8):
                        pe.wait_ge(s_evV, i * 16 + (v0 + q + 9))
                        product(loop0 + 16 + q, HALF[q // 4][1], quad_pieces(w0, q % 4, q // 4))
                L = 2 * l + 1
                pe.wait_ge(s_wlo, j0 + 8 * CHUNKS)
                for h in range(2):
                    pe.wait_ge(s_hlo, t0 + 8 * (CHUNKS - 1) + 4 * h + 6)
                    for m in range(KT):
                        if (h, m) == (1, 2):
                            norm_sums(L, 0)
                        n0 = unit_of("down", L, h, m)
                        free_bank(n0)
                        product(n0, HALF[h][1], down_pieces(w0 + 4, m, h))

            def scores(T):
                b0 = score_bank(T)
                if T >= 2:
                    pe.wait_ge(s_sm, T - 1)
                if T < 16:
                    n = T // 4
                    lo = 0 if n == 0 else WIN * (n - 1)
                    w = step_width(T)
                    for v in range(2):
                        for e in range(2):
                            ins = mm(bank[:, b0 + v, 256 * e:256 * e + w],
                                     q_tile(2 * (T % 4) + e)[HD * v:HD * v + HD, WIN * n:WIN * n + WIN],
                                     k_t[HD * v:HD * v + HD, lo:lo + w], start=True, stop=True)
                else:
                    for v in range(2):
                        for bq in range(2):
                            for j in range(4):
                                b = 4 * bq + j
                                out = bank[32 * j:32 * j + 32, b0 + v, 256 * bq:256 * bq + WIN + NS]
                                qs = q_s[HD * v:HD * v + HD, b, :, :]
                                mm(out[:, 0:WIN], qs, kc_t[HD * v:HD * v + HD, b, :], start=True, stop=True)
                                ins = mm(out[:, WIN:WIN + NS], qs, k_t[HD * v:HD * v + HD, SEQ:TOK],
                                         start=True, stop=True)
                ins.then_inc(s_sc, 1)

            def transposes(T):
                w = step_width(T)
                pe.wait_ge(s_diag, T + 1)
                if T:
                    pe.wait_ge(s_ptA, T)
                    if wide_steps(T):
                        pe.wait_ge(s_ptV, wide_steps(T))
                for kb in range(2 if w > WIN else 1):
                    wk = min(WIN, w - WIN * kb)
                    for e in range(4):
                        ins = mm(bank[0:wk, trans_bank(kb), 128 * e:128 * e + 128],
                                 probs[:, T % 3, e, WIN * kb:WIN * kb + wk], scale_by[:, T % 2, e, :],
                                 start=True, stop=True)
                ins.then_inc(s_pt, 1)

            def values(T):
                pe.wait_ge(s_ptA, T + 1)
                if wide_steps(T + 1):
                    pe.wait_ge(s_ptV, wide_steps(T + 1))
                if T >= 2:
                    pe.wait_ge(s_olo, T - 1)
                for v in range(2):
                    out = bank[HD * v:HD * v + HD, pv_bank(T), 0:256]
                    if T < 16:
                        n = T // 4
                        blocks = [n] if n == 0 else [n - 1, n]
                        for kb, blk in enumerate(blocks):
                            ins = mm(out, v_tok[:, blk, HD * v:HD * v + HD],
                                     probs_t[:, T % 2, kb, 256 * v:256 * v + 256],
                                     start=(kb == 0), stop=(kb == len(blocks) - 1))
                    else:
                        for b in range(DEC_B):
                            at = 128 * (2 * v + b // 4) + 32 * (b % 4)
                            mm(out[:, 32 * b:32 * b + 32], vc[:, b, HD * v:HD * v + HD],
                               probs_t[:, T % 2, 0, at:at + 32], start=True, stop=False)
                            ins = mm(out[:, 32 * b:32 * b + 32], kv_new[:, 1, HD * v:HD * v + HD],
                                     probs_t[0:NS, T % 2, 1, at:at + 32], start=False, stop=True)
                ins.then_inc(s_pv, 1)

            project(0)
            mlp(0)
            def qkv(g, h, only=None):
                j, w0 = job_at[("qkv", g)]
                nu = 4 if g < 2 else 2
                if h == 0 and not only:
                    pe.wait_ge(s_wlo, j + nu)
                n0 = mark[("qkv", g, h)]
                if g == 0:
                    group_by_k(range(n0, n0 + 4), h, lambda t: quad_pieces(w0, t, h),
                               lambda k: ((s_ylo, 8 * (2 + h) + k + 1),),
                               (lambda: norm_sums(1, 1)) if h == 0 else None)
                    return
                if g == 2:
                    pair_unit(n0 + only, w0, only, h)
                    return
                for t in range(nu):
                    free_bank(n0 + t)
                    product(n0 + t, HALF[h][1], quad_pieces(w0, t, h))

            for g in range(2):
                for h in range(2):
                    qkv(g, h)
            ident = V("ident", 0, 128)
            tb = score_bank(1)
            qkv(2, 0, 0)
            pe.wait_ge(s_evA, read_by(mark[("qkv", 2, 0)], "A"))
            pe.wait_ge(s_evV, read_by(mark[("qkv", 2, 0)], "V"))
            scores(0)
            for n in range(NB):
                ins = nc.tensor.transpose(bank[:, tb, 128 * n:128 * n + 128], v_t[:, 128 * n:128 * n + 128], ident)
            ins.then_inc(s_tok, 1)
            nc.tensor.transpose(bank[:, tb + 1, 0:128], k_t[:, SEQ - 128:SEQ], ident)
            nc.tensor.transpose(bank[0:NS, tb + 1, 128:256], k_t[:, SEQ:TOK], ident)
            nc.tensor.transpose(bank[0:NS, tb + 1, 256:384], v_t[:, SEQ:TOK], ident).then_inc(s_tok, 1)
            qkv(2, 0, 1)
            pe.wait_ge(s_tokc, 3)
            scores(1)
            qkv(2, 1, 0)
            qkv(2, 1, 1)
            scores(2)
            pe.wait_ge(s_evA, read_by(mark["attention"], "A"))
            for T in range(16):
                transposes(T)
                if T == 13:
                    pe.wait_ge(s_cache, 32)
                if T + 3 < 17:
                    scores(T + 3)
                if T:
                    values(T - 1)
            floor[0] = mark["attention"]
            transposes(16)
            values(15)
            project(1, {1: lambda: values(16)})
            mlp(1)
            norm_sums(3, 1)


def kernel(x_prompt, x_sample, state_lru_h, state_lru_conv, cache_swa_k, cache_swa_v,
           lru_w_x, lru_b_x, lru_w_y, lru_b_y, lru_conv_w, lru_conv_b,
           lru_w_ga, lru_b_ga, lru_w_gi, lru_b_gi, lru_lam, lru_w_out, lru_b_out,
           swa_w_qkv, swa_b_qkv, swa_sinks, swa_w_o, swa_b_o,
           mlp_w_up, mlp_w_down, ln1_g, ln1_b, ln2_g, ln2_b):
    import concourse.bacc as bacc
    from concourse.bass_utils import run_bass_kernel_spmd

    (x_prompt, x_sample, state_lru_h, state_lru_conv, cache_swa_k, cache_swa_v, lru_w_x, lru_b_x, lru_w_y, lru_b_y,
     lru_conv_w, lru_conv_b, lru_w_ga, lru_b_ga, lru_w_gi, lru_b_gi, lru_lam, lru_w_out, lru_b_out, swa_w_qkv,
     swa_b_qkv, swa_sinks, swa_w_o, swa_b_o, mlp_w_up, mlp_w_down, ln1_g, ln1_b, ln2_g, ln2_b) = map(np.asarray, (
         x_prompt, x_sample, state_lru_h, state_lru_conv, cache_swa_k, cache_swa_v, lru_w_x, lru_b_x, lru_w_y,
         lru_b_y, lru_conv_w, lru_conv_b, lru_w_ga, lru_b_ga, lru_w_gi, lru_b_gi, lru_lam, lru_w_out, lru_b_out,
         swa_w_qkv, swa_b_qkv, swa_sinks, swa_w_o, swa_b_o, mlp_w_up, mlp_w_down, ln1_g, ln1_b, ln2_g, ln2_b))

    nq = NKV * GRP * HD
    q_cols = np.arange(nq).reshape(NKV, GRP, HD).transpose(1, 0, 2).reshape(-1)
    cols = np.concatenate([np.arange(nq, nq + 2 * NKV * HD), q_cols])

    def tiles(a):
        a = a.reshape(-1, a.shape[-1] // 128, 128)
        return a.transpose(2, 0, 1).reshape(128, -1)

    def tiles_first(a):
        return a.reshape(-1, KT, 128).transpose(2, 1, 0).reshape(128, -1)

    row, col = np.arange(WIN)[:, None], np.arange(2 * WIN)[None, :]
    mask = np.where((col > row) & (col <= row + WIN), 0.0, NEG).astype(np.float32)
    j, t = np.arange(128) // 32, np.arange(128) % DEC_T
    rows = np.full((128, 2, WIN + NS), NEG, np.float32)
    for bq in range(2):
        rows[:, bq, :WIN][np.arange(WIN)[None, :] > t[:, None]] = 0.0
        c = np.arange(NS)[None, :]
        rows[:, bq, WIN:][(c // DEC_T == 4 * bq + j[:, None]) & (c % DEC_T <= t[:, None])] = 0.0
    sinks = swa_sinks.reshape(NKV, GRP)
    head_of_row = (np.arange(128) % 32) // DEC_T
    parts = {
        "b_y": tiles(lru_b_y), "b_x": tiles(lru_b_x), "conv_w": tiles(lru_conv_w[0]), "conv_b": tiles(lru_conv_b),
        "b_ga": tiles(lru_b_ga.reshape(1, D)), "b_gi": tiles(lru_b_gi.reshape(1, D)), "lam": tiles(lru_lam),
        "b_out": tiles(lru_b_out), "b_o": tiles(swa_b_o),
        "ln_g": tiles(np.stack([ln1_g[0], ln2_g[0], ln1_g[1], ln2_g[1]])),
        "ln_b": tiles(np.stack([ln1_b[0], ln2_b[0], ln1_b[1], ln2_b[1]])),
        "b_qkv": tiles(swa_b_qkv[:, cols]), "h0": tiles_first(state_lru_h[0]),
        "conv_state": tiles_first(state_lru_conv[0].reshape(-1, D)),
        "sinks": np.broadcast_to(sinks.reshape(NKV, GRP // 2, 2).transpose(1, 0, 2).reshape(1, 16), (128, 16)),
        "sink_rows": np.stack([sinks[v][head_of_row] for v in (0, 0, 1, 1)], axis=1),
        "mask": mask, "mask_rows": rows.reshape(128, -1), "ident": np.eye(128, dtype=np.float32),
    }
    vec = np.ascontiguousarray(np.concatenate([parts[n] for n in VEC], axis=1))
    kv = NKV * HD
    arrays = {
        "xp_t": x_prompt[0].T, "xs_t": x_sample.reshape(NS, D).T, "vec": vec,
        "w_y": lru_w_y[0], "w_x": lru_w_x[0], "w_ga": lru_w_ga[0], "w_gi": lru_w_gi[0], "w_out": lru_w_out[0],
        "w_qkv": swa_w_qkv[0][:, cols], "w_o": swa_w_o[0][q_cols], "w_up": mlp_w_up, "w_down": mlp_w_down,
        "ck_t": cache_swa_k[0].reshape(DEC_B, WIN, kv).transpose(2, 0, 1),
        "cache_k": cache_swa_k[0].reshape(DEC_B, WIN, kv), "cache_v": cache_swa_v[0].reshape(DEC_B, WIN, kv),
    }
    arrays = {k: np.ascontiguousarray(v) for k, v in arrays.items()}
    outs = {"y_t": (D, TOK), "small": (128, KT, 36), "k_p": (WIN, kv), "v_p": (WIN, kv),
            "k_s": (DEC_B, WIN, kv), "v_s": (DEC_B, WIN, kv)}

    nc = bacc.Bacc("TRN2", target_bir_lowering=False, num_devices=1)
    args = [nc.dram_tensor(k, v.shape, mybir.dt.from_np(v.dtype), kind="ExternalInput").ap()
            for k, v in arrays.items()]
    args += [nc.dram_tensor(k, s, F32, kind="ExternalOutput").ap() for k, s in outs.items()]
    build(nc, *args)
    got = run_bass_kernel_spmd(nc, [arrays], core_ids=[0]).results[0]

    y = got["y_t"].T
    small = got["small"].transpose(1, 0, 2).reshape(D, 36)
    h, conv = small[:, 0:9].T, small[:, 9:36].reshape(D, 9, CONV - 1).transpose(1, 2, 0)
    heads = (NKV, HD)
    return (y[:SEQ].reshape(1, SEQ, D), y[SEQ:].reshape(DEC_B, DEC_T, D),
            h[0:1].reshape(1, 1, D), conv[0:1][None],
            got["k_p"].reshape(1, 1, WIN, *heads), got["v_p"].reshape(1, 1, WIN, *heads),
            h[1:9].reshape(1, DEC_B, D), conv[1:9][None],
            got["k_s"].reshape(1, DEC_B, WIN, *heads), got["v_s"].reshape(1, DEC_B, WIN, *heads))
```

```python
import numpy as np
import concourse.bass as bass
from concourse import mybir
from contextlib import ExitStack

F32 = mybir.dt.float32
F32R = mybir.dt.float32r
ALU = mybir.AluOpType
ACT = mybir.ActivationFunctionType
AX = mybir.AxisListType

D = 1024
SEQ, DEC_B, DEC_T = 512, 8, 4
NS = DEC_B * DEC_T
TOK = SEQ + NS
KT = D // 128
DFF = 4 * D
CHUNKS = DFF // 512
WIN = 128
NB = SEQ // WIN
NKV, GRP, HD = 2, 8, 64
CONV = 4
ALPHA = float(4.0 ** 0.25)
EPS = 1e-5
GELU_IN = 1.0 / 0.044715
GELU_OUT = 0.044715 * float(np.sqrt(2.0 / np.pi))
NEG = -1.0e30

HALF = [(0, 256), (256, TOK - 256)]
HW = TOK - 256

VEC = {}
_at = 0
for _name, _cols in [("b_y", KT), ("b_x", KT), ("conv_w", CONV * KT), ("conv_b", KT), ("b_ga", KT), ("b_gi", KT),
                     ("lam", KT), ("b_out", KT), ("b_o", KT), ("ln_g", 4 * KT), ("ln_b", 4 * KT), ("b_qkv", KT + 2),
                     ("h0", KT * DEC_B), ("conv_state", KT * DEC_B * (CONV - 1)), ("sinks", 16), ("sink_rows", 4),
                     ("mask", 2 * WIN), ("mask_rows", 2 * (WIN + NS)), ("ident", 128)]:
    VEC[_name] = (_at, _cols)
    _at += _cols
NVEC = _at



def step_width(T):
    return WIN + NS if T == 16 else (WIN if T < 4 else 2 * WIN)


def tile_pos(L, h, m):
    return 16 * L + 8 * h + m


BESIDE = [(2,), (3, 4), (5, 6), (7,)]
STAGES = 4
SLOTS = 8
BANKS = 8


def build(nc, xp_t, xs_t, vec, w_y, w_x, w_ga, w_gi, w_out, w_qkv, w_o, w_up, w_down,
          ck_t, cache_k, cache_v, y_t, small, k_p, v_p, k_s, v_s):
    ctx = ExitStack()
    with ctx:
        top = [nc.sbuf_base]

        def place(name, shape, dt, at=None):
            size = int(np.prod(shape[1:])) * 4
            if at is None:
                at = (top[0] + 31) // 32 * 32
                top[0] = at + size
            t = nc.alloc_sbuf_tensor_at(name, shape, dt, offset=at)
            t_at[name] = at
            return t

        t_at = {}
        w_hi = place("w_hi", [128, SLOTS, 1024], F32R)
        w_lo = place("w_lo", [128, SLOTS, 1024], F32R)
        stage = place("stage", [128, STAGES, 1024], F32)
        x_hi = place("x_hi", [128, KT, TOK], F32R)
        x_lo = place("x_lo", [128, KT, TOK], F32R)
        m_hi = place("m_hi", [128, KT, TOK], F32R)
        m_lo = place("m_lo", [128, KT, TOK], F32R)
        acc = place("acc", [128, KT, TOK], F32)
        vecs = place("vecs", [128, NVEC], F32)
        gate_hi = place("gate_hi", [128, 2, 512], F32R)
        gate_lo = place("gate_lo", [128, 2, 512], F32R)
        xc_hi = place("xc_hi", [128, 2, HW], F32R)
        xc_lo = place("xc_lo", [128, 2, HW], F32R)
        ones = place("ones", [128, 128], F32)
        zeros = place("zeros", [128, HW], F32)
        dv = place("dv", [128, 12, KT], F32)
        tiny = place("tiny", [128, 8, KT], F32)
        out_small = place("out_small", [128, KT, 9 * 4], F32)
        scratch = (top[0] + 31) // 32 * 32
        z = place("z", [128, 2, 2, HW], F32)
        sq = place("sq", [128, 2, HW], F32)
        xc_at = place("xc_even", [128, 2, HW], F32)
        th_r = place("th_r", [128, 2, HW], F32)
        th_g = place("th_g", [128, 2, HW], F32)
        decay = place("decay", [128, 2, HW], F32)
        u = place("u", [128, 2, 3 + 256], F32)
        us = place("us", [128, 2, DEC_B, 3 + DEC_T], F32)
        sums = [[place("sum_a", [128, HW], F32, t_at["z"]), place("sumsq_a", [128, HW], F32, t_at["z"] + 4 * HW)],
                [place("sum_b", [128, HW], F32), place("sumsq_b", [128, HW], F32)]]
        sqt = place("sqt", [128, 2, HW], F32, t_at["sq"])
        xc = [xc_at, place("xc_odd", [128, 2, HW], F32, t_at["sum_b"])]
        mean = place("mean", [128, HW], F32, t_at["th_r"])
        rstd = place("rstd", [128, HW], F32, t_at["th_r"] + 4 * HW)
        msq = place("msq", [128, HW], F32, t_at["decay"])
        y_tmp = place("y_tmp", [128, 2, HW], F32, t_at["th_g"])
        relu = place("relu", [128, 2, HW], F32, t_at["xc_even"])
        h_sq = place("h_sq", [128, 2, HW], F32, t_at["z"] + 8 * HW)
        assert top[0] <= nc.sbuf_usable_end, (top[0], nc.sbuf_usable_end)
        m_half = 4 * TOK * 4
        kc_t = place("kc_t", [128, DEC_B, WIN], F32, t_at["m_hi"] + m_half)
        vc = place("vc", [128, DEC_B, WIN], F32, t_at["m_hi"] + m_half + 4096)
        v_t = place("v_t", [128, TOK], F32, t_at["m_lo"] + m_half)
        k_t = place("k_t", [128, TOK], F32, t_at["m_lo"] + m_half + 4 * TOK)
        v_tok = place("v_tok", [128, NB, 128], F32, t_at["m_lo"] + m_half + 8 * TOK)
        k_tok = place("k_tok", [128, 128], F32, t_at["m_lo"] + m_half + 8 * TOK + 2048)
        kv_new = place("kv_new", [NS, 2, 128], F32, t_at["m_lo"] + m_half + 8 * TOK + 2560)
        q_a = place("q_a", [128, 4, SEQ], F32, t_at["m_hi"])
        q_b = place("q_b", [128, 4, SEQ], F32, t_at["m_lo"])
        probs = place("probs", [128, 4, 4, 256], F32, scratch)
        probs_t = place("probs_t", [128, 2, 2, 512], F32, t_at["gate_hi"])
        stat = place("stat", [128, 4, 8, 4], F32, t_at["xc_lo"])
        q_s = place("q_s", [128, DEC_B, KT, DEC_T], F32, t_at["xc_hi"])
        assert scratch + 16384 <= top[0]

        def q_tile(i):
            return (q_a if i < 4 else q_b)[:, i % 4, :]

        bank = ctx.enter_context(nc.psum_tensor("bank", [128, BANKS, 512], F32))

        def sem(name):
            return ctx.enter_context(nc.semaphore(name))

        s_vec = sem("vec_loaded")
        s_xa = [sem(f"x_half_a_loaded_{k}") for k in range(4)]
        s_xb = sem("x_half_b_loaded")
        s_arrived = [sem(f"slab_arrived_{i}") for i in range(STAGES)]
        s_whi, s_wlo = sem("slab_hi_done"), sem("slab_lo_done")
        s_unit = sem("unit_done")
        s_evA, s_evV = sem("read_by_scalar"), sem("read_by_vector")
        s_xhi, s_xlo, s_res0 = sem("x_hi_done"), sem("x_lo_done"), sem("residual_ready")
        s_const = sem("constants_ready")
        s_sp, s_spe = sem("softplus_in"), sem("softplus_exp")
        s_dv = sem("derived_ready")
        s_gsq, s_gin, s_gth, s_gy = sem("gelu_sq"), sem("gelu_in"), sem("gelu_tanh"), sem("gelu_y")
        s_halo, s_conv0, s_conv = sem("halo_ready"), sem("conv_first"), sem("conv_done")
        s_xchi, s_xclo = sem("xc_hi_done"), sem("xc_lo_done")
        s_root, s_gated = sem("root_ready"), sem("gated_ready")
        s_scan, s_p = sem("scan_done"), sem("product_ready")
        s_phi, s_plo = sem("product_hi_done"), sem("product_lo_done")
        s_sqt, s_s1, s_s2 = sem("square_ready"), sem("sum_added"), sem("square_added")
        s_var, s_std = sem("variance_ready"), sem("deviation_ready")
        s_xhat, s_y, s_ylo, s_res = sem("normed"), sem("y_ready"), sem("y_lo_done"), sem("residual_done")
        s_yout = [sem("y_out_even"), sem("y_out_odd")]
        s_hhi, s_hsq, s_hlo = sem("hidden_hi"), sem("hidden_sq"), sem("hidden_lo")
        s_cache = sem("cache_loaded")
        s_tok = sem("token_major_transposed")
        s_tokc = sem("token_major_copied")
        s_sc, s_sm, s_max = sem("scores_done"), sem("scores_masked"), sem("max_ready")
        s_cent = sem("centred")
        s_exp, s_den, s_nrm = sem("exp_done"), sem("denominators_ready"), sem("probs_normed")
        s_pt, s_pt_read = sem("probs_transposed"), sem("probs_t_copied")
        s_pv, s_ohi, s_olo = sem("values_done"), sem("mixed_hi"), sem("mixed_lo")
        s_out, s_kept, s_kv_kept = sem("trunk_written"), sem("states_written"), sem("new_keys_values_written")
        s_seqA, s_seqV, s_seqP = sem("scalar_order"), sem("vector_order"), sem("pool_order")

        block = ctx.enter_context(nc.Block())

        def V(name, a=0, n=1):
            at = VEC[name][0]
            return vecs[:, at + a:at + a + n]

        reader = []
        mark = {}

        def plan(name, who):
            mark[name] = len(reader)
            reader.extend(who)

        for s in range(8):
            plan(("x", s), "AA")
            if s:
                plan(("gate", s - 1), "AAAA")
            plan(("y", s), "AA")
        plan(("gate", 7), "AAAA")

        def plan_tiles(name, L):
            plan((name, L, 0, 0), "V" * 2)
            plan((name, L, 0, 2), "V" * 6)
            plan((name, L, 1, 0), "V" * 2)
            plan(("ln", L, 0), "AV")
            plan((name, L, 1, 2), "V" * 6)

        def plan_mlp(l):
            plan(("ln", 2 * l, 1), "AV")
            plan(("up", l), "A" * 8)
            plan(("loop", l), ("V" * 16 + "A" * 8) * (CHUNKS - 1))
            plan_tiles("down", 2 * l + 1)

        def unit_of(name, L, h, m):
            return mark[(name, L, h, 0 if m < 2 else 2)] + (m if m < 2 else m - 2)

        plan_tiles("o", 0)
        plan_mlp(0)
        plan(("ln", 1, 1), "AV")
        for g in range(3):
            for h in (0, 1):
                plan(("qkv", g, h), "AAAA" if g < 2 else "AA")
        mark["attention"] = len(reader)
        plan_tiles("o", 2)
        plan_mlp(1)
        plan(("ln", 3, 1), "AV")

        def read_by(n, who):
            return sum(1 for r in reader[:n] if r == who)

        yv, xv, ov, qv, pv = (w.rearrange("(k p) c -> p k c", p=128) for w in (w_y, w_x, w_out, w_qkv, w_o))
        uv = [w_up[l].rearrange("(k p) c -> p k c", p=128) for l in range(2)]
        dwv = [w_down[l].rearrange("(k p) c -> p k c", p=128) for l in range(2)]

        def quad(view, g, j):
            return view[:, 2 * j:2 * j + 2, 512 * g:512 * g + 512]

        job_at = {}
        jobs = []
        ring = [0]

        def plan_jobs(name, kinds):
            job_at[name] = (len(jobs), ring[0])
            for k in kinds:
                jobs.append((k, ring[0]))
                ring[0] += k == "w"

        for p in range(4):
            plan_jobs(("pair", p), "wwww")
            plan_jobs(("gates", p), "g")
        for g in range(2):
            plan_jobs(("o", 0, g), "wwww")
        plan_jobs(("mlp", 0), "w" * 8 * CHUNKS)
        for g, k in enumerate(["wwww", "wwww", "ww"]):
            plan_jobs(("qkv", g), k)
        for g in range(2):
            plan_jobs(("o", 1, g), "wwww")
        plan_jobs(("mlp", 1), "w" * 8 * CHUNKS)

        free_at = {}

        def frees(name, end, n=4):
            w = job_at[name][1]
            for k in range(n):
                free_at[w + k] = end

        for p in range(4):
            frees(("pair", p), mark[("y", 2 * p + 1)] + 2)
        for l in range(2):
            frees(("o", l, 0), unit_of("o", 2 * l, 1, 3) + 1)
            frees(("o", l, 1), unit_of("o", 2 * l, 1, 7) + 1)
            w0 = job_at[("mlp", l)][1]
            for c in range(CHUNKS):
                for k in range(4):
                    free_at[w0 + 8 * c + k] = mark[("up", l)] + 24 * c + 8
                    free_at[w0 + 8 * c + 4 + k] = mark[("loop", l)] + 24 * c + 16 + (2 if c == CHUNKS - 1 else 0)
        for g, n in enumerate((4, 4, 2)):
            frees(("qkv", g), mark[("qkv", g, 1)] + n, n)

        def next_jobs(s):
            p, h = s // 2, s % 2
            j = (job_at[("pair", p + 1)] if p < 3 else job_at[("o", 0, 0)])[0]
            return range(j, j + 2) if h == 0 else range(j + 2, j + (5 if p < 3 else 4))

        def next_slabs(name):
            return range(job_at[name][0], job_at[name][0] + 4)

        def score_bank(T):
            return (mark["attention"] + 2 * (T % 2)) % BANKS

        def trans_bank(kb):
            return (mark["attention"] + 4 + kb) % BANKS

        def pv_bank(T):
            return (mark["attention"] + 6 + T % 2) % BANKS

        def mixed(T, dst):
            src = bank[:, pv_bank(T), 0:256]
            if T < 16:
                n, i = T // 4, 2 * (T % 4)
                return (dst[:, i:i + 2, WIN * n:WIN * n + WIN],
                        src.rearrange("p (i q) -> p i q", i=2))
            return (dst[:, :, SEQ:TOK].rearrange("p i (b t) -> p b i t", t=DEC_T),
                    src.rearrange("p (b i t) -> p b i t", b=DEC_B, i=KT))

        @block.sync
        def _(sp):
            def load(j, src, i=None, per=0):
                if i is None:
                    if j >= STAGES:
                        sp.wait_ge(s_wlo, j - STAGES + 1)
                else:
                    sp.wait_ge(s_wlo, i * per + (j - STAGES + 1))
                n = int(np.prod(src.shape[1:]))
                dst = stage[:, j % STAGES, 0:n]
                if len(src.shape) == 3:
                    dst = dst.rearrange("p (k c) -> p k c", k=src.shape[1])
                sp.dma_start(dst, src).then_inc(s_arrived[j % STAGES], 16)

            def load_pair(name, view, c, jj=0):
                for k in range(2):
                    load(job_at[name][0] + jj + k, view[:, 4 * k:4 * k + 4, c:c + 256])

            def load_quad(name, view, g):
                for k in range(4):
                    load(job_at[name][0] + k, quad(view, g, k))

            def load_mlp(l):
                j0 = job_at[("mlp", l)][0]
                for k in range(4):
                    load(j0 + k, quad(uv[l], 0, k))
                with sp.Fori(0, CHUNKS - 1) as i:
                    for k in range(4):
                        load(j0 + 4 + k, dwv[l][:, bass.ds(i * 4 + k, 1), :], i, 8)
                    for k in range(4):
                        load(j0 + 8 + k, uv[l][:, 2 * k:2 * k + 2, bass.ds(i * 512 + 512, 512)], i, 8)
                for k in range(4):
                    load(j0 + 8 * (CHUNKS - 1) + 4 + k, dwv[l][:, 4 * (CHUNKS - 1) + k, :])

            def load_x(k):
                sp.dma_start(acc[:, 2 * k:2 * k + 2, 0:256],
                             xp_t[256 * k:256 * k + 256, 0:256].rearrange("(k p) t -> p k t", p=128))\
                    .then_inc(s_xa[k], 16)

            load_x(0)
            load(0, xv[:, 0:4, 0:256])
            for k in (1, 2):
                load_x(k)
            load(1, xv[:, 4:8, 0:256])
            load_x(3)
            load_pair(("pair", 0), yv, 0, 2)
            for p in range(4):
                if p == 0:
                    sp.dma_start(acc[:, :, 256:512],
                                 xp_t[:, 256:512].rearrange("(k p) t -> p k t", p=128)).then_inc(s_xb, 16)
                    sp.dma_start(acc[:, :, 512:TOK], xs_t.rearrange("(k p) t -> p k t", p=128)).then_inc(s_xb, 16)
                else:
                    load_pair(("pair", p), xv, 256 * p)
                    load_pair(("pair", p), yv, 256 * p, 2)
                j = job_at[("gates", p)][0]
                sp.wait_ge(s_wlo, j - STAGES + 1)
                dst = stage[:, j % STAGES, 0:512].rearrange("p (b g c) -> p b g c", b=2, g=2)
                for n, w in enumerate((w_ga, w_gi)):
                    sp.dma_start(dst[:, :, n, :], w[2 * p:2 * p + 2].rearrange("b i j -> i b j"))\
                      .then_inc(s_arrived[j % STAGES], 16)
            for g in range(2):
                load_quad(("o", 0, g), ov, g)
            load_mlp(0)
            for g in range(2):
                load_quad(("qkv", g), qv, g)
            load_pair(("qkv", 2), qv, 1024)
            load_quad(("o", 1, 0), pv, 0)
            sp.wait_ge(s_tokc, 3)
            sp.dma_start(k_p, k_tok[:, :]).then_inc(s_kv_kept, 16)
            sp.dma_start(v_p, v_tok[:, NB - 1, :]).then_inc(s_kv_kept, 16)
            for n, dst in ((0, k_s), (1, v_s)):
                for b in range(DEC_B):
                    sp.dma_start(dst[b, WIN - DEC_T:WIN, :], kv_new[DEC_T * b:DEC_T * b + DEC_T, n, :])\
                      .then_inc(s_kv_kept, 16)
            load_quad(("o", 1, 1), pv, 1)
            load_mlp(1)
            for h, (c0, n) in enumerate(HALF):
                for k in range(KT):
                    sp.wait_ge(s_yout[k % 2], 4 * h + k // 2 + 1)
                    sp.dma_start(y_t[128 * k:128 * k + 128, c0:c0 + n], acc[:, k, c0:c0 + n]).then_inc(s_out, 16)
            sp.wait_ge(s_out, 16 * 2 * KT)
            sp.wait_ge(s_kept, 16 * 3)
            sp.wait_ge(s_kv_kept, 16 * (2 + 2 * DEC_B))

        arrivals = []
        count = [0] * STAGES
        for j, (kind, _) in enumerate(jobs):
            count[j % STAGES] += 32 if kind == "g" else 16
            arrivals.append(count[j % STAGES])

        def split_targets(j):
            kind, w = jobs[j]
            if kind == "g":
                p = (j - 4) // 5
                return gate_hi[:, p % 2, :], gate_lo[:, p % 2, :], stage[:, j % STAGES, 0:512]
            return w_hi[:, w % SLOTS, :], w_lo[:, w % SLOTS, :], stage[:, j % STAGES, :]

        @block.scalar
        def _(act):
            A = nc.scalar.activation
            seq = [0]

            def ordered(ins):
                seq[0] += 1
                ins.then_inc(s_seqA, 1)
                return seq[0]

            def split(js, i=None, per=0, per_units=0, freed=0):
                for j in js:
                    hi, _, raw = split_targets(j)
                    kind, w = jobs[j]
                    if i is None:
                        act.wait_ge(s_arrived[j % STAGES], arrivals[j])
                        if kind == "w" and w >= SLOTS:
                            act.wait_ge(s_unit, free_at[w - SLOTS])
                        if kind == "g" and j >= 14:
                            act.wait_ge(s_unit, mark[("gate", 2 * ((j - 4) // 5) - 3)] + 4)
                    else:
                        act.wait_ge(s_arrived[j % STAGES], i * (16 * per // STAGES) + arrivals[j])
                        act.wait_ge(s_unit, i * per_units + freed)
                    A(hi, raw, ACT.Copy).then_inc(s_whi, 1)

            def unit(n):
                act.wait_ge(s_unit, n + 1)
                return bank[:, n % BANKS, :]

            def x_split(h, ks=range(4)):
                c0, n = HALF[h]
                for k in ks:
                    if h == 0:
                        act.wait_ge(s_xa[k], 16)
                    elif k == 0:
                        act.wait_ge(s_xb, 32)
                    A(x_hi[:, 2 * k:2 * k + 2, c0:c0 + n], acc[:, 2 * k:2 * k + 2, c0:c0 + n], ACT.Copy)\
                        .then_inc(s_xhi, 1)

            x_split(0, [0])
            late = VEC["sinks"][0]
            act.dma_start(vecs[:, 0:late], vec[:, 0:late]).then_inc(s_vec, 16)
            split([0])
            x_split(0, [1, 2])
            split([1])
            x_split(0, [3])
            split([2, 3])
            act.wait_ge(s_vec, 16)
            act.dma_start(vecs[:, late:NVEC], vec[:, late:NVEC]).then_inc(s_vec, 16)
            def chain(s):
                p, (_, n) = s // 2, HALF[s % 2]
                m0 = mark[("gate", s)]
                if s >= 1:
                    act.wait_ge(s_p, s)
                for t in range(2):
                    m = 2 * p + t
                    A(th_r[:, t, :n], unit(m0 + 2 * t)[:, :n], ACT.Tanh, bias=dv[:, 0, m:m + 1], scale=0.5)\
                        .then_inc(s_evA, 1)
                    A(th_g[:, t, :n], unit(m0 + 2 * t + 1)[:, :n], ACT.Tanh, bias=dv[:, 1, m:m + 1], scale=0.5)\
                        .then_inc(s_evA, 1)
                act.wait_ge(s_evA, read_by(m0 + 4, "A"))
                for t in range(2):
                    m = 2 * p + t
                    last = ordered(A(decay[:, t, :n], th_r[:, t, :n], ACT.Exp, bias=dv[:, 2, m:m + 1],
                                     scale=dv[:, 2, m:m + 1]))
                act.wait_ge(s_seqA, last)
                for t in range(2):
                    m = 2 * p + t
                    last = ordered(A(th_r[:, t, :n], th_r[:, t, :n], ACT.Tanh, bias=dv[:, 3, m:m + 1],
                                     scale=dv[:, 3, m:m + 1]))
                return last

            def chain_root(s, last):
                _, n = HALF[s % 2]
                act.wait_ge(s_seqA, last)
                A(th_r[:, :, :n], th_r[:, :, :n], ACT.Sqrt).then_inc(s_root, 1)

            def chain_hi(s):
                p, (c0, n) = s // 2, HALF[s % 2]
                act.wait_ge(s_p, s + 1)
                A(m_hi[:, 2 * p:2 * p + 2, c0:c0 + n], z[:, s % 2, :, :n], ACT.Copy).then_inc(s_phi, 1)

            def copy_u(s, t):
                p, h = s // 2, s % 2
                n = HALF[h][1]
                src = unit(mark[("x", s)] + t)
                if h == 1:
                    ordered(A(us[:, t, :, 3:], src[:, 256:n].rearrange("p (b t) -> p b t", t=DEC_T),
                              ACT.Identity, bias=V("b_x", 2 * p + t)))
                A(u[:, t, 3:3 + 256], src[:, 0:256], ACT.Identity, bias=V("b_x", 2 * p + t)).then_inc(s_evA, 1)

            def gelu_in(s, t):
                p, (_, n) = s // 2, HALF[s % 2]
                A(z[:, s % 2, t, :n], unit(mark[("y", s)] + t)[:, :n], ACT.Identity,
                  bias=V("b_y", 2 * p + t)).then_inc(s_evA, 1)
                if t:
                    act.wait_ge(s_evA, read_by(mark[("y", s)] + 2, "A"))
                    if s >= 1:
                        act.wait_ge(s_gy, s)
                    A(sq[:, :, :n], z[:, s % 2, :, :n], ACT.Square).then_inc(s_gsq, 1)

            def gelu_tanh(s):
                _, n = HALF[s % 2]
                act.wait_ge(s_gin, s + 1)
                A(sq[:, :, :n], sq[:, :, :n], ACT.Tanh, scale=GELU_OUT).then_inc(s_gth, 1)

            for s in range(8):
                _, n = HALF[s % 2]
                act.wait_ge(s_halo, s + 1)
                copy_u(s, 0)
                if s:
                    split(next_jobs(s)[:1])
                copy_u(s, 1)
                if s == 0:
                    x_split(1)
                    split([4])
                    split(next_jobs(s)[:1])
                    act.wait_ge(s_sp, 1)
                    A(tiny[:, 2, :], tiny[:, 1, :], ACT.Exp, scale=-1.0).then_inc(s_spe, 1)
                if s == 1:
                    act.wait_ge(s_dv, 1)
                if s >= 1:
                    gelu_tanh(s - 1)
                if s >= 2:
                    chain_hi(s - 2)
                if s >= 1:
                    last = chain(s - 1)
                act.wait_ge(s_conv, s + 1)
                if s >= 1:
                    act.wait_ge(s_unit, mark[("gate", s - 1)] + 4)
                A(xc_hi[:, :, :n], xc[s % 2][:, :, :n], ACT.Copy).then_inc(s_xchi, 1)
                if s >= 2:
                    act.wait_ge(s_plo, s - 1)
                gelu_in(s, 0)
                if s >= 1:
                    chain_root(s - 1, last)
                gelu_in(s, 1)
                split(next_jobs(s)[1:])
            chain_hi(6)
            split(range(job_at[("o", 0, 1)][0], job_at[("o", 0, 1)][0] + 4))
            gelu_tanh(7)
            chain_root(7, chain(7))
            chain_hi(7)

            def square(L, h, m):
                c0, n = HALF[h]
                pos = tile_pos(L, h, m)
                act.wait_ge(s_evV, read_by(unit_of("down" if L % 2 else "o", L, h, m) + 1, "V"))
                if pos >= 2:
                    act.wait_ge(s_s2, pos - 1)
                A(sqt[:, pos % 2, :n], acc[:, m, c0:c0 + n], ACT.Square).then_inc(s_sqt, 1)

            def norm_stats(L, h):
                _, n = HALF[h]
                m0 = mark[("ln", L, h)]
                idx = 2 * L + h
                if idx:
                    act.wait_ge(s_xhat, 4 * idx)
                A(mean[:, :n], unit(m0)[:, :n], ACT.Copy).then_inc(s_evA, 1)
                act.wait_ge(s_var, idx + 1)
                A(rstd[:, :n], msq[:, :n], ACT.Sqrt).then_inc(s_std, 1)

            def norm_apply(L, h, beside=lambda t: None):
                c0, n = HALF[h]
                idx = 2 * L + h
                for k in range(KT):
                    act.wait_ge(s_xhat, 4 * idx + k // 2 + 1)
                    g, b = V("ln_g", L * KT + k), V("ln_b", L * KT + k)
                    xhat = acc[:, k, c0:c0 + n]
                    if L < 3:
                        A(x_hi[:, k, c0:c0 + n], xhat, ACT.Identity, bias=b, scale=g)
                        if 8 * idx + k >= 2:
                            act.wait_ge(s_ylo, 8 * idx + k - 1)
                        A(y_tmp[:, k % 2, :n], xhat, ACT.Identity, bias=b, scale=g).then_inc(s_y, 1)
                    elif k % 2 == 0:
                        A(xhat, xhat, ACT.Identity, bias=b, scale=g).then_inc(s_yout[0], 1)
                    if k % 2:
                        beside(k // 2)

            def tiles(L, early, late):
                def beside(t):
                    for m in BESIDE[t]:
                        square(L, 1, m)
                    split(late[t:t + 1])

                for m in range(KT):
                    split(early[m:m + 1])
                    square(L, 0, m)
                square(L, 1, 0)
                square(L, 1, 1)
                norm_stats(L, 0)
                norm_apply(L, 0, beside)

            def up(l, q, c=0, i=0):
                c0, n = HALF[q // 4]
                n0 = mark[("up", l)] + 24 * c + q
                t0 = (CHUNKS * l + c) * 8 + q
                act.wait_ge(s_unit, i * 24 + (n0 + 1))
                act.wait_ge(s_hsq, i * 8 + (t0 + 1))
                A(relu[:, q % 2, :n], bank[:, n0 % BANKS, :n], ACT.Relu).then_inc(s_evA, 1)
                act.wait_ge(s_evA, i * 8 + read_by(n0 + 1, "A"))
                A(m_hi[:, q % 4, c0:c0 + n], relu[:, q % 2, :n], ACT.Square).then_inc(s_hhi, 1)

            def mlp(l):
                j0 = job_at[("mlp", l)][0]
                split(range(j0 + 4, j0 + 6))
                norm_stats(2 * l, 1)

                def beside(t):
                    up(l, t)
                    split(range(j0 + 6 + t, min(j0 + 7 + t, j0 + 8)))

                norm_apply(2 * l, 1, beside)
                for q in range(4, 8):
                    up(l, q)
                with act.Fori(0, CHUNKS - 1) as i:
                    split(range(j0 + 8, j0 + 12), i, 8, 24, mark[("loop", l)])
                    for q in range(8):
                        if q % 2 == 0:
                            split([j0 + 12 + q // 2], i, 8, 24, mark[("loop", l)] + 16)
                        up(l, q, 1, i)
                tiles(2 * l + 1, next_slabs(("qkv", 0)) if l == 0 else (), ())

            tiles(0, (), next_slabs(("mlp", 0)))
            mlp(0)
            def qkv(g, h, ts=range(4)):
                c0, n = HALF[h]
                for t in ts:
                    i = 4 * g + t
                    src = unit(mark[("qkv", g, h)] + t)[:, :n]
                    if i < 2:
                        A((k_t if i == 0 else v_t)[:, c0:c0 + n], src, ACT.Identity, bias=V("b_qkv", i))\
                            .then_inc(s_evA, 1)
                    else:
                        bq = dv[:, 4, i - 2:i - 1]
                        if h == 1:
                            ordered(A(q_s[:, :, i - 2, :], src[:, 256:n].rearrange("p (b t) -> p b t", t=DEC_T),
                                      ACT.Identity, bias=bq, scale=HD ** -0.5))
                        A(q_tile(i - 2)[:, c0:c0 + 256], src[:, 0:256], ACT.Identity, bias=bq, scale=HD ** -0.5)\
                            .then_inc(s_evA, 1)
            qj = [job_at[("qkv", g)][0] for g in range(3)]
            split(range(qj[1], qj[1] + 2))
            norm_stats(1, 1)

            def beside_qkv(t):
                qkv(0, 0, [t])
                split(range(qj[1] + 2 + t, min(qj[1] + 3 + t, qj[1] + 4)))

            norm_apply(1, 1, beside_qkv)
            qkv(0, 1)
            split([qj[2], qj[2] + 1])
            qkv(1, 0)
            qkv(1, 1)
            act.wait_ge(s_tok, 1)
            A(v_tok[:, :, :], bank[:, score_bank(1), :].rearrange("p (n d) -> p n d", n=NB), ACT.Copy)\
                .then_inc(s_tokc, 1)
            act.wait_ge(s_tok, 2)
            A(k_tok[:, :], bank[:, score_bank(1) + 1, 0:128], ACT.Copy).then_inc(s_tokc, 1)
            A(kv_new[:, :, :], bank[0:NS, score_bank(1) + 1, 128:384].rearrange("p (n d) -> p n d", n=2), ACT.Copy)\
                .then_inc(s_tokc, 1)
            oj = job_at[("o", 1, 0)][0]

            def exponentials(T):
                w = step_width(T)
                act.wait_ge(s_max, T + 1)
                for e in range(4):
                    pr = probs[:, T % 4, e, 0:w]
                    ordered(A(pr, pr, ACT.Exp, bias=stat[:, T % 4, 1, e:e + 1], accum_out=stat[:, T % 4, 2, e:e + 1]))
                A(stat[:, T % 4, 4, :], stat[:, T % 4, 3, :], ACT.Exp).then_inc(s_exp, 1)

            exponentials(0)
            qkv(2, 0, range(2))
            qkv(2, 1, range(2))
            exponentials(1)
            for it in range(17 + 2):
                if it + 2 < 17:
                    exponentials(it + 2)
                if it < 17:
                    act.wait_ge(s_pt, it + 1)
                    if it >= 2:
                        act.wait_ge(s_pv, it - 1)
                    ins = A(probs_t[:, it % 2, 0, :], bank[:, trans_bank(0), :], ACT.Copy)
                    if step_width(it) > WIN:
                        ordered(ins)
                        rows = NS if it == 16 else 128
                        ins = A(probs_t[0:rows, it % 2, 1, :], bank[0:rows, trans_bank(1), :], ACT.Copy)
                    ins.then_inc(s_pt_read, 1)
                if it >= 2:
                    act.wait_ge(s_pv, it - 1)
                    dst, src = mixed(it - 2, x_hi)
                    A(dst, src, ACT.Copy).then_inc(s_ohi, 1)
                if it % 2 == 0 and it < 16:
                    split([oj + it // 2])
            tiles(2, (), next_slabs(("mlp", 1)))
            mlp(1)
            norm_stats(3, 1)
            norm_apply(3, 1)

        @block.vector
        def _(dve):
            vt = nc.vector
            seq = [0]

            def ordered(ins):
                seq[0] += 1
                ins.then_inc(s_seqV, 1)
                dve.wait_ge(s_seqV, seq[0])

            def split(js, i=None, per=0):
                for j in js:
                    hi, lo, raw = split_targets(j)
                    dve.wait_ge(s_whi, j + 1 if i is None else i * per + (j + 1))
                    vt.tensor_tensor(lo, raw, hi.bitcast(F32), ALU.subtract).then_inc(s_wlo, 1)

            def unit(n):
                dve.wait_ge(s_unit, n + 1)
                return bank[:, n % BANKS, :]

            def x_split(h, ks=range(4)):
                c0, n = HALF[h]
                for k in ks:
                    dve.wait_ge(s_xhi, 4 * h + k + 1)
                    vt.tensor_tensor(x_lo[:, 2 * k:2 * k + 2, c0:c0 + n], acc[:, 2 * k:2 * k + 2, c0:c0 + n],
                                     x_hi[:, 2 * k:2 * k + 2, c0:c0 + n].bitcast(F32), ALU.subtract).then_inc(s_xlo, 1)

            vt.memset(ones[:, :], 1.0 / D).then_inc(s_const, 1)
            vt.memset(zeros[:, :], 0.0).then_inc(s_const, 1)
            vt.memset(tiny[:, 6, :], 0.0).then_inc(s_hsq, 2)
            vt.memset(tiny[:, 7, :], 0.0).then_inc(s_hlo, 2)
            x_split(0, [0])
            split([0])
            x_split(0, [1, 2])
            split([1])
            x_split(0, [3])
            split([2, 3])

            def derive():
                lam = V("lam", 0, KT)
                ordered(vt.tensor_scalar(tiny[:, 0, :], lam, -1.0, None, ALU.mult))
                vt.tensor_tensor(tiny[:, 1, :], tiny[:, 0, :], lam, ALU.max).then_inc(s_sp, 1)
                vt.tensor_scalar(dv[:, 0, :], V("b_ga", 0, KT), 0.5, None, ALU.mult)
                vt.tensor_scalar(dv[:, 1, :], V("b_gi", 0, KT), 0.5, None, ALU.mult)
                vt.tensor_scalar(dv[:, 4, :], V("b_qkv", 2, KT), HD ** -0.5, None, ALU.mult)
                for L in range(3):
                    vt.tensor_scalar(dv[:, 5 + L, :], V("ln_g", L * KT, KT), ALPHA, None, ALU.mult)
                    if L == 1:
                        vt.scalar_tensor_tensor(dv[:, 8 + L, :], V("ln_b", L * KT, KT), ALPHA, V("b_o", 0, KT),
                                                ALU.mult, ALU.add)
                    else:
                        vt.tensor_scalar(dv[:, 8 + L, :], V("ln_b", L * KT, KT), ALPHA, None, ALU.mult)
                dve.wait_ge(s_spe, 1)
                e, zz, z2, f = (tiny[:, k, :] for k in (2, 3, 4, 5))
                ordered(vt.tensor_scalar(zz, e, 2.0, None, ALU.add))
                ordered(vt.reciprocal(z2, zz))
                ordered(vt.tensor_tensor(zz, e, z2, ALU.mult))
                ordered(vt.tensor_tensor(z2, zz, zz, ALU.mult))
                ordered(vt.tensor_scalar(f, z2, 1.0 / 15.0, None, ALU.mult))
                for k in (13, 11, 9, 7, 5, 3):
                    ordered(vt.scalar_tensor_tensor(f, f, 1.0 / k, z2, ALU.add, ALU.mult))
                ordered(vt.scalar_tensor_tensor(f, f, 1.0, zz, ALU.add, ALU.mult))
                ordered(vt.tensor_scalar(f, f, 2.0, None, ALU.mult))
                ordered(vt.tensor_scalar(tiny[:, 0, :], tiny[:, 0, :], 0.0, None, ALU.max))
                ordered(vt.tensor_tensor(f, f, tiny[:, 0, :], ALU.add))
                ordered(vt.tensor_scalar(dv[:, 3, :], f, 2.0, None, ALU.mult))
                vt.tensor_scalar(dv[:, 2, :], f, -4.0, None, ALU.mult).then_inc(s_dv, 1)

            def halo(s):
                p, h = s // 2, s % 2
                if s:
                    dve.wait_ge(s_conv, s)
                if h == 0:
                    vt.memset(u[:, :, 0:3], 0.0).then_inc(s_halo, 1)
                else:
                    at = VEC["conv_state"][0] + 2 * p * DEC_B * 3
                    state = vecs[:, at:at + 2 * DEC_B * 3].rearrange("p (t b k) -> p t b k", t=2, b=DEC_B)
                    for t in range(2):
                        seq[0] += 1
                        vt.tensor_copy(us[:, t, :, 0:3], state[:, t]).then_inc(s_seqV, 1)
                    vt.tensor_copy(u[:, :, 0:3], u[:, :, 256:259]).then_inc(s_halo, 1)

            def gated(s):
                _, n = HALF[s % 2]
                dve.wait_ge(s_evA, read_by(mark[("gate", s)] + 4, "A"))
                vt.scalar_tensor_tensor(th_g[:, :, :n], th_g[:, :, :n], 1.0, xc[s % 2][:, :, :n], ALU.add, ALU.mult)\
                    .then_inc(s_gated, 1)

            def recur(s):
                p, h = s // 2, s % 2
                c0, n = HALF[h]
                dve.wait_ge(s_root, s + 1)
                dve.wait_ge(s_gated, s + 1)
                ordered(vt.scalar_tensor_tensor(th_r[:, :, :n], decay[:, :, :n], 1.0, th_r[:, :, :n],
                                                ALU.add, ALU.mult))
                ordered(vt.scalar_tensor_tensor(th_g[:, :, :n], th_r[:, :, :n], 0.5, th_g[:, :, :n],
                                                ALU.mult, ALU.mult))
                if h == 1:
                    first = slice(256, n, DEC_T)
                    h0 = V("h0", 2 * p * DEC_B, 2 * DEC_B).rearrange("p (t b) -> p t b", t=2)
                    t3 = tiny[:, 6:8, :]
                    ordered(vt.tensor_tensor(t3, decay[:, :, first], h0, ALU.mult))
                    ordered(vt.tensor_tensor(th_g[:, :, first], th_g[:, :, first], t3, ALU.add))
                    ordered(vt.memset(decay[:, :, first], 0.0))
                for t in range(2):
                    m = 2 * p + t
                    init = 0.0 if h == 0 else out_small[:, m, 0:1]
                    ins = vt.tensor_tensor_scan(th_r[:, t, :n], decay[:, t, :n], th_g[:, t, :n], init,
                                                ALU.mult, ALU.add)
                    ins.then_inc(s_scan, 1)
                dve.wait_ge(s_scan, 2 * s + 2)
                for t in range(2):
                    m = 2 * p + t
                    seq[0] += 1
                    vt.tensor_copy(out_small[:, m, 0:1], th_r[:, t, 255:256]).then_inc(s_seqV, 1)
                    if h == 1:
                        seq[0] += 1
                        vt.tensor_copy(out_small[:, m, 1:9], th_r[:, t, 256 + DEC_T - 1:n:DEC_T]).then_inc(s_seqV, 1)
                dve.wait_ge(s_gy, s + 1)
                vt.scalar_tensor_tensor(z[:, s % 2, :, :n], th_r[:, :, :n], 0.5, z[:, s % 2, :, :n],
                                        ALU.mult, ALU.mult).then_inc(s_p, 1)

            def gelu_out(s):
                _, n = HALF[s % 2]
                dve.wait_ge(s_gth, s + 1)
                vt.scalar_tensor_tensor(z[:, s % 2, :, :n], sq[:, :, :n], 1.0, z[:, s % 2, :, :n], ALU.add, ALU.mult)\
                    .then_inc(s_gy, 1)

            halo(0)
            dve.wait_ge(s_vec, 16)
            for s in range(8):
                p, h = s // 2, s % 2
                c0, n = HALF[h]
                if s == 0:
                    x_split(1)
                    split([4])
                split(next_jobs(s)[:1])
                if s:
                    gelu_out(s - 1)
                xcs = xc[s % 2]
                dve.wait_ge(s_conv0, s + 1)
                for k in range(1, CONV):
                    for t in range(2):
                        m = 2 * p + t
                        wk = V("conv_w", k * KT + m)
                        ins = vt.scalar_tensor_tensor(xcs[:, t, 0:256], u[:, t, k:k + 256], wk, xcs[:, t, 0:256],
                                                      ALU.mult, ALU.add)
                        if h == 1:
                            seq[0] += 1
                            ins.then_inc(s_seqV, 1)
                            xs = xcs[:, t, 256:n].rearrange("p (b t) -> p b t", t=DEC_T)
                            ins = vt.scalar_tensor_tensor(xs, us[:, t, :, k:k + DEC_T], wk, xs, ALU.mult, ALU.add)
                        if k == CONV - 1 and t == 1:
                            ins.then_inc(s_conv, 1)
                        else:
                            seq[0] += 1
                            ins.then_inc(s_seqV, 1)
                    if k < CONV - 1:
                        dve.wait_ge(s_seqV, seq[0])
                if h == 1:
                    for t in range(2):
                        m = 2 * p + t
                        rows = out_small[:, m, 9:36].rearrange("p (b k) -> p b k", k=3)
                        seq[0] += 2
                        vt.tensor_copy(rows[:, 0, :], u[:, t, 256:259]).then_inc(s_seqV, 1)
                        vt.tensor_copy(rows[:, 1:9, :], us[:, t, :, DEC_T:DEC_T + 3]).then_inc(s_seqV, 1)
                if s < 7:
                    halo(s + 1)
                if s == 0:
                    derive()
                    dve.wait_ge(s_vec, 32)
                if s:
                    gated(s - 1)
                    recur(s - 1)
                dve.wait_ge(s_gsq, s + 1)
                vt.scalar_tensor_tensor(sq[:, :, :n], sq[:, :, :n], GELU_IN, z[:, s % 2, :, :n], ALU.add, ALU.mult)\
                    .then_inc(s_gin, 1)
                split(next_jobs(s)[1:])
            split(range(job_at[("o", 0, 1)][0], job_at[("o", 0, 1)][0] + 4))
            gelu_out(7)
            gated(7)
            recur(7)

            def tile_done(L, h, m, src, n_read):
                c0, n = HALF[h]
                if n_read > 8:
                    dve.wait_ge(s_evV, n_read - 8)
                vt.tensor_tensor(acc[:, m, c0:c0 + n], src[:, :n], acc[:, m, c0:c0 + n], ALU.add)\
                    .then_inc(s_evV, 1)
                pos = tile_pos(L, h, m)
                dve.wait_ge(s_evV, n_read)
                if pos:
                    dve.wait_ge(s_s1, pos)
                s1 = sums[h][0]
                vt.tensor_tensor(s1[:, :n], acc[:, m, c0:c0 + n], zeros[:, :n] if m == 0 else s1[:, :n], ALU.add)\
                    .then_inc(s_s1, 1)

            def norm_stats(L, h):
                _, n = HALF[h]
                m0 = mark[("ln", L, h)]
                idx = 2 * L + h
                dve.wait_ge(s_evA, read_by(m0 + 1, "A"))
                ordered(vt.tensor_tensor(msq[:, :n], mean[:, :n], mean[:, :n], ALU.mult))
                vt.tensor_tensor(msq[:, :n], unit(m0 + 1)[:, :n], msq[:, :n], ALU.subtract).then_inc(s_evV, 1)
                dve.wait_ge(s_evV, read_by(m0 + 2, "V"))
                vt.tensor_scalar(msq[:, :n], msq[:, :n], 0.0, EPS, ALU.max, ALU.add).then_inc(s_var, 1)

            def norm_apply(L, h, beside=lambda t: None):
                c0, n = HALF[h]
                idx = 2 * L + h

                def pair(a, t):
                    return a[:, 2 * t:2 * t + 2, c0:c0 + n]

                def wide(a):
                    return a[:, 0:n].rearrange("p (o n) -> p o n", o=1).broadcast_to([128, 2, n])

                def low(k):
                    if L == 3:
                        return
                    dve.wait_ge(s_y, 8 * idx + k + 1)
                    vt.tensor_tensor(x_lo[:, k, c0:c0 + n], y_tmp[:, k % 2, :n],
                                     x_hi[:, k, c0:c0 + n].bitcast(F32), ALU.subtract).then_inc(s_ylo, 1)

                for t in range(2):
                    seq[0] += 1
                    vt.tensor_tensor(pair(acc, t), pair(acc, t), wide(mean), ALU.subtract).then_inc(s_seqV, 1)
                dve.wait_ge(s_std, idx + 1)
                ordered(vt.reciprocal(rstd[:, :n], rstd[:, :n]))
                for t in range(4):
                    if t >= 2:
                        dve.wait_ge(s_cent, 2 * idx + t - 1)
                    vt.tensor_tensor(pair(acc, t), pair(acc, t), wide(rstd), ALU.mult).then_inc(s_xhat, 1)
                    if t:
                        low(2 * t - 2)
                        low(2 * t - 1)
                    beside(t)
                low(6)
                low(7)

            def add_tile(name, L, h, m):
                n0 = unit_of(name, L, h, m)
                tile_done(L, h, m, unit(n0), read_by(n0 + 1, "V"))

            def tiles(name, L, early, late):
                def beside(t):
                    if t:
                        split(late[t - 1:t])
                    for m in BESIDE[t]:
                        add_tile(name, L, 1, m)

                for m in range(KT):
                    add_tile(name, L, 0, m)
                    if m % 2:
                        split(early[m // 2:m // 2 + 1])
                add_tile(name, L, 1, 0)
                add_tile(name, L, 1, 1)
                norm_stats(L, 0)
                norm_apply(L, 0, beside)
                split(late[3:])

            def up(l, q, c=0, i=0):
                c0, n = HALF[q // 4]
                n0 = mark[("up", l)] + 24 * c + q
                t0 = (CHUNKS * l + c) * 8 + q
                dve.wait_ge(s_evA, i * 8 + read_by(n0 + 1, "A"))
                dve.wait_ge(s_hlo, i * 8 + (t0 + 1))
                vt.tensor_tensor(h_sq[:, q % 2, :n], relu[:, q % 2, :n], relu[:, q % 2, :n], ALU.mult)\
                    .then_inc(s_hsq, 1)
                dve.wait_ge(s_hhi, i * 8 + (t0 + 1))
                dve.wait_ge(s_hsq, i * 8 + (t0 + 3))
                vt.tensor_tensor(m_lo[:, q % 4, c0:c0 + n], h_sq[:, q % 2, :n],
                                 m_hi[:, q % 4, c0:c0 + n].bitcast(F32), ALU.subtract).then_inc(s_hlo, 1)

            def mlp(l):
                j0 = job_at[("mlp", l)][0]
                split(range(j0 + 4, j0 + 6))
                norm_stats(2 * l, 1)

                def beside(t):
                    if t:
                        up(l, t - 1)
                        split(range(j0 + 5 + t, min(j0 + 6 + t, j0 + 8)))

                norm_apply(2 * l, 1, beside)
                for q in range(3, 8):
                    up(l, q)
                dve.wait_ge(s_res, 8 * (4 * l + 2))
                with dve.Fori(0, CHUNKS - 1) as i:
                    for q in range(16):
                        c0, n = HALF[q // 8]
                        n0 = mark[("loop", l)] + q
                        if q % 4 == 0:
                            split([j0 + 8 + q // 4], i, 8)
                        dve.wait_ge(s_unit, i * 24 + (n0 + 1))
                        dve.wait_ge(s_evV, i * 16 + (read_by(n0, "V") - 8))
                        vt.tensor_tensor(acc[:, q % 8, c0:c0 + n], bank[:, n0 % BANKS, :n],
                                         acc[:, q % 8, c0:c0 + n], ALU.add).then_inc(s_evV, 1)
                    for q in range(8):
                        if q % 2 == 0:
                            split([j0 + 12 + q // 2], i, 8)
                        up(l, q, 1, i)
                tiles("down", 2 * l + 1, next_slabs(("qkv", 0)) if l == 0 else (), ())

            dve.wait_ge(s_res0, 2)
            tiles("o", 0, (), next_slabs(("mlp", 0)))
            mlp(0)
            qj = job_at[("qkv", 1)][0]
            split(range(qj, qj + 2))
            norm_stats(1, 1)
            norm_apply(1, 1, lambda t: split(range(qj + 1 + t, qj + 2 + t)) if t in (1, 2) else None)
            split(range(qj + 4, qj + 6))
            oj = job_at[("o", 1, 0)][0]

            def mask_max(T):
                w = step_width(T)
                st = stat[:, T % 4]
                dve.wait_ge(s_sc, T + 1)
                if T >= 4:
                    dve.wait_ge(s_pt, T - 3)
                pr = probs[:, T % 4, :, 0:w]
                src = bank[:, score_bank(T):score_bank(T) + 2, :].rearrange("p v (i c) -> p (v i) c", i=2)[:, :, 0:w]
                if T < 16:
                    mk = V("mask", 2 * WIN - w, w).rearrange("p (o c) -> p o c", o=1).broadcast_to([128, 4, w])
                    vt.tensor_tensor(pr, src, mk, ALU.add).then_inc(s_sm, 1)
                else:
                    mk = V("mask_rows", 0, 2 * w).rearrange("p (b c) -> p b c", b=2)
                    for v in range(2):
                        ins = vt.tensor_tensor(pr[:, 2 * v:2 * v + 2, :], src[:, 2 * v:2 * v + 2, :], mk, ALU.add)
                        if v == 0:
                            seq[0] += 1
                            ins.then_inc(s_seqV, 1)
                    ins.then_inc(s_sm, 1)
                sink = V("sinks", 4 * (T % 4), 4) if T < 16 else V("sink_rows", 0, 4)
                dve.wait_ge(s_sm, T + 1)
                ordered(vt.tensor_reduce(st[:, 0, :], pr, AX.X, ALU.max))
                ordered(vt.tensor_tensor(st[:, 0, :], st[:, 0, :], sink, ALU.max))
                seq[0] += 1
                vt.tensor_tensor(st[:, 3, :], sink, st[:, 0, :], ALU.subtract).then_inc(s_seqV, 1)
                vt.tensor_scalar(st[:, 1, :], st[:, 0, :], -1.0, None, ALU.mult).then_inc(s_max, 1)

            def denominators(T):
                st = stat[:, T % 4]
                dve.wait_ge(s_exp, T + 1)
                ordered(vt.tensor_tensor(st[:, 5, :], st[:, 2, :], st[:, 4, :], ALU.add))
                vt.reciprocal(st[:, 6, :], st[:, 5, :]).then_inc(s_den, 1)

            mask_max(0)
            mask_max(1)
            denominators(0)
            mask_max(2)
            denominators(1)
            for it in range(17 + 2):
                if it + 3 < 17:
                    mask_max(it + 3)
                if it + 2 < 17:
                    denominators(it + 2)
                if it >= 2:
                    dve.wait_ge(s_ohi, it - 1)
                    dst, src = mixed(it - 2, x_lo)
                    hi, _ = mixed(it - 2, x_hi)
                    vt.tensor_tensor(dst, src, hi.bitcast(F32), ALU.subtract).then_inc(s_olo, 1)
            dve.wait_ge(s_wlo, oj + 8)
            dve.wait_ge(s_res, 8 * 4)
            tiles("o", 2, (), next_slabs(("mlp", 1)))
            mlp(1)
            norm_stats(3, 1)
            norm_apply(3, 1)

        @block.gpsimd
        def _(pool):
            pt = nc.gpsimd
            seq = [0]
            pool.wait_ge(s_vec, 16)
            def residual0(h):
                c0, n = HALF[h]
                for k in range(KT):
                    pool.wait_ge(s_xlo, 4 * h + k // 2 + 1)
                    ins = pt.tensor_scalar(acc[:, k, c0:c0 + n], acc[:, k, c0:c0 + n], ALPHA, V("b_out", k),
                                           ALU.mult, ALU.add)
                    if k < KT - 1:
                        ins.then_inc(s_seqP, 1)
                ins.then_inc(s_res0, 1)
            residual0(0)

            def low_product(s):
                p, (c0, n) = s // 2, HALF[s % 2]
                pool.wait_ge(s_phi, s + 1)
                pt.tensor_tensor(m_lo[:, 2 * p:2 * p + 2, c0:c0 + n], z[:, s % 2, :, :n],
                                 m_hi[:, 2 * p:2 * p + 2, c0:c0 + n].bitcast(F32), ALU.subtract).then_inc(s_plo, 1)

            for s in range(8):
                p, h = s // 2, s % 2
                c0, n = HALF[h]
                pool.wait_ge(s_evA, read_by(mark[("x", s)] + 2, "A"))
                if s >= 2:
                    pool.wait_ge(s_gated, s - 1)
                    pool.wait_ge(s_xclo, s - 1)
                xcs = xc[s % 2]
                for t in range(2):
                    m = 2 * p + t
                    ins = pt.tensor_scalar(xcs[:, t, 0:256], u[:, t, 0:256], V("conv_w", m), V("conv_b", m),
                                           ALU.mult, ALU.add)
                    if h == 1:
                        ins.then_inc(s_seqP, 1)
                        ins = pt.tensor_scalar(xcs[:, t, 256:n].rearrange("p (b t) -> p b t", t=DEC_T),
                                               us[:, t, :, 0:DEC_T], V("conv_w", m), V("conv_b", m),
                                               ALU.mult, ALU.add)
                    if t == 0:
                        ins.then_inc(s_seqP, 1)
                ins.then_inc(s_conv0, 1)
                if s >= 2:
                    low_product(s - 2)
                pool.wait_ge(s_xchi, s + 1)
                if s:
                    pool.wait_ge(s_unit, mark[("gate", s - 1)] + 4)
                pt.tensor_tensor(xc_lo[:, :, :n], xcs[:, :, :n], xc_hi[:, :, :n].bitcast(F32), ALU.subtract)\
                  .then_inc(s_xclo, 1)
                if s == 0:
                    residual0(1)
            low_product(6)
            low_product(7)

            def add_square(L, h, m):
                _, n = HALF[h]
                pos = tile_pos(L, h, m)
                s2 = sums[h][1]
                pool.wait_ge(s_sqt, pos + 1)
                if pos:
                    pool.wait_ge(s_s2, pos)
                pt.tensor_tensor(s2[:, :n], sqt[:, pos % 2, :n], zeros[:, :n] if m == 0 else s2[:, :n], ALU.add)\
                  .then_inc(s_s2, 1)

            def centre(L, h):
                c0, n = HALF[h]
                pool.wait_ge(s_evA, read_by(mark[("ln", L, h)] + 1, "A"))
                for t in (2, 3):
                    pair = acc[:, 2 * t:2 * t + 2, c0:c0 + n]
                    wide = mean[:, 0:n].rearrange("p (o n) -> p o n", o=1).broadcast_to([128, 2, n])
                    pt.tensor_tensor(pair, pair, wide, ALU.subtract).then_inc(s_cent, 1)

            def residual(L, h):
                c0, n = HALF[h]
                idx = 2 * L + h
                for k in range(KT):
                    a = acc[:, k, c0:c0 + n]
                    if L < 3:
                        pool.wait_ge(s_y, 8 * idx + k + 1)
                        pt.tensor_scalar(a, a, dv[:, 5 + L, k:k + 1], dv[:, 8 + L, k:k + 1], ALU.mult, ALU.add)\
                          .then_inc(s_res, 1)
                    elif k % 2:
                        pool.wait_ge(s_xhat, 4 * idx + k // 2 + 1)
                        pt.tensor_scalar(a, a, V("ln_g", L * KT + k), V("ln_b", L * KT + k), ALU.mult, ALU.add)\
                          .then_inc(s_yout[1], 1)

            def tiles(L):
                for pos in range(2 * KT):
                    if pos == KT + 2:
                        centre(L, 0)
                    add_square(L, pos // KT, pos % KT)

            def after_tiles(L):
                centre(L, 1)
                residual(L, 0)
                residual(L, 1)

            def mlp(l):
                after_tiles(2 * l)
                tiles(2 * l + 1)
                after_tiles(2 * l + 1)

            tiles(0)
            pool.dma_start(kc_t[:, :, :], ck_t).then_inc(s_cache, 16)
            pool.dma_start(vc[:, :, :], cache_v.rearrange("b s c -> s b c")).then_inc(s_cache, 16)
            pool.dma_start(k_s[:, 0:WIN - DEC_T, :], cache_k[:, DEC_T:WIN, :]).then_inc(s_kept, 16)
            pool.dma_start(v_s[:, 0:WIN - DEC_T, :], cache_v[:, DEC_T:WIN, :]).then_inc(s_kept, 16)
            pool.dma_start(small, out_small[:, :, :]).then_inc(s_kept, 16)
            mlp(0)
            oj = job_at[("o", 1, 0)][0]
            for T in range(17):
                w = step_width(T)
                pool.wait_ge(s_den, T + 1)
                for e in range(4):
                    pr = probs[:, T % 4, e, 0:w]
                    pt.tensor_scalar(pr, pr, stat[:, T % 4, 6, e:e + 1], 1.0, ALU.mult, ALU.mult).then_inc(s_nrm, 1)
                if T in (1, 3, 5, 7, 9, 11, 13, 16):
                    j = oj + T // 2 - T // 16
                    hi, lo, raw = split_targets(j)
                    pool.wait_ge(s_whi, j + 1)
                    pool.wait_ge(s_wlo, j)
                    pt.tensor_tensor(lo, raw, hi.bitcast(F32), ALU.subtract).then_inc(s_wlo, 1)
            tiles(2)
            mlp(1)

        @block.tensor
        def _(pe):
            mm = nc.tensor.matmul

            def free_bank(n):
                prev = n - BANKS
                if prev >= floor[0]:
                    who = reader[prev]
                    pe.wait_ge(s_evA if who == "A" else s_evV, read_by(prev + 1, who))

            floor = [0]

            def product(n, width, pieces):
                out = bank[:, n % BANKS, :width]
                last = len(pieces) - 1
                for k, (wh, wl, xh, xl) in enumerate(pieces):
                    mm(out, wh, xh, start=(k == 0), stop=False)
                    mm(out, wh, xl, start=False, stop=False)
                    ins = mm(out, wl, xh, start=False, stop=(k == last))
                ins.then_inc(s_unit, 1)

            def slab(w0, k, off):
                s = (w0 + k) % SLOTS
                return w_hi[:, s, off:off + 128], w_lo[:, s, off:off + 128]

            def act_cols(hi, lo, k, h):
                c0, n = HALF[h]
                return hi[:, k, c0:c0 + n], lo[:, k, c0:c0 + n]

            def pair_unit(n, w0, t, h):
                free_bank(n)
                product(n, HALF[h][1], [(*slab(w0, k // 4, 256 * (k % 4) + 128 * t), *act_cols(x_hi, x_lo, k, h))
                                        for k in range(KT)])

            def quad_pieces(w0, t, h, hi=x_hi, lo=x_lo):
                return [(*slab(w0, k // 2, 512 * (k % 2) + 128 * t), *act_cols(hi, lo, k, h)) for k in range(KT)]

            def down_pieces(w0, m, h):
                return [(*slab(w0, k, 128 * m), *act_cols(m_hi, m_lo, k, h)) for k in range(4)]

            def gates(s):
                p, h = s // 2, s % 2
                n = HALF[h][1]
                pe.wait_ge(s_wlo, job_at[("gates", p)][0] + 1)
                pe.wait_ge(s_xclo, s + 1)
                for t in range(2):
                    for g in range(2):
                        n0 = mark[("gate", s)] + 2 * t + g
                        free_bank(n0)
                        off = 256 * t + 128 * g
                        product(n0, n, [(gate_hi[:, p % 2, off:off + 128], gate_lo[:, p % 2, off:off + 128],
                                         xc_hi[:, t, :n], xc_lo[:, t, :n])])

            def norm_sums(L, h):
                _, n = HALF[h]
                n0 = mark[("ln", L, h)]
                pe.wait_ge(s_s1, tile_pos(L, h, 7) + 1)
                free_bank(n0)
                mm(bank[:, n0 % BANKS, :n], ones[:, :], sums[h][0][:, :n], start=True, stop=True).then_inc(s_unit, 1)
                pe.wait_ge(s_s2, tile_pos(L, h, 7) + 1)
                free_bank(n0 + 1)
                mm(bank[:, (n0 + 1) % BANKS, :n], ones[:, :], sums[h][1][:, :n], start=True, stop=True)\
                    .then_inc(s_unit, 1)

            def group_by_k(ns, h, pieces_of, ready, middle=None):
                width = HALF[h][1]
                for n in ns:
                    free_bank(n)
                for k in range(KT):
                    for on in ready(k):
                        pe.wait_ge(*on)
                    for t, n in enumerate(ns):
                        wh, wl, xh, xl = pieces_of(t)[k]
                        out = bank[:, n % BANKS, :width]
                        mm(out, wh, xh, start=(k == 0), stop=False)
                        mm(out, wh, xl, start=False, stop=False)
                        ins = mm(out, wl, xh, start=False, stop=(k == KT - 1))
                        if k == KT - 1:
                            ins.then_inc(s_unit, 1)
                    if k == 2 and middle:
                        middle()

            pe.wait_ge(s_const, 2)
            for s in range(8):
                p, h = s // 2, s % 2
                j, w0 = job_at[("pair", p)]
                if s == 0:
                    def pieces0(t):
                        return [(*slab(w0, k // 4, 256 * (k % 4) + 128 * t), *act_cols(x_hi, x_lo, k, 0))
                                for k in range(KT)]

                    group_by_k(range(2), 0, pieces0,
                               lambda k: ((s_xlo, k // 2 + 1), (s_wlo, k // 4 + 1)))
                else:
                    if s == 1:
                        pe.wait_ge(s_xlo, 8)
                    pe.wait_ge(s_wlo, j + 2)
                    for t in range(2):
                        pair_unit(mark[("x", s)] + t, w0, t, h)
                if s:
                    gates(s - 1)
                pe.wait_ge(s_wlo, j + 4)
                for t in range(2):
                    pair_unit(mark[("y", s)] + t, w0 + 2, t, h)

            def project(l, between={}):
                L = 2 * l
                src = (m_hi, m_lo) if l == 0 else (x_hi, x_lo)
                for h in range(2):
                    for m in range(KT):
                        j, w0 = job_at[("o", l, m // 4)]
                        if l == 0 and h == 0 and m < 4:
                            if m == 0:
                                n0 = unit_of("o", L, 0, 0)
                                group_by_k(range(n0, n0 + 4), 0, lambda t: quad_pieces(w0, t, 0, *src),
                                           lambda k: ((s_wlo, j + 1 + k // 2), (s_plo, 2 * (k // 2) + 1)),
                                           lambda: gates(7))
                            continue
                        if h == 0 and m % 4 == 0:
                            pe.wait_ge(s_wlo, j + 4)
                        if (h, m) == (1, 2):
                            norm_sums(L, 0)
                        if l == 0 and m == 0 and h == 1:
                            pe.wait_ge(s_plo, 8)
                        if l == 1 and h == 0 and m in (0, 4, 6):
                            pe.wait_ge(*((s_sm, 17) if m == 0 else (s_pt_read, 17) if m == 4 else (s_olo, 17)))
                        n0 = unit_of("o", L, h, m)
                        free_bank(n0)
                        pieces = quad_pieces(w0, m % 4, h, *src)
                        product(n0, HALF[h][1], pieces)
                        if h == 0 and m in between:
                            between[m]()

            def mlp(l):
                j0, w0 = job_at[("mlp", l)]
                u0, loop0 = mark[("up", l)], mark[("loop", l)]
                v0, a0 = read_by(loop0, "V"), read_by(loop0, "A")
                t0 = 8 * CHUNKS * l
                idx = 4 * l
                for h in range(2):
                    group_by_k(range(u0 + 4 * h, u0 + 4 * h + 4), h, lambda t: quad_pieces(w0, t, h),
                               lambda k: ((s_wlo, j0 + k // 2 + 1), (s_ylo, 8 * (idx + h) + k + 1)),
                               (lambda: norm_sums(2 * l, 1)) if h == 0 else None)
                with pe.Fori(0, CHUNKS - 1) as i:
                    pe.wait_ge(s_wlo, i * 8 + (j0 + 8))
                    for q in range(16):
                        h, m = q // 8, q % 8
                        if m == 0:
                            pe.wait_ge(s_hlo, i * 8 + (t0 + 4 * h + 6))
                        if q < 8:
                            pe.wait_ge(s_evA, i * 8 + (a0 - 7 + q))
                        else:
                            pe.wait_ge(s_evV, i * 16 + (v0 + q - 7))
                        product(loop0 + q, HALF[h][1], down_pieces(w0 + 4, m, h))
                    pe.wait_ge(s_wlo, i * 8 + (j0 + 12))
                    for q in range(8):
                        pe.wait_ge(s_evV, i * 16 + (v0 + q + 9))
                        product(loop0 + 16 + q, HALF[q // 4][1], quad_pieces(w0, q % 4, q // 4))
                L = 2 * l + 1
                pe.wait_ge(s_wlo, j0 + 8 * CHUNKS)
                for h in range(2):
                    pe.wait_ge(s_hlo, t0 + 8 * (CHUNKS - 1) + 4 * h + 6)
                    for m in range(KT):
                        if (h, m) == (1, 2):
                            norm_sums(L, 0)
                        n0 = unit_of("down", L, h, m)
                        free_bank(n0)
                        product(n0, HALF[h][1], down_pieces(w0 + 4, m, h))

            def scores(T):
                b0 = score_bank(T)
                if T >= 2:
                    pe.wait_ge(s_sm, T - 1)
                if T < 16:
                    n = T // 4
                    lo = 0 if n == 0 else WIN * (n - 1)
                    w = step_width(T)
                    for v in range(2):
                        for e in range(2):
                            ins = mm(bank[:, b0 + v, 256 * e:256 * e + w],
                                     q_tile(2 * (T % 4) + e)[HD * v:HD * v + HD, WIN * n:WIN * n + WIN],
                                     k_t[HD * v:HD * v + HD, lo:lo + w], start=True, stop=True)
                else:
                    for v in range(2):
                        for bq in range(2):
                            for j in range(4):
                                b = 4 * bq + j
                                out = bank[32 * j:32 * j + 32, b0 + v, 256 * bq:256 * bq + WIN + NS]
                                qs = q_s[HD * v:HD * v + HD, b, :, :]
                                mm(out[:, 0:WIN], qs, kc_t[HD * v:HD * v + HD, b, :], start=True, stop=True)
                                ins = mm(out[:, WIN:WIN + NS], qs, k_t[HD * v:HD * v + HD, SEQ:TOK],
                                         start=True, stop=True)
                ins.then_inc(s_sc, 1)

            def transposes(T):
                w = step_width(T)
                pe.wait_ge(s_nrm, 4 * T + 4)
                if T:
                    pe.wait_ge(s_pt_read, T)
                for kb in range(2 if w > WIN else 1):
                    wk = min(WIN, w - WIN * kb)
                    for e in range(4):
                        ins = nc.tensor.transpose(bank[0:wk, trans_bank(kb), 128 * e:128 * e + 128],
                                                  probs[:, T % 4, e, WIN * kb:WIN * kb + wk], ident)
                ins.then_inc(s_pt, 1)

            def values(T):
                pe.wait_ge(s_pt_read, T + 1)
                if T >= 2:
                    pe.wait_ge(s_olo, T - 1)
                for v in range(2):
                    out = bank[HD * v:HD * v + HD, pv_bank(T), 0:256]
                    if T < 16:
                        n = T // 4
                        blocks = [n] if n == 0 else [n - 1, n]
                        for kb, blk in enumerate(blocks):
                            ins = mm(out, v_tok[:, blk, HD * v:HD * v + HD],
                                     probs_t[:, T % 2, kb, 256 * v:256 * v + 256],
                                     start=(kb == 0), stop=(kb == len(blocks) - 1))
                    else:
                        for b in range(DEC_B):
                            at = 128 * (2 * v + b // 4) + 32 * (b % 4)
                            mm(out[:, 32 * b:32 * b + 32], vc[:, b, HD * v:HD * v + HD],
                               probs_t[:, T % 2, 0, at:at + 32], start=True, stop=False)
                            ins = mm(out[:, 32 * b:32 * b + 32], kv_new[:, 1, HD * v:HD * v + HD],
                                     probs_t[0:NS, T % 2, 1, at:at + 32], start=False, stop=True)
                ins.then_inc(s_pv, 1)

            project(0)
            mlp(0)
            def qkv(g, h, only=None):
                j, w0 = job_at[("qkv", g)]
                nu = 4 if g < 2 else 2
                if h == 0 and not only:
                    pe.wait_ge(s_wlo, j + nu)
                n0 = mark[("qkv", g, h)]
                if g == 0:
                    group_by_k(range(n0, n0 + 4), h, lambda t: quad_pieces(w0, t, h),
                               lambda k: ((s_ylo, 8 * (2 + h) + k + 1),),
                               (lambda: norm_sums(1, 1)) if h == 0 else None)
                    return
                if g == 2:
                    pair_unit(n0 + only, w0, only, h)
                    return
                for t in range(nu):
                    free_bank(n0 + t)
                    product(n0 + t, HALF[h][1], quad_pieces(w0, t, h))

            for g in range(2):
                for h in range(2):
                    qkv(g, h)
            ident = V("ident", 0, 128)
            tb = score_bank(1)
            qkv(2, 0, 0)
            pe.wait_ge(s_evA, read_by(mark[("qkv", 2, 0)], "A"))
            pe.wait_ge(s_evV, read_by(mark[("qkv", 2, 0)], "V"))
            scores(0)
            for n in range(NB):
                ins = nc.tensor.transpose(bank[:, tb, 128 * n:128 * n + 128], v_t[:, 128 * n:128 * n + 128], ident)
            ins.then_inc(s_tok, 1)
            nc.tensor.transpose(bank[:, tb + 1, 0:128], k_t[:, SEQ - 128:SEQ], ident)
            nc.tensor.transpose(bank[0:NS, tb + 1, 128:256], k_t[:, SEQ:TOK], ident)
            nc.tensor.transpose(bank[0:NS, tb + 1, 256:384], v_t[:, SEQ:TOK], ident).then_inc(s_tok, 1)
            qkv(2, 0, 1)
            pe.wait_ge(s_tokc, 3)
            scores(1)
            qkv(2, 1, 0)
            qkv(2, 1, 1)
            scores(2)
            pe.wait_ge(s_evA, read_by(mark["attention"], "A"))
            scores(3)
            for T in range(16):
                transposes(T)
                if T == 12:
                    pe.wait_ge(s_cache, 32)
                if T + 4 < 17:
                    scores(T + 4)
                if T:
                    values(T - 1)
            floor[0] = mark["attention"]
            transposes(16)
            values(15)
            project(1, {1: lambda: values(16)})
            mlp(1)
            norm_sums(3, 1)


def kernel(x_prompt, x_sample, state_lru_h, state_lru_conv, cache_swa_k, cache_swa_v,
           lru_w_x, lru_b_x, lru_w_y, lru_b_y, lru_conv_w, lru_conv_b,
           lru_w_ga, lru_b_ga, lru_w_gi, lru_b_gi, lru_lam, lru_w_out, lru_b_out,
           swa_w_qkv, swa_b_qkv, swa_sinks, swa_w_o, swa_b_o,
           mlp_w_up, mlp_w_down, ln1_g, ln1_b, ln2_g, ln2_b):
    import concourse.bacc as bacc
    from concourse.bass_utils import run_bass_kernel_spmd

    (x_prompt, x_sample, state_lru_h, state_lru_conv, cache_swa_k, cache_swa_v, lru_w_x, lru_b_x, lru_w_y, lru_b_y,
     lru_conv_w, lru_conv_b, lru_w_ga, lru_b_ga, lru_w_gi, lru_b_gi, lru_lam, lru_w_out, lru_b_out, swa_w_qkv,
     swa_b_qkv, swa_sinks, swa_w_o, swa_b_o, mlp_w_up, mlp_w_down, ln1_g, ln1_b, ln2_g, ln2_b) = map(np.asarray, (
         x_prompt, x_sample, state_lru_h, state_lru_conv, cache_swa_k, cache_swa_v, lru_w_x, lru_b_x, lru_w_y,
         lru_b_y, lru_conv_w, lru_conv_b, lru_w_ga, lru_b_ga, lru_w_gi, lru_b_gi, lru_lam, lru_w_out, lru_b_out,
         swa_w_qkv, swa_b_qkv, swa_sinks, swa_w_o, swa_b_o, mlp_w_up, mlp_w_down, ln1_g, ln1_b, ln2_g, ln2_b))

    nq = NKV * GRP * HD
    q_cols = np.arange(nq).reshape(NKV, GRP, HD).transpose(1, 0, 2).reshape(-1)
    cols = np.concatenate([np.arange(nq, nq + 2 * NKV * HD), q_cols])

    def tiles(a):
        a = a.reshape(-1, a.shape[-1] // 128, 128)
        return a.transpose(2, 0, 1).reshape(128, -1)

    def tiles_first(a):
        return a.reshape(-1, KT, 128).transpose(2, 1, 0).reshape(128, -1)

    row, col = np.arange(WIN)[:, None], np.arange(2 * WIN)[None, :]
    mask = np.where((col > row) & (col <= row + WIN), 0.0, NEG).astype(np.float32)
    j, t = np.arange(128) // 32, np.arange(128) % DEC_T
    rows = np.full((128, 2, WIN + NS), NEG, np.float32)
    for bq in range(2):
        rows[:, bq, :WIN][np.arange(WIN)[None, :] > t[:, None]] = 0.0
        c = np.arange(NS)[None, :]
        rows[:, bq, WIN:][(c // DEC_T == 4 * bq + j[:, None]) & (c % DEC_T <= t[:, None])] = 0.0
    sinks = swa_sinks.reshape(NKV, GRP)
    head_of_row = (np.arange(128) % 32) // DEC_T
    parts = {
        "b_y": tiles(lru_b_y), "b_x": tiles(lru_b_x), "conv_w": tiles(lru_conv_w[0]), "conv_b": tiles(lru_conv_b),
        "b_ga": tiles(lru_b_ga.reshape(1, D)), "b_gi": tiles(lru_b_gi.reshape(1, D)), "lam": tiles(lru_lam),
        "b_out": tiles(lru_b_out), "b_o": tiles(swa_b_o),
        "ln_g": tiles(np.stack([ln1_g[0], ln2_g[0], ln1_g[1], ln2_g[1]])),
        "ln_b": tiles(np.stack([ln1_b[0], ln2_b[0], ln1_b[1], ln2_b[1]])),
        "b_qkv": tiles(swa_b_qkv[:, cols]), "h0": tiles_first(state_lru_h[0]),
        "conv_state": tiles_first(state_lru_conv[0].reshape(-1, D)),
        "sinks": np.broadcast_to(sinks.reshape(NKV, GRP // 2, 2).transpose(1, 0, 2).reshape(1, 16), (128, 16)),
        "sink_rows": np.stack([sinks[v][head_of_row] for v in (0, 0, 1, 1)], axis=1),
        "mask": mask, "mask_rows": rows.reshape(128, -1), "ident": np.eye(128, dtype=np.float32),
    }
    vec = np.ascontiguousarray(np.concatenate([parts[n] for n in VEC], axis=1))
    kv = NKV * HD
    arrays = {
        "xp_t": x_prompt[0].T, "xs_t": x_sample.reshape(NS, D).T, "vec": vec,
        "w_y": lru_w_y[0], "w_x": lru_w_x[0], "w_ga": lru_w_ga[0], "w_gi": lru_w_gi[0], "w_out": lru_w_out[0],
        "w_qkv": swa_w_qkv[0][:, cols], "w_o": swa_w_o[0][q_cols], "w_up": mlp_w_up, "w_down": mlp_w_down,
        "ck_t": cache_swa_k[0].reshape(DEC_B, WIN, kv).transpose(2, 0, 1),
        "cache_k": cache_swa_k[0].reshape(DEC_B, WIN, kv), "cache_v": cache_swa_v[0].reshape(DEC_B, WIN, kv),
    }
    arrays = {k: np.ascontiguousarray(v) for k, v in arrays.items()}
    outs = {"y_t": (D, TOK), "small": (128, KT, 36), "k_p": (WIN, kv), "v_p": (WIN, kv),
            "k_s": (DEC_B, WIN, kv), "v_s": (DEC_B, WIN, kv)}

    nc = bacc.Bacc("TRN2", target_bir_lowering=False, num_devices=1)
    args = [nc.dram_tensor(k, v.shape, mybir.dt.from_np(v.dtype), kind="ExternalInput").ap()
            for k, v in arrays.items()]
    args += [nc.dram_tensor(k, s, F32, kind="ExternalOutput").ap() for k, s in outs.items()]
    build(nc, *args)
    got = run_bass_kernel_spmd(nc, [arrays], core_ids=[0]).results[0]

    y = got["y_t"].T
    small = got["small"].transpose(1, 0, 2).reshape(D, 36)
    h, conv = small[:, 0:9].T, small[:, 9:36].reshape(D, 9, CONV - 1).transpose(1, 2, 0)
    heads = (NKV, HD)
    return (y[:SEQ].reshape(1, SEQ, D), y[SEQ:].reshape(DEC_B, DEC_T, D),
            h[0:1].reshape(1, 1, D), conv[0:1][None],
            got["k_p"].reshape(1, 1, WIN, *heads), got["v_p"].reshape(1, 1, WIN, *heads),
            h[1:9].reshape(1, DEC_B, D), conv[1:9][None],
            got["k_s"].reshape(1, DEC_B, WIN, *heads), got["v_s"].reshape(1, DEC_B, WIN, *heads))
```
